# Optimizing a Trainium2 kernel written in Bass

```python
import math
import jax, jax.numpy as jnp
from jax import lax
import numpy as np

D_MODEL = 1024
BATCH = 1
SEQ = 512
DEPTH = 1
DEC_BATCH = 8
DEC_SEQ = 8
PAST_LEN = 4096
PAGE_SIZE = 128

D_CONV = D_MODEL // 2
CONV_WIDTH = 3
GLA_HEADS = 4
GLA_DK = D_MODEL // 2 // GLA_HEADS
GLA_DV = D_MODEL // GLA_HEADS
GLA_RANK = 16
GLA_GATE_NORM = 16.0
GLA_CHUNK = 32
N_GROUPS = 4
EXPERTS_PER_GROUP = 8
N_EXPERTS = N_GROUPS * EXPERTS_PER_GROUP
TOP_K = 2
D_EXPERT = 256
EPS = 1e-6

SPLIT_SIZES = (D_CONV, D_CONV, D_CONV,
               GLA_HEADS * GLA_DK, GLA_HEADS * GLA_DK,
               GLA_HEADS * GLA_DV, GLA_HEADS * GLA_DV,
               GLA_RANK, D_MODEL, D_MODEL)
D_IN = sum(SPLIT_SIZES)

kernel_name = "hybrid_conv_gla_hmoe_step"

def rmsnorm(x, g):
    xf = x.astype(jnp.float32)
    y = xf * lax.rsqrt(jnp.mean(xf * xf, axis=-1, keepdims=True) + EPS)
    return (y * g.astype(jnp.float32)).astype(x.dtype)

def short_conv(u, conv_state, w_conv):
    full = jnp.concatenate([conv_state.astype(u.dtype), u], axis=1)
    rhs = w_conv.astype(u.dtype)[:, None, :]
    z = lax.conv_general_dilated(full, rhs, window_strides=(1,), padding='VALID',
                                 dimension_numbers=('NWC', 'WIO', 'NWC'),
                                 feature_group_count=u.shape[-1])
    return z, full[:, -(CONV_WIDTH - 1):]

def gla(q, k, v, log_a, s0):
    B, L = q.shape[:2]
    c = L if L <= GLA_CHUNK else math.gcd(L, GLA_CHUNK)
    n = L // c
    f32 = jnp.float32
    blk = lambda t: t.astype(f32).reshape(B, n, c, *t.shape[2:])
    qc = blk(q) * (GLA_DK ** -0.5)
    kc, vc, ac = blk(k), blk(v), blk(log_a)
    b = jnp.cumsum(ac, axis=2)
    b_last = b[:, :, -1]
    q_in = qc * jnp.exp(b)
    k_in = kc * jnp.exp(-b)
    k_st = kc * jnp.exp(b_last[:, :, None] - b)
    scores = jnp.einsum('bnthd,bnshd->bnhts', q_in, k_in)
    mask = jnp.tril(jnp.ones((c, c), dtype=bool))
    scores = jnp.where(mask, scores, 0.0)
    o_intra = jnp.einsum('bnhts,bnshv->bnthv', scores, vc)

    def step(S, inp):
        q_i, k_i, v_i, d_i = inp
        o = jnp.einsum('bthd,bhdv->bthv', q_i, S)
        S = S * jnp.exp(d_i)[..., None] + jnp.einsum('bthd,bthv->bhdv', k_i, v_i)
        return S, o

    xs = tuple(jnp.moveaxis(t, 1, 0) for t in (q_in, k_st, vc, b_last))
    S_final, o_inter = lax.scan(step, s0.astype(f32), xs)
    o = o_intra + jnp.moveaxis(o_inter, 0, 1)
    return o.reshape(B, L, GLA_HEADS, GLA_DV), S_final

def mixer(xn, conv_state, gla_state, w_in, w_conv, w_alpha_up, b_alpha, gla_norm,
          w_conv_out, w_gla_out, w_o):
    B, L = xn.shape[:2]
    splits = np.cumsum(SPLIT_SIZES)[:-1].tolist()
    cb, cc, ch, q, k, v, g, a_lr, ga, gb = jnp.split(xn @ w_in, splits, axis=-1)
    z, conv_new = short_conv(cc * ch, conv_state, w_conv)
    y_a = (cb * z) @ w_conv_out
    hd = lambda t, d: t.reshape(B, L, GLA_HEADS, d)
    log_a = jax.nn.log_sigmoid((a_lr @ w_alpha_up + b_alpha).astype(jnp.float32)) / GLA_GATE_NORM
    o, S = gla(hd(q, GLA_DK), hd(k, GLA_DK), hd(v, GLA_DV), hd(log_a, GLA_DK), gla_state)
    o = rmsnorm(o, gla_norm) * jax.nn.silu(hd(g, GLA_DV).astype(jnp.float32))
    y_b = o.astype(xn.dtype).reshape(B, L, GLA_HEADS * GLA_DV) @ w_gla_out
    m = jax.nn.sigmoid(ga) * y_a + jax.nn.sigmoid(gb) * y_b
    return m @ w_o, conv_new, S.astype(gla_state.dtype)

def hmoe(xn, w_group_router, b_group_router, w_expert_router, b_expert_router, w_gate, w_up, w_down):
    B, L, D = xn.shape
    xt = xn.reshape(B * L, D)
    T = xt.shape[0]
    g_prob = jax.nn.softmax((xt @ w_group_router).astype(jnp.float32) + b_group_router.astype(jnp.float32), axis=-1)
    g_top, g_idx = lax.top_k(g_prob, 1)
    e_logits = ((xt @ w_expert_router).astype(jnp.float32)
                + b_expert_router.astype(jnp.float32)).reshape(T, N_GROUPS, EXPERTS_PER_GROUP)
    e_sel = jnp.take_along_axis(e_logits, g_idx[:, :, None], axis=1)[:, 0]
    e_top, e_idx = lax.top_k(jax.nn.softmax(e_sel, axis=-1), TOP_K)
    weights = g_top * (e_top / jnp.sum(e_top, axis=-1, keepdims=True))
    expert_id = g_idx * EXPERTS_PER_GROUP + e_idx
    combine = jnp.einsum('tk,tke->te', weights,
                         jax.nn.one_hot(expert_id, N_EXPERTS, dtype=jnp.float32)).astype(xn.dtype)
    y = jnp.zeros((T, D), dtype=xn.dtype)
    for gi in range(N_GROUPS):
        sl = slice(gi * EXPERTS_PER_GROUP, (gi + 1) * EXPERTS_PER_GROUP)
        hg = jax.nn.silu(jnp.einsum('td,edh->teh', xt, w_gate[sl])) * jnp.einsum('td,edh->teh', xt, w_up[sl])
        y = y + jnp.einsum('teh,ehd->td', hg * combine[:, sl, None], w_down[sl])
    return y.reshape(B, L, D)

def trunk(x, conv_states, gla_states, norm_mix, w_in, w_conv, w_alpha_up, b_alpha, gla_norm,
          w_conv_out, w_gla_out, w_o, norm_ffn, w_group_router, b_group_router,
          w_expert_router, b_expert_router, w_gate, w_up, w_down, norm_final):
    h = x
    new_conv, new_gla = [], []
    for l in range(DEPTH):
        m, c_new, s_new = mixer(rmsnorm(h, norm_mix[l]), conv_states[l], gla_states[l], w_in[l], w_conv[l],
                                w_alpha_up[l], b_alpha[l], gla_norm[l], w_conv_out[l], w_gla_out[l], w_o[l])
        h = h + m
        h = h + hmoe(rmsnorm(h, norm_ffn[l]), w_group_router[l], b_group_router[l], w_expert_router[l],
                     b_expert_router[l], w_gate[l], w_up[l], w_down[l])
        new_conv.append(c_new)
        new_gla.append(s_new)
    return rmsnorm(h, norm_final), jnp.stack(new_conv), jnp.stack(new_gla)

def setup_inputs(seed: int = 0) -> dict:
    key = jax.random.key(seed)
    ks = jax.random.split(key, 24)
    nrm = lambda k, shape, s: jax.random.normal(k, shape, jnp.float32) * s
    return {
        "x_prompt": nrm(ks[0], (BATCH, SEQ, D_MODEL), 1.0),
        "x_sample": nrm(ks[1], (DEC_BATCH, DEC_SEQ, D_MODEL), 1.0),
        "state_conv": nrm(ks[2], (DEPTH, DEC_BATCH, CONV_WIDTH - 1, D_CONV), 1.0),
        "state_gla": nrm(ks[3], (DEPTH, DEC_BATCH, GLA_HEADS, GLA_DK, GLA_DV), 1.0),
        "norm_mix": 1.0 + nrm(ks[4], (DEPTH, D_MODEL), 0.02),
        "w_in": nrm(ks[5], (DEPTH, D_MODEL, D_IN), D_MODEL ** -0.5),
        "w_conv": nrm(ks[6], (DEPTH, CONV_WIDTH, D_CONV), CONV_WIDTH ** -0.5),
        "w_alpha_up": nrm(ks[7], (DEPTH, GLA_RANK, GLA_HEADS * GLA_DK), GLA_RANK ** -0.5),
        "b_alpha": nrm(ks[8], (DEPTH, GLA_HEADS * GLA_DK), 0.1),
        "gla_norm": 1.0 + nrm(ks[9], (DEPTH, GLA_DV), 0.02),
        "w_conv_out": nrm(ks[10], (DEPTH, D_CONV, D_MODEL), D_CONV ** -0.5),
        "w_gla_out": nrm(ks[11], (DEPTH, GLA_HEADS * GLA_DV, D_MODEL), (GLA_HEADS * GLA_DV) ** -0.5),
        "w_o": nrm(ks[12], (DEPTH, D_MODEL, D_MODEL), D_MODEL ** -0.5),
        "norm_ffn": 1.0 + nrm(ks[13], (DEPTH, D_MODEL), 0.02),
        "w_group_router": nrm(ks[14], (DEPTH, D_MODEL, N_GROUPS), D_MODEL ** -0.5),
        "b_group_router": nrm(ks[15], (DEPTH, N_GROUPS), 0.01),
        "w_expert_router": nrm(ks[16], (DEPTH, D_MODEL, N_EXPERTS), D_MODEL ** -0.5),
        "b_expert_router": nrm(ks[17], (DEPTH, N_EXPERTS), 0.01),
        "w_gate": nrm(ks[18], (DEPTH, N_EXPERTS, D_MODEL, D_EXPERT), D_MODEL ** -0.5),
        "w_up": nrm(ks[19], (DEPTH, N_EXPERTS, D_MODEL, D_EXPERT), D_MODEL ** -0.5),
        "w_down": nrm(ks[20], (DEPTH, N_EXPERTS, D_EXPERT, D_MODEL), D_EXPERT ** -0.5),
        "norm_final": 1.0 + nrm(ks[21], (D_MODEL,), 0.02),
    }

def reference(x_prompt, x_sample, state_conv, state_gla, norm_mix, w_in, w_conv, w_alpha_up, b_alpha,
              gla_norm, w_conv_out, w_gla_out, w_o, norm_ffn, w_group_router, b_group_router,
              w_expert_router, b_expert_router, w_gate, w_up, w_down, norm_final):
    weights = (norm_mix, w_in, w_conv, w_alpha_up, b_alpha, gla_norm, w_conv_out, w_gla_out, w_o,
               norm_ffn, w_group_router, b_group_router, w_expert_router, b_expert_router,
               w_gate, w_up, w_down, norm_final)
    b_p = x_prompt.shape[0]
    conv0 = jnp.zeros((DEPTH, b_p, CONV_WIDTH - 1, D_CONV), dtype=x_prompt.dtype)
    gla0 = jnp.zeros((DEPTH, b_p, GLA_HEADS, GLA_DK, GLA_DV), dtype=x_prompt.dtype)
    y_prompt, conv_prompt_new, gla_prompt_new = trunk(x_prompt, conv0, gla0, *weights)
    y_sample, conv_sample_new, gla_sample_new = trunk(x_sample, state_conv, state_gla, *weights)
    return (y_prompt, y_sample, conv_prompt_new, gla_prompt_new, conv_sample_new, gla_sample_new)


_drawn_inputs = setup_inputs


def setup_inputs(seed=0):
    import zlib

    import numpy as np

    out = dict(_drawn_inputs(seed))
    spreads = {}
    factors = {'gla_norm': 26.311,
     'b_group_router': 200.0,
     'b_expert_router': 27.255,
     'norm_final': 20.481,
     'norm_ffn': 5.637}
    for name, (base, spread) in spreads.items():
        noise = np.random.default_rng([zlib.crc32(name.encode()), seed]).standard_normal(out[name].shape)
        drawn = base * np.exp(spread * noise) if base else spread * noise
        out[name] = __import__('jax').numpy.asarray(drawn.astype(out[name].dtype))
    for name, factor in factors.items():
        out[name] = (out[name] * factor).astype(out[name].dtype)
    return out
```

```python
from contextlib import ExitStack

import concourse.bass as bass
from concourse import mybir

F32 = mybir.dt.float32
F32R = mybir.dt.float32r
I32 = mybir.dt.int32
U32 = mybir.dt.uint32
ALU = mybir.AluOpType
ACT = mybir.ActivationFunctionType
AX = mybir.AxisListType

P = 128
D = 1024
KD = D // P
SEQ = 512
DB, DS = 8, 8
ND = DB * DS
T = SEQ + ND
NT = (T + P - 1) // P
TP = NT * P
NPT = SEQ // P
HALF = T // 2
DC = D // 2
H = 4
DK = DC // H
DV = D // H
RANK = 16
CH = 32
NCH = P // CH
NG, NEG = 4, 8
NE = NG * NEG
NR = NG + NE
DE = 256
EPS = 1e-6
GATE_NORM = 16.0
QSCALE = DK ** -0.5
GW = 2048
C_CB, C_CC, C_CH, C_Q, C_K, C_V, C_G = 0, 512, 1024, 1536, 2048, 2560, 3584
C_A = 4608
C_GA = C_A + RANK
C_GB = C_GA + D
B = 64
XB = 2 * T // (B + 1)
NBLK = NE + XB
NSMALL = 11
FAR = 1 << 20
G_QK, G_V, G_G, G_CONV, G_CO, G_GA, G_GB, G_GO, G_WO, G_END = 0, 4, 8, 12, 18, 20, 24, 28, 32, 36
N_A, N_AL, N_SC, N_QK, N_V, N_G, N_CONV, N_CO, N_GA, N_GB, N_GO, N_WO, N_END = (
    0, 1, 5, 6, 14, 34, 42, 54, 62, 70, 78, 86, 106)


class Chain:

    def __init__(self, eng, sem):
        self.eng, self.sem, self.n, self.off = eng, sem, 0, 0

    def __call__(self, ins):
        ins.then_inc(self.sem, 1)
        self.n += 1

    def sync(self):
        self.eng.wait_ge(self.sem, self.off + self.n)

    def enter(self, i, per):
        self.n0, self.per, self.off = self.n, per, i * per

    def leave(self, times):
        assert self.n - self.n0 == self.per, (self.n - self.n0, self.per)
        self.n, self.off = self.n0 + self.per * times, 0


def build(nc, x_prompt, x_sample, state_conv, state_gla, norm_mix, w_in, w_conv, w_alpha_up, b_alpha, gla_norm,
          w_conv_out, w_gla_out, w_o, norm_ffn, w_group_router, b_group_router, w_expert_router, b_expert_router,
          w_gate, w_up, w_down, norm_final,
          y_prompt, y_sample, conv_prompt_new, gla_prompt_new, conv_sample_new, gla_sample_new):
    rows_d = nc.dram_tensor("moe_rows", (T, D), F32).ap()
    table_d = nc.dram_tensor("slot_table", (B * NBLK, 1), I32).ap()
    res_d = nc.dram_tensor("moe_results", (2 * T, D), F32).ap()
    xp = x_prompt.rearrange("b (n p) d -> p (b n) d", p=P)
    xs = x_sample.rearrange("b t d -> (b t) d")
    win = w_in[0].rearrange("(k p) c -> p k c", p=P)
    wco = w_conv_out[0].rearrange("(k p) c -> p k c", p=P)
    wgo = w_gla_out[0].rearrange("(k p) c -> p k c", p=P)
    woo = w_o[0].rearrange("(k p) c -> p k c", p=P)
    st_in = state_gla[0].rearrange("s h d v -> s d h v")
    st_out = gla_sample_new[0].rearrange("s h d v -> s d h v")

    ctx = ExitStack()
    with ctx:
        place = [(nc.sbuf_base + 31) // 32 * 32]

        def sb(name, shape, dt=F32, at=None):
            n = 4
            for s in shape[1:]:
                n *= s
            if at is not None:
                place[0] = at
            t = nc.alloc_sbuf_tensor_at(name, shape, dt, offset=place[0])
            place[0] += (n + 31) // 32 * 32
            assert place[0] <= nc.sbuf_usable_end, (name, place[0] - nc.sbuf_usable_end)
            return t

        ident = sb("ident", [P, P])
        ones = sb("ones", [P, P])
        before = sb("before", [P, P])
        causal_f = sb("causal_f", [P, P])
        causal = sb("causal", [P, P], I32)
        causal8_f = sb("causal8_f", [ND, ND])
        causal8 = sb("causal8", [ND, ND], I32)
        inseq = sb("inseq", [ND, DB])
        ss = sb("ss", [P, 32])
        ms = sb("ms", [P, 32])
        rs = sb("rs", [P, 32])
        expo = sb("expo", [P, H])
        balpha = sb("balpha", [P, H])
        gn = sb("gn", [P, DV // P])
        gnh = sb("gnh", [P, DV // P + 2])
        wtap = sb("wtap", [P, 3, H])
        hist = sb("hist", [P, H, DB * 2])
        wr = sb("wr", [P, KD, NR])
        rb = sb("rb", [P, NR])
        xinfo = sb("xinfo", [1, XB + 1], I32)
        slotd = sb("slotd", [B, NBLK], I32)
        slots = sb("slots", [B, NBLK], I32)
        curs = [sb(f"curs{i}", [B, 1], I32) for i in range(2)]
        curd = [sb(f"curd{i}", [B, 1], I32) for i in range(2)]
        lg = sb("lg", [P, NT, NR])
        wts = sb("wts", [P, 2, NT])
        far = sb("far", [B, NBLK], I32)
        mark = sb("mark", [P, 64])
        raw = [sb(f"raw{i}", [P, GW]) for i in range(2)]
        wh = [sb(f"wh{i}", [P, GW], F32R) for i in range(2)]
        wl = [sb(f"wl{i}", [P, GW], F32R) for i in range(2)]
        zone_a = place[0]
        raw += [sb(f"raw{i}", [P, GW]) for i in range(2, 6)]
        wh.append(sb("wh2", [P, GW], F32R))
        wl.append(sb("wl2", [P, GW], F32R))
        zone_b = place[0]
        xh = sb("xh", [P, KD, TP], F32R)
        xl = sb("xl", [P, KD, TP], F32R)
        zone_v = place[0]
        v = sb("v", [P, NT, D])
        zone_s = place[0]
        sg = sb("sg", [P, KD, T])
        zone_q = place[0]
        qk = sb("qk", [P, 2 * H, T])
        zone_z = place[0]
        xin = sb("xin", [P, NT, D], at=zone_v)
        la = sb("la", [P, NT, H, P], at=zone_a)
        s1 = place[0]
        nmb = sb("nmb", [P, D])
        xn = [sb(f"xn{i}", [P, D]) for i in range(2)]
        junk1 = sb("junk1", [P, D])
        rawa = sb("rawa", [P, KD, P])
        ah = sb("ah", [P, KD, P], F32R)
        al = sb("al", [P, KD, P], F32R)
        assert place[0] <= zone_b
        aT = sb("aT", [RANK, T], at=zone_z)
        wau = sb("wau", [RANK, H * DK])
        sct = sb("sct", [DB * 2, DC])
        abt = sb("abt", [P, T], at=zone_s)
        mnt = sb("mnt", [P, T])
        m_tile = sb("m_tile", [P, H, P], at=s1)
        m_ch = sb("m_ch", [P, H, P])
        m_seq = sb("m_seq", [P, H, P])
        bt = sb("bt", [P, H, P])
        bc = sb("bc", [P, H, P])
        eb = sb("eb", [P, H, P])
        ec = sb("ec", [P, H, P])
        qg = sb("qg", [P, H, P])
        ql = sb("ql", [P, H, P])
        kst = sb("kst", [P, H, P])
        kt = sb("kt", [P, H, P])
        sc = sb("sc", [P, H, P])
        NKI = CH * NCH * (NCH + 1) // 2
        dif_at = place[0]
        dif = sb("dif", [P, H, NKI])
        S = sb("S", [P, H, DV], at=zone_z)
        ta = sb("ta", [P, T])
        tb = sb("tb", [P, T], at=dif_at + 4 * H * NKI)
        kiv = sb("kiv", [P, H, NKI], at=dif_at)
        qm = sb("qm", [P, DB, H, ND], at=dif_at)
        assert place[0] <= zone_b - 4 * H * DV
        s0 = [sb("s0a", [P, H, DV], at=zone_b - 4 * H * DV), sb("s0b", [P, H, DV], at=zone_z + 4 * H * DV), S]
        ksm = [bc, ec]
        zh = sb("zh", [P, H, T], F32R, at=zone_q)
        zl = sb("zl", [P, H, T], F32R)
        m1 = sb("m1", [P, KD, T], at=zone_a)
        sgb = sb("sgb", [P, KD, T])
        up = sb("up", [P, H, SEQ + 2])
        assert place[0] <= zone_b
        tmp = [sb("tmp0", [P, T], at=zone_z), sb("tmp1", [P, T])]
        ud = sb("ud", [P, H, DB, DS + 2])
        cs = sb("cs", [P, H, 2 + 2 * DB])
        cso = sb("cso", [2 + 2 * DB, DC])
        mh = sb("mh", [P, KD, TP], F32R, at=zone_v)
        ml = sb("ml", [P, KD, TP], F32R)
        assert place[0] <= zone_z
        h = sb("h", [P, NT, D], at=zone_b)
        nfb = sb("nfb", [P, D])
        nlb = sb("nlb", [P, D])
        x2 = [sb(f"x2{i}", [P, D]) for i in range(2)]
        junk = sb("junk", [P, D])
        assert place[0] <= zone_v
        xr = [sb(f"xr{i}", [P, KD, P], at=None if i else zone_z) for i in range(2)]
        xg = [sb(f"xg{i}", [B, D], at=None if i else zone_v) for i in range(2)]
        gh = [sb(f"gh{i}", [P, KD, P], F32R) for i in range(2)]
        gl = [sb(f"gl{i}", [P, KD, P], F32R) for i in range(2)]
        yb = [sb(f"yb{i}", [B, D]) for i in range(2)]
        hh = [sb(f"hh{i}", [P, DE // P, P], F32R) for i in range(2)]
        hl = [sb(f"hl{i}", [P, DE // P, P], F32R) for i in range(2)]
        si = [sb(f"si{i}", [B, DE]) for i in range(2)]
        hm = [sb(f"hm{i}", [B, DE]) for i in range(2)]
        rt = {}
        for n, w in (("em", NE), ("c1", NE), ("e1", NE), ("e2", NE), ("mk", NE), ("io", NE), ("pr", NE),
                     ("gd", NG), ("gx", NG), ("gc", NG), ("go", NG)):
            rt[n] = sb("r_" + n, [P, NT, w])
        for n in ("gmax", "gsum", "gtop", "gi", "m1v", "i1", "m2v", "i2", "dd", "ex"):
            rt[n] = sb("r_" + n, [P, NT])
        for n in ("pk", "bk", "ek", "q", "is0", "pf", "t1", "t2"):
            rt[n] = sb("r_" + n, [P, 2, NT])
        for n in ("pi", "qi", "sl"):
            rt[n] = sb("r_" + n, [P, 2, NT], I32)
        for n in ("cnt", "nb", "xe", "ci", "base", "oneb"):
            rt[n] = sb("r_" + n, [P, NE])
        cnt_i = sb("cnt_i", [P, NE], I32)
        ig = sb("ig", [P, NT, NG])
        valid = sb("valid", [P, NT])
        vals = sb("vals", [P, 2, NT], I32)
        iox = sb("iox", [1, XB, NE])
        gex = sb("gex", [1, XB, NE])
        xf = sb("xf", [1, XB + 1])
        assert place[0] <= zone_z, place[0] - zone_z
        y2 = [sb(f"y2{i}", [P, 2, D], at=None if i else zone_a) for i in range(2)]
        yo = [sb(f"yo{i}", [P, D]) for i in range(2)]

        ps = ctx.enter_context(nc.psum_tensor("ps", [P, 8, 512], F32))
        pair = [ps[:, 0:2, :], ps[:, 2:4, :]]
        TB, UB = 4, 6

        def sem(name):
            return ctx.enter_context(nc.semaphore(name))

        raw_in = [sem(f"raw_in{i}") for i in range(6)]
        x_in = [sem(f"x_in{i}") for i in range(NT)]
        nm_in, small_in, a_in, h_in, nf_in = (sem(n) for n in ("nm_in", "small_in", "a_in", "h_in", "nf_in"))
        pool_const, dve_const = sem("pool_const"), sem("dve_const")
        hi_ready, lo_ready, w_used = sem("hi_ready"), sem("lo_ready"), sem("w_used")
        unit_full = sem("unit_full")
        unit_free = [sem(f"unit_free{i}") for i in range(2)]
        sq_done, rs_ready = sem("sq_done"), sem("rs_ready")
        xn_ready, xt_full, xh_ready, xt_free = (sem(n) for n in ("xn_ready", "xt_full", "xh_ready", "xt_free"))
        ah_ready, al_ready, aT_ready = sem("ah_ready"), sem("al_ready"), sem("aT_ready")
        ls_act, la_ready = sem("ls_act"), sem("la_ready")
        scans_done, ebec_done, diffs_done, exps_done = (
            sem(n) for n in ("scans_done", "ebec_done", "diffs_done", "exps_done"))
        gla_in, p1_full, kt_ready, sc_ready, o_full, kv_full, on_ready, s_ready = (
            sem(n) for n in ("gla_in", "p1_full", "kt_ready", "sc_ready", "o_full", "kv_full", "on_ready", "s_ready"))
        g_act, sg_ready = sem("g_act"), sem("sg_ready")
        st_load = [sem(f"st_load{i}") for i in range(3)]
        st_store, km_ready, dkv_full, st_ready = (sem(n) for n in ("st_store", "km_ready", "dkv_full", "st_ready"))
        cc_ready, z_mul, z_hi, z_ready, cs_ready, cs_full, cso_ready = (
            sem(n) for n in ("cc_ready", "z_mul", "z_hi", "z_ready", "cs_ready", "cs_full", "cso_ready"))
        ya_ready, sig_ready, m1_ready, sgb_ready = (sem(n) for n in ("ya_ready", "sig_ready", "m1_ready", "sgb_ready"))
        og_full, og_mul, og_hi, og_ready = (sem(n) for n in ("og_full", "og_mul", "og_hi", "og_ready"))
        m_mul, m_hi, m_ready, h_ready = (sem(n) for n in ("m_mul", "m_hi", "m_ready", "h_ready"))
        x2_out = [sem(f"x2_out{i}") for i in range(2)]
        x2_ready, x2t_full, xr_ready, lg_full, lg_ready = (
            sem(n) for n in ("x2_ready", "x2t_full", "xr_ready", "lg_full", "lg_ready"))
        r_dve, r_act, r_pos, slot_ready, tab_init, tab_done, tab_load, idx_ready, moe_zero, xinfo_ready = (
            sem(n) for n in ("r_dve", "r_act", "r_pos", "slot_ready", "tab_init", "tab_done", "tab_load", "idx_ready",
                             "moe_zero", "xinfo_ready"))
        xg_in = [sem(f"xg_in{i}") for i in range(2)]
        y_out = [sem(f"y_out{i}") for i in range(2)]
        e_cur = sem("e_cur")
        bt_full, bh_ready, bl_ready, g_full, u_full, si_ready, hm_ready, ht_full, hh_ready, hl_ready, y_full, yb_ready = (
            sem(n) for n in ("bt_full", "bh_ready", "bl_ready", "g_full", "u_full", "si_ready", "hm_ready", "ht_full",
                             "hh_ready", "hl_ready", "y_full", "yb_ready"))
        e_raw, e_hi, e_lo, e_xg, e_xt, e_bh, e_bl, e_gu, e_si, e_hm, e_ht, e_hh, e_hl, e_y, e_yb, e_out = (
            sem("e_" + n) for n in ("raw", "hi", "lo", "xg", "xt", "bh", "bl", "gu", "si", "hm", "ht", "hh", "hl",
                                    "y", "yb", "out"))
        moe_done = sem("moe_done")
        y2_in = [sem(f"y2_in{i}") for i in range(2)]
        hf_ready, yo_ready = sem("hf_ready"), sem("yo_ready")
        yo_out = [sem(f"yo_out{i}") for i in range(2)]
        out_done = sem("out_done")
        c_act, c_dve, c_pool = sem("c_act"), sem("c_dve"), sem("c_pool")

        def raw_count(m):
            return m // 6 + 1 + (G_END // 2 if (m + 2) % 6 < 2 else 0)

        block = ctx.enter_context(nc.Block())

        def unit_free_count(n_even, step, c):
            return n_even // 2 + step + c // 2

        def wait_unit(eng, g, k, c, ncol, base):
            if c == ncol - 1:
                eng.wait_ge(w_used, g + 1)
            else:
                eng.wait_ge(unit_full, base + k * (ncol - 1) + c + 1)

        def store(sp, i):
            sp.wait_ge(yo_ready, i + 1)
            dst = y_sample.rearrange("b t d -> (b t) d") if i == NPT else y_prompt[0, i * P:(i + 1) * P, :]
            sp.dma_start(dst, yo[i % 2][0:ND if i == NPT else P, :]).then_inc(yo_out[i % 2], 16)

        @block.sync
        def _(sp):
            for i in range(NPT):
                sp.dma_start(xin[:, i, :], xp[:, i, :]).then_inc(x_in[i], 16)
                if i == 0:
                    sp.dma_start(nmb[:, :], norm_mix.to_broadcast((P, D))).then_inc(nm_in, 16)
            sp.wait_ge(dve_const, 1)
            sp.dma_start(xin[0:ND, NPT, :], xs).then_inc(x_in[NPT], 16)
            sp.dma_start(rawa[:, :, :], win[:, :, C_A:C_A + P]).then_inc(a_in, 16)
            sp.dma_start(wau[:, :], w_alpha_up[0]).then_inc(small_in, 16)
            sp.dma_start(balpha[:, :], b_alpha[0].rearrange("(h p) -> p h", p=P),
                         allow_slow_non_contiguous=True).then_inc(small_in, 16)
            sp.dma_start(sct[:, :], state_conv[0].rearrange("s w c -> (s w) c")).then_inc(small_in, 16)
            sp.dma_start(gn[:, :], gla_norm[0].rearrange("(c p) -> p c", p=P),
                         allow_slow_non_contiguous=True).then_inc(small_in, 16)
            for w in range(3):
                sp.dma_start(wtap[:, w, :], w_conv[0, w].rearrange("(c p) -> p c", p=P),
                         allow_slow_non_contiguous=True).then_inc(small_in, 16)
            sp.dma_start(wr[:, :, 0:NG], w_group_router[0].rearrange("(k p) e -> p k e", p=P)).then_inc(small_in, 16)
            sp.dma_start(wr[:, :, NG:NR], w_expert_router[0].rearrange("(k p) e -> p k e", p=P)).then_inc(small_in, 16)
            sp.dma_start(rb[:, 0:NG], b_group_router.to_broadcast((P, NG))).then_inc(small_in, 16)
            sp.dma_start(rb[:, NG:NR], b_expert_router.to_broadcast((P, NE))).then_inc(small_in, 16)

            def load(par, src, kt=KD):
                sp.dma_start(raw[par][:, :].rearrange("p (k c) -> p k c", k=kt), src).then_inc(raw_in[par], 16)

            for g in range(2):
                load(g, win[:, :, C_Q + g * 256:C_Q + (g + 1) * 256])
            with sp.Fori(0, (G_CONV - 2) // 2) as i:
                for p in range(2):
                    sp.wait_ge(lo_ready, 2 * i + p + 1)
                    load(p, win[:, :, bass.ds(i * 512 + (C_Q + 512 + p * 256), 256)])
            conv = [c + t * 256 for t in range(2) for c in (C_CC, C_CH, C_CB)]
            for g in range(G_CONV, G_CONV + 2):
                sp.wait_ge(lo_ready, g - 1)
                load(g % 2, win[:, :, conv[g - G_CONV]:conv[g - G_CONV] + 256])
            sp.wait_ge(s_ready, NPT + 1)
            sp.dma_start(gla_prompt_new[0, 0].rearrange("h d v -> d h v"), S[:, :, :]).then_inc(out_done, 16)
            for s in range(2):
                if s == 1:
                    sp.wait_ge(sg_ready, 2 * NPT + 1)
                sp.dma_start(s0[s][:, :, :], st_in[s]).then_inc(st_load[s], 16)
            sp.wait_ge(out_done, 16)
            sp.dma_start(s0[2][:, :, :], st_in[2]).then_inc(st_load[2], 16)
            for s in range(DB):
                sp.wait_ge(st_ready, s + 1)
                sp.dma_start(st_out[s], s0[s % 3][:, :, :]).then_inc(st_store, 16)
                if s + 3 < DB:
                    sp.wait_ge(st_store, 16 * (s + 1))
                    sp.dma_start(s0[s % 3][:, :, :], st_in[s + 3]).then_inc(st_load[s % 3], 16)
            for g in range(G_CONV + 2, G_CO):
                sp.wait_ge(lo_ready, g - 1)
                load(g % 2, win[:, :, conv[g - G_CONV]:conv[g - G_CONV] + 256])
            for g in range(G_CO, G_GA):
                sp.wait_ge(lo_ready, g - 1)
                load(g % 2, wco[:, :, (g - G_CO) * 512:(g - G_CO + 1) * 512], kt=H)
            with sp.Fori(0, (G_GO - G_GA) // 2) as i:
                for p in range(2):
                    sp.wait_ge(lo_ready, 2 * i + (G_GA + p - 1))
                    load(p, win[:, :, bass.ds(i * 512 + (C_GA + p * 256), 256)])
            with sp.Fori(0, 2) as i:
                for p in range(2):
                    sp.wait_ge(lo_ready, 2 * i + (G_GO + p - 1))
                    load(p, wgo[:, :, bass.ds(i * 512 + p * 256, 256)])
            for g in range(G_WO, G_WO + 2):
                sp.wait_ge(lo_ready, g - 1)
                load(g % 2, woo[:, :, (g - G_WO) * 256:(g - G_WO + 1) * 256])
            sp.wait_ge(cso_ready, 1)
            sp.dma_start(conv_prompt_new[0, 0], cso[0:2, :]).then_inc(out_done, 16)
            sp.dma_start(conv_sample_new[0].rearrange("s w c -> (s w) c"), cso[2:2 + 2 * DB, :]).then_inc(out_done, 16)
            sp.wait_ge(w_used, G_WO)
            sp.wait_ge(dve_const, 2)
            sp.dma_start(h[:, 0:NPT, :], xp).then_inc(h_in, 16)
            sp.dma_start(h[0:ND, NPT, :], xs).then_inc(h_in, 16)
            sp.dma_start(nfb[:, :], norm_ffn.to_broadcast((P, D))).then_inc(nf_in, 16)
            sp.dma_start(nlb[:, :], norm_final.rearrange("(a d) -> a d", a=1).to_broadcast((P, D))).then_inc(nf_in, 16)
            for g in range(G_WO + 2, G_END):
                sp.wait_ge(lo_ready, g - 1)
                load(g % 2, woo[:, :, (g - G_WO) * 256:(g - G_WO + 1) * 256])

            def expert(m_slot, which, e):
                dst = raw[(m_slot + 2) % 6]
                if which == "down":
                    src = w_down[0, e].rearrange("(k p) d -> p k d", p=P)
                else:
                    src = (w_gate if which == "gate" else w_up)[0, e].rearrange("(k p) c -> p k c", p=P)
                return dst[:, :].rearrange("p (k c) -> p k c", k=DE // P if which == "down" else KD), src

            sp.wait_ge(m_ready, 2 * (G_WO - G_GO))
            for m, (which, e) in enumerate((("gate", 0), ("up", 0), ("gate", 1), ("up", 1), ("down", 0))):
                if m >= 4:
                    sp.wait_ge(lo_ready, G_END + m - 5)
                dst, src = expert(m, which, e)
                sp.dma_start(dst, src).then_inc(raw_in[(m + 2) % 6], 16)
            for i in range(NT):
                n = ND if i == NPT else P
                sp.wait_ge(x2_ready, i + 1)
                sp.dma_start(rows_d[i * P:i * P + n, :], x2[i % 2][0:n, :]).then_inc(x2_out[i % 2], 16)
            sp.wait_ge(tab_done, 16 * 2 * NT)
            sp.dma_start(slotd[:, :], table_d.rearrange("(p b) a -> p (b a)", b=NBLK)).then_inc(tab_load, 16)
            with sp.Fori(0, (NE - 2) // 2) as i:
                for r in range(6):
                    q = r // 3
                    which = ("gate", "up", "down")[r % 3]
                    e = i * 2 + (2 + q - (which == "down"))
                    sp.wait_ge(lo_ready, 6 * i + (G_END + 5 + r - 5))
                    dst = raw[(5 + r + 2) % 6]
                    if which == "down":
                        src = w_down[0, bass.ds(e, 1)].rearrange("e (k p) d -> p (e k) d", p=P)
                    else:
                        src = (w_gate if which == "gate" else w_up)[0, bass.ds(e, 1)].rearrange(
                            "e (k p) c -> p (e k) c", p=P)
                    sp.dma_start(dst[:, :].rearrange("p (k c) -> p k c", k=DE // P if which == "down" else KD),
                                 src).then_inc(raw_in[(5 + r + 2) % 6], 16)
            m = 3 * NE - 1
            sp.wait_ge(lo_ready, G_END + m - 5)
            dst, src = expert(m, "down", NE - 1)
            sp.dma_start(dst, src).then_inc(raw_in[(m + 2) % 6], 16)
            sp.wait_ge(xinfo_ready, 1)
            nx = sp.value_load(xinfo[0:1, XB:XB + 1], min_val=0, max_val=XB)
            sp.wait_ge(lo_ready, G_END + 3 * NE)
            with sp.Fori(0, XB) as j:
                with sp.If(nx > j):
                    sp.wait_ge(e_yb, j + 1)
                    e = sp.value_load(xinfo[0:1, bass.ds(j, 1)], min_val=0, max_val=NE - 1)
                    for s, w in enumerate((w_gate, w_up, w_down)):
                        kt = DE // P if s == 2 else KD
                        sp.dma_start(raw[s][:, :].rearrange("p (k c) -> p k c", k=kt),
                                     w[0, bass.ds(e, 1)].rearrange("e (k p) c -> p (e k) c", p=P)).then_inc(e_raw, 16)
            sp.wait_ge(moe_done, 1)
            for i in range(NT):
                n = ND if i == NPT else P
                if i >= 2:
                    sp.wait_ge(hf_ready, i - 1)
                sp.dma_start(y2[i % 2][0:n, :, :], res_d[2 * i * P:2 * (i * P + n), :].rearrange(
                    "(p k) d -> p k d", k=2)).then_inc(y2_in[i % 2], 16)
                if i >= 1:
                    store(sp, i - 1)
            store(sp, NT - 1)
            sp.wait_ge(yo_out[0], 16 * ((NT + 1) // 2))
            sp.wait_ge(yo_out[1], 16 * (NT // 2))
            sp.wait_ge(out_done, 16 * 3)
            sp.wait_ge(st_store, 16 * DB)

        @block.gpsimd
        def _(pool):
            c = Chain(pool, c_pool)
            c(pool.memset(ident[:, :], 0.0))
            c(pool.memset(ones[:, :], 1.0))
            c(pool.memset(expo[:, :], -0.5))
            c.sync()
            c(pool.affine_select(out=ident[:, :], in_=ident[:, :], compare_op=ALU.not_equal, fill=1.0, base=0,
                                 pattern=[[-1, P]], channel_multiplier=1))
            c(pool.affine_select(out=before[:, :], in_=ones[:, :], compare_op=ALU.is_gt, fill=0.0, base=0,
                                 pattern=[[1, P]], channel_multiplier=-1))
            c(pool.affine_select(out=causal_f[:, :], in_=ones[:, :], compare_op=ALU.is_ge, fill=0.0, base=0,
                                 pattern=[[1, P]], channel_multiplier=-1))
            c(pool.affine_select(out=inseq[:, :], in_=ones[0:ND, 0:DB], compare_op=ALU.is_ge, fill=0.0, base=0,
                                 pattern=[[-DS, DB]], channel_multiplier=1))
            c.sync()
            c(pool.affine_select(out=inseq[:, :], in_=inseq[:, :], compare_op=ALU.is_ge, fill=0.0, base=DS - 1,
                                 pattern=[[DS, DB]], channel_multiplier=-1))
            c(pool.affine_select(out=causal8_f[:, :], in_=causal_f[0:ND, 0:ND], compare_op=ALU.is_ge, fill=0.0,
                                 base=0, pattern=[[-DS, DB], [0, DS]], channel_multiplier=1))
            c.sync()
            pool.memset(far[:, :], FAR).then_inc(pool_const, 1)
            pool.wait_ge(pool_const, 1)
            pool.dma_start(table_d.rearrange("(p b) a -> p (b a)", b=NBLK), far[:, :]).then_inc(tab_init, 16)

            def carry():
                return pool.tensor_tensor(ms[:, 29:30], expo[:, 0:1], expo[:, 0:1], ALU.add)

            def rms(n, lo, hi, size, rows=P):
                pool.wait_ge(sq_done, n + 1)
                c(carry())
                c(pool.tensor_scalar(ms[0:rows, lo:hi], ss[0:rows, lo:hi], 1.0 / size, EPS, ALU.mult, ALU.add))
                c.sync()
                pool.tensor_tensor(rs[0:rows, lo:hi], ms[0:rows, lo:hi], expo[0:rows, 0:hi - lo], ALU.pow).then_inc(rs_ready, 1)

            for i in range(NT):
                rms(i, i, i + 1, D)
            with pool.Fori(0, NPT // 2) as i:
                c.enter(i, 4)
                for p in range(2):
                    rms(i * 2 + (NT + p), 8 + 4 * p, 12 + 4 * p, DV)
                c.leave(NPT // 2)
            pool.wait_ge(kt_ready, NPT + 1)
            for s in range(DB):
                if s >= 2:
                    pool.wait_ge(dkv_full, s - 1)
                pool.tensor_scalar(ksm[s % 2][0:ND, :, :], kt[0:ND, :, :], inseq[:, s:s + 1], None,
                                   ALU.mult).then_inc(km_ready, 1)
            pool.wait_ge(sq_done, NT + NPT + 1)
            c(pool.tensor_scalar(ms[0:ND, 8:12], ss[0:ND, 8:12], 1.0 / DV, EPS, ALU.mult, ALU.add))
            c.sync()
            pool.tensor_tensor(rs[0:ND, 8:12], ms[0:ND, 8:12], expo[0:ND, 0:H], ALU.pow).then_inc(rs_ready, 1)
            for i in range(NT):
                rms(NT + NPT + 1 + i, 16 + i, 17 + i, D)
            pool.wait_ge(w_used, G_END)
            c(pool.iota(rt["io"][:, :, :], pattern=[[0, NT], [1, NE]], base=0, channel_multiplier=0,
                        allow_small_or_imprecise_dtypes=True))
            c(pool.iota(ig[:, :, :], pattern=[[0, NT], [1, NG]], base=0, channel_multiplier=0,
                        allow_small_or_imprecise_dtypes=True))
            for k in range(2):
                c(pool.iota(vals[:, k, :], pattern=[[2 * P, NT]], base=k, channel_multiplier=2))
            c(pool.iota(iox[:, :, :], pattern=[[1, XB], [0, NE]], base=0, channel_multiplier=0,
                        allow_small_or_imprecise_dtypes=True))
            c(pool.memset(valid[:, :], 1.0))
            c(pool.memset(rt["oneb"][:, :], 1.0))
            c.sync()
            c(pool.memset(valid[ND:P, NPT:NT], 0.0))
            c.sync()
            for i in range(2):
                c(pool.memset(xg[i][:, :], 0.0))
                c.sync()
                c(pool.memset(gh[i][:, :, :].bitcast(F32), 0.0))
                c(pool.memset(gl[i][:, :, :].bitcast(F32), 0.0))
                c(pool.memset(hh[i][:, :, :].bitcast(F32), 0.0))
                c(pool.memset(hl[i][:, :, :].bitcast(F32), 0.0))
            c.sync()
            pool.memset(ms[:, 30:31], 0.0).then_inc(moe_zero, 1)
            pool.wait_ge(tab_init, 16)
            pool.wait_ge(slot_ready, 1)
            for i in range(NT):
                n = ND if i == NPT else P
                for k in range(2):
                    pool.indirect_dma_start(
                        out=table_d, out_offset=bass.IndirectOffsetOnAxis(ap=rt["sl"][0:n, k, i:i + 1].bitcast(U32), axis=0),
                        in_=vals[0:n, k, i:i + 1], in_offset=None).then_inc(tab_done, 16)
            pool.wait_ge(idx_ready, 1)
            pool.wait_ge(x2_out[0], 16 * ((NT + 1) // 2))
            pool.wait_ge(x2_out[1], 16 * (NT // 2))

            def gather(p, e):
                if not isinstance(e, int) or e >= 2:
                    pool.wait_ge(bt_full, e - 1)
                c(pool.tensor_copy(curs[p][:, :], slots[:, bass.ds(e, 1)]))
                c.sync()
                c(carry())
                pool.indirect_dma_start(
                    out=xg[p][:, :], out_offset=None, in_=rows_d,
                    in_offset=bass.IndirectOffsetOnAxis(ap=curs[p][:, 0:1].bitcast(U32), axis=0),
                    bounds_check=T - 1, oob_is_err=False).then_inc(xg_in[p], 16)

            def scatter(p, e, before_it):
                pool.wait_ge(yb_ready, e + 1)
                if not isinstance(before_it, int) or before_it:
                    pool.wait_ge(y_out[p], 16 * before_it)
                c(pool.tensor_copy(curd[p][:, :], slotd[:, bass.ds(e, 1)]))
                c.sync()
                c(carry())
                pool.indirect_dma_start(
                    out=res_d, out_offset=bass.IndirectOffsetOnAxis(ap=curd[p][:, 0:1].bitcast(U32), axis=0),
                    in_=yb[p][:, :], in_offset=None, bounds_check=2 * T - 1, oob_is_err=False).then_inc(y_out[p], 16)

            for e in range(4):
                gather(e % 2, e)
                if e >= 3:
                    scatter(0, 0, 0)
            for e in range(1, 3):
                gather(1 - e % 2, e + 3)
                scatter(e % 2, e, e // 2)
            loops = (NE - 4) // 2
            with pool.Fori(0, loops) as i:
                c.enter(i, 8)
                for p in range(2):
                    gather(p, i * 2 + (6 + p))
                    scatter(1 - p, i * 2 + (3 + p), i + (1 + p))
                c.leave(loops)
            scatter(1, NE - 1, NE // 2 - 1)
            pool.wait_ge(xinfo_ready, 1)
            nx = pool.value_load(xinfo[0:1, XB:XB + 1], min_val=0, max_val=XB)
            for p in range(2):
                pool.wait_ge(y_out[p], 16 * NE // 2)
                pool.wait_ge(xg_in[p], 16 * (NE + 2) // 2)
            with pool.Fori(0, XB) as j:
                with pool.If(nx > j):
                    pool.tensor_copy(curs[0][:, :], slots[:, bass.ds(j + NE, 1)]).then_inc(e_cur, 1)
                    pool.tensor_copy(curd[0][:, :], slotd[:, bass.ds(j + NE, 1)]).then_inc(e_cur, 1)
                    pool.wait_ge(e_cur, j * 5 + 2)
                    carry().then_inc(e_cur, 1)
                    pool.indirect_dma_start(
                        out=xg[0][:, :], out_offset=None, in_=rows_d,
                        in_offset=bass.IndirectOffsetOnAxis(ap=curs[0][:, 0:1].bitcast(U32), axis=0),
                        bounds_check=T - 1, oob_is_err=False).then_inc(e_xg, 16)
                    pool.wait_ge(e_cur, j * 5 + 3)
                    pool.wait_ge(e_yb, j + 2)
                    carry().then_inc(e_cur, 1)
                    pool.indirect_dma_start(
                        out=res_d, out_offset=bass.IndirectOffsetOnAxis(ap=curd[0][:, 0:1].bitcast(U32), axis=0),
                        in_=yb[0][:, :], in_offset=None, bounds_check=2 * T - 1,
                        oob_is_err=False).then_inc(e_out, 16)
                    pool.wait_ge(e_cur, j * 5 + 4)
                    pool.wait_ge(e_out, j * 16 + 16)
                    carry().then_inc(e_cur, 1)
            pool.memset(ms[:, 31:32], 0.0).then_inc(moe_done, 1)
            for i in range(NT):
                rms(2 * NT + NPT + 1 + i, 24 + i, 25 + i, D, ND if i == NPT else P)

        @block.scalar
        def _(act):
            c = Chain(act, c_act)
            copy = act.copy

            def carry():
                c.sync()
                c(act.mul(gnh[:, 3:4], gnh[:, 0:1], 1.0))

            def high(par, half):
                act.wait_ge(raw_in[par], 16 * half + 16)
                if not isinstance(half, int) or half:
                    act.wait_ge(w_used, 2 * half + (par - 1))
                copy(wh[par][:, :], raw[par][:, :]).then_inc(hi_ready, 1)

            for i in range(NT):
                act.wait_ge(x_in[i], 16)
                if i:
                    act.wait_ge(sq_done, i)
                act.activation(junk1[:, :], xin[:, i, :], ACT.Square, accum_out=ss[:, i:i + 1]).then_inc(sq_done, 1)
            act.wait_ge(a_in, 16)
            copy(ah[:, :, :], rawa[:, :, :]).then_inc(ah_ready, 1)
            high(0, 0)
            high(1, 0)
            for i in range(NT):
                act.wait_ge(xt_full, i + 1)
                b = TB + 2 * (i % 2)
                copy(xh[:, :, i * P:(i + 1) * P], ps[:, b:b + 2, :].rearrange("p a (c t) -> p (a c) t", t=P)
                     ).then_inc(xh_ready, 1)
            act.wait_ge(unit_full, 1)
            c(copy(aT[:, 0:SEQ], ps[0:RANK, 0, :]))
            copy(aT[:, SEQ:T], ps[0:RANK, 1, 0:ND]).then_inc(unit_free[0], 1)
            act.wait_ge(small_in, 16 * NSMALL)
            c(act.mul(gnh[:, 0:DV // P], gn[:, :], 0.5))
            act.wait_ge(la_ready, 1)
            for hd in range(H):
                n = N_AL + hd
                bank = 2 * (n % 2)
                act.wait_ge(unit_full, n + 1)
                if hd:
                    act.wait_ge(la_ready, hd + 1)
                c(act.activation(abt[:, 0:SEQ], ps[:, bank, :], ACT.Abs, bias=balpha[:, hd:hd + 1]))
                c(act.activation(abt[:, SEQ:T], ps[:, bank + 1, 0:ND], ACT.Abs, bias=balpha[:, hd:hd + 1]))
                c.sync()
                c(act.activation(abt[:, :], abt[:, :], ACT.Exp, scale=-1.0))
                c.sync()
                act.activation(abt[:, :], abt[:, :], ACT.Ln, bias=1.0).then_inc(ls_act, 1)
            act.wait_ge(unit_full, N_SC + 1)
            copy(hist[:, :, :], ps[:, 2, 0:H * DB * 2].rearrange("p (c s) -> p c s", c=H)).then_inc(unit_free[1], 1)

            def pair_view(par):
                return pair[par][:, :, 0:HALF]

            def halves(ap):
                return ap.rearrange("p (a t) -> p a t", a=2)

            with act.Fori(0, 2) as i:
                for p in range(2):
                    g = i * 2 + p
                    for u in range(2):
                        wait_unit(act, g, g, u, 2, 6)
                        copy(qk[:, bass.ds(i * 4 + (2 * p + u), 1), :].rearrange("p b (a t) -> p (b a) t", a=2),
                             pair_view(u)).then_inc(unit_free[u], 1)
                    high(p, i + 1)
            with act.Fori(0, 2) as i:
                for p in range(2):
                    k = i * 2 + p
                    for t in range(NT):
                        u = (NT * p + t) % 2
                        wait_unit(act, k + G_V, k, t, NT, 10)
                        copy(v[:, t, bass.ds(k * 256, 256)], ps[:, 2 * u, 0:256]).then_inc(unit_free[u], 1)
                    high(p, i + (G_V // 2 + 1))
            act.mul(gnh[:, 2:3], gnh[:, 0:1], 1.0).then_inc(on_ready, 1)
            with act.Fori(0, NPT // 2) as i:
                c.enter(i, 2 * (4 + 2 * (H - 1)))
                for p in range(2):
                    j = i * 2 + p
                    act.wait_ge(scans_done, j + 1)
                    c(act.activation(eb[:, :, :], bt[:, :, :], ACT.Exp, scale=1 / GATE_NORM))
                    act.activation(ec[:, :, :], bc[:, :, :], ACT.Exp, scale=1 / GATE_NORM).then_inc(ebec_done, 1)
                    act.wait_ge(diffs_done, j + 1)
                    c(act.activation(kst[:, :, :], kst[:, :, :], ACT.Exp, scale=1 / GATE_NORM))
                    act.activation(dif[:, :, :], dif[:, :, :], ACT.Exp, scale=1 / GATE_NORM).then_inc(exps_done, 1)
                    for u in range(2):
                        wait_unit(act, j + G_G, j, u, 2, 26)
                        act.wait_ge(sg_ready, j * 2 + (u + 1))
                        act.activation(halves(ta[:, :]), pair_view(u), ACT.Tanh, scale=0.5).then_inc(g_act, 1)
                        act.activation(halves(tb[:, :]), pair_view(u), ACT.Copy,
                                       scale=gnh[:, u:u + 1]).then_inc(unit_free[u], 1)
                        if u == 0:
                            act.wait_ge(p1_full, j + 1)
                            copy(kt[:, :, :], ps[:, TB + 1, :].rearrange("p (h d) -> p h d", h=H)
                                 ).then_inc(kt_ready, 1)
                    act.wait_ge(kv_full, j + 1)
                    carry()
                    for hd in range(H):
                        src = ps[:, UB + hd // 2, (hd % 2) * DV:(hd % 2 + 1) * DV]
                        ins = act.activation(v[:, bass.ds(j, 1), hd * DV:(hd + 1) * DV].rearrange("p a b -> p (a b)"),
                                             src, ACT.Square,
                                             accum_out=ss[:, 8 + 4 * p + hd:9 + 4 * p + hd])
                        if hd == H - 1:
                            ins.then_inc(sq_done, 1)
                        else:
                            c(ins)
                    act.wait_ge(rs_ready, j + (NT + 1))
                    carry()
                    for hd in range(H):
                        src = ps[:, UB + hd // 2, (hd % 2) * DV:(hd % 2 + 1) * DV]
                        ins = act.activation(v[:, bass.ds(j, 1), hd * DV:(hd + 1) * DV].rearrange("p a b -> p (a b)"),
                                             src, ACT.Copy, scale=rs[:, 8 + 4 * p + hd:9 + 4 * p + hd])
                        if hd == H - 1:
                            ins.then_inc(on_ready, 1)
                        else:
                            c(ins)
                    high(p, i + (G_G // 2 + 1))
                c.leave(NPT // 2)
            act.wait_ge(scans_done, NPT + 1)
            c(act.activation(eb[:, :, :], bt[:, :, :], ACT.Exp, scale=1 / GATE_NORM))
            act.activation(ql[:, :, :], bt[:, :, :], ACT.Exp, scale=-1 / GATE_NORM).then_inc(ebec_done, 1)
            act.wait_ge(diffs_done, NPT + 1)
            act.activation(kst[:, :, 0:ND], kst[:, :, 0:ND], ACT.Exp, scale=1 / GATE_NORM).then_inc(exps_done, 1)
            act.wait_ge(p1_full, NPT + 1)
            copy(kt[0:ND, :, :], ps[0:ND, TB + 1, :].rearrange("p (h d) -> p h d", h=H)).then_inc(kt_ready, 1)
            act.wait_ge(o_full, 1)
            act.wait_ge(dkv_full, DB)
            for hd in range(H):
                src = ps[0:ND, UB + hd // 2, (hd % 2) * DV:(hd % 2 + 1) * DV]
                ins = act.activation(v[0:ND, NPT, hd * DV:(hd + 1) * DV], src, ACT.Square,
                                     accum_out=ss[0:ND, 8 + hd:9 + hd])
                if hd == H - 1:
                    ins.then_inc(sq_done, 1)
                else:
                    c(ins)
            act.wait_ge(rs_ready, NT + NPT + 1)
            for hd in range(H):
                src = ps[0:ND, UB + hd // 2, (hd % 2) * DV:(hd % 2 + 1) * DV]
                ins = act.activation(v[0:ND, NPT, hd * DV:(hd + 1) * DV], src, ACT.Copy,
                                     scale=rs[0:ND, 8 + hd:9 + hd])
                if hd == H - 1:
                    ins.then_inc(on_ready, 1)
                else:
                    c(ins)
            act.wait_ge(st_store, 16 * DB)
            for t in range(2):
                g0 = G_CONV + 3 * t
                for u in range(2):
                    wait_unit(act, g0, 3 * t, u, 2, 30)
                    if t:
                        act.wait_ge(z_ready, 2 * t)
                    copy(halves(tmp[u][:, :]), pair_view(u)).then_inc(unit_free[u], 1)
                high(g0 % 2, g0 // 2 + 1)
                high((g0 + 1) % 2, (g0 + 1) // 2 + 1)
                for u in range(2):
                    act.wait_ge(z_mul, 2 * t + u + 1)
                    copy(zh[:, 2 * t + u, :], tmp[u][:, :]).then_inc(z_hi, 1)
                high((g0 + 2) % 2, (g0 + 2) // 2 + 1)
            for g in range(G_CO, G_GA):
                for u in range(4):
                    wait_unit(act, g, g - G_CO, u, 4, 36)
                    copy(halves(m1[:, 4 * (g - G_CO) + u, :]), pair_view(u % 2)).then_inc(unit_free[u % 2], 1)
                high(g % 2, g // 2 + 1)
                if g == G_CO:
                    act.wait_ge(cs_full, 1)
                    copy(cso[:, :], ps[0:2 + 2 * DB, TB, :]).then_inc(cso_ready, 1)
            with act.Fori(0, 2) as i:
                for p in range(2):
                    k = i * 2 + p
                    for u in range(2):
                        wait_unit(act, k + G_GA, k, u, 2, 42)
                        act.wait_ge(m1_ready, k * 2 + (u + 1))
                        act.activation(halves(tmp[u][:, :]), pair_view(u), ACT.Sigmoid).then_inc(unit_free[u], 1)
                    high(p, i + (G_GA // 2 + 1))
            with act.Fori(0, 2) as i:
                c.enter(i, 4)
                for p in range(2):
                    k = i * 2 + p
                    for u in range(2):
                        wait_unit(act, k + G_GB, k, u, 2, 46)
                        carry()
                        act.activation(sgb[:, bass.ds(k * 2 + u, 1), :].rearrange("p b (a t) -> p (b a) t", a=2),
                                       pair_view(u), ACT.Sigmoid).then_inc(unit_free[u], 1)
                    high(p, i + (G_GB // 2 + 1))
                c.leave(2)
            for j in range(NT):
                n = ND if j == NPT else P
                for b in range(2):
                    act.wait_ge(og_mul, 2 * j + b + 1)
                    copy(xh[:, 4 * b:4 * b + 4, j * P:j * P + n],
                         tmp[b][:, 0:4 * n].rearrange("p (c t) -> p c t", c=4)).then_inc(og_hi, 1)
            with act.Fori(0, 2) as i:
                for p in range(2):
                    k = i * 2 + p
                    for u in range(2):
                        act.wait_ge(m_mul, k * 2 + (u + 1))
                        copy(mh[:, bass.ds(k * 2 + u, 1), 0:T].rearrange("p a t -> p (a t)"),
                             tmp[u][:, :]).then_inc(m_hi, 1)
                    high(p, i + (G_GO // 2 + 1))
            for g in range(G_WO, G_WO + 2):
                high(g % 2, g // 2 + 1)
            for i in range(NT):
                act.wait_ge(h_ready, 4 * NT - (NT - 1 - i))
                act.wait_ge(sq_done, NT + NPT + 1 + i)
                act.activation(junk[:, :], h[:, i, :], ACT.Square, accum_out=ss[:, 16 + i:17 + i]).then_inc(sq_done, 1)
            for i in range(NT):
                act.wait_ge(x2t_full, i + 1)
                if i >= 2:
                    act.wait_ge(lg_full, i - 1)
                b = TB + 2 * (i % 2)
                copy(xr[i % 2][:, :, :], ps[:, b:b + 2, :].rearrange("p a (c t) -> p (a c) t", t=P)
                     ).then_inc(xr_ready, 1)

            def expert_high(m0, i=0):
                s = (m0 + 2) % 6
                act.wait_ge(raw_in[s], 16 * i + 16 * raw_count(m0))
                act.wait_ge(w_used, 6 * i + (G_END + max(m0 - 2, 0)))
                copy(wh[m0 % 3][:, :], raw[s][:, :]).then_inc(hi_ready, 1)

            for m in range(3):
                expert_high(m)
            for n, (dst, src) in enumerate(((rt["gx"], rt["gd"]), (rt["ex"], rt["dd"]))):
                act.wait_ge(r_dve, n + 1)
                act.activation(dst[:], src[:], ACT.Exp).then_inc(r_act, 1)

            def block_high(e0, i=0):
                act.wait_ge(bt_full, 2 * i + (e0 + 1))
                if e0 >= 2:
                    act.wait_ge(w_used, 6 * i + (G_END + 3 * e0 - 5))
                copy(gh[e0 % 2][:, :, 0:B], ps[:, TB + 2 * (e0 % 2), :].rearrange("p (k t) -> p k t", k=KD)
                     ).then_inc(bh_ready, 1)

            def silu(e0, i=0):
                act.wait_ge(w_used, 6 * i + (G_END + max(3 * e0 - 1, 0) + 1))
                act.activation(si[e0 % 2][:, :], ps[0:B, 0, 0:DE], ACT.Silu).then_inc(si_ready, 1)

            def hidden_high(e0, i=0):
                act.wait_ge(ht_full, 2 * i + (e0 + 1))
                copy(hh[e0 % 2][:, :, 0:B], ps[:, TB + 1 + 2 * (e0 % 2), 0:2 * B].rearrange("p (k t) -> p k t", k=2)
                     ).then_inc(hh_ready, 1)

            def result(e0, i=0):
                act.wait_ge(w_used, 6 * i + (G_END + (3 * e0 + 5 if e0 < NE - 1 else 3 * NE)))
                if e0 >= 2:
                    act.wait_ge(y_out[e0 % 2], 16 * i + 16 * (e0 // 2))
                copy(yb[e0 % 2][:, :].rearrange("p (a c) -> p a c", a=2), ps[0:B, 2:4, :]).then_inc(yb_ready, 1)

            act.wait_ge(moe_zero, 1)
            block_high(0)
            silu(0)
            block_high(1)
            expert_high(3)
            hidden_high(0)
            expert_high(4)
            silu(1)
            block_high(2)
            expert_high(5)
            expert_high(6)
            hidden_high(1)
            result(0)
            expert_high(7)

            def step(e0, i=0):
                silu(e0, i)
                block_high(e0 + 1, i)
                if e0 < NE - 1:
                    expert_high(3 * e0 + 2, i)
                    expert_high(3 * e0 + 3, i)
                hidden_high(e0, i)
                result(e0 - 1, i)
                expert_high(3 * e0 + 4 if e0 < NE - 1 else 3 * NE - 1, i)

            with act.Fori(0, (NE - 4) // 2) as i:
                step(2, i)
                step(3, i)
            step(NE - 2)
            step(NE - 1)
            result(NE - 1)
            act.wait_ge(xinfo_ready, 1)
            nx = act.value_load(xinfo[0:1, XB:XB + 1], min_val=0, max_val=XB)
            act.mul(gnh[:, 2:3], gnh[:, 0:1], 1.0).then_inc(e_yb, 1)
            with act.Fori(0, XB) as j:
                with act.If(nx > j):
                    act.wait_ge(e_xt, j + 1)
                    copy(gh[0][:, :, 0:B], ps[:, TB, :].rearrange("p (k t) -> p k t", k=KD)).then_inc(e_bh, 1)
                    act.wait_ge(e_raw, j * 48 + 48)
                    for s in range(3):
                        copy(wh[s][:, :], raw[s][:, :]).then_inc(e_hi, 1)
                    act.wait_ge(e_gu, j + 1)
                    act.activation(si[0][:, :], ps[0:B, 0, 0:DE], ACT.Silu).then_inc(e_si, 1)
                    act.wait_ge(e_ht, j + 1)
                    copy(hh[0][:, :, 0:B], ps[:, TB + 1, 0:2 * B].rearrange("p (k t) -> p k t", k=2)).then_inc(e_hh, 1)
                    act.wait_ge(e_y, j + 1)
                    copy(yb[0][:, :].rearrange("p (a c) -> p a c", a=2), ps[0:B, 2:4, :]).then_inc(e_yb, 1)
            for i in range(NT):
                n = ND if i == NPT else P
                act.wait_ge(hf_ready, i + 1)
                act.wait_ge(sq_done, 2 * NT + NPT + 1 + i)
                act.activation(junk[0:n, :], h[0:n, i, :], ACT.Square,
                               accum_out=ss[0:n, 24 + i:25 + i]).then_inc(sq_done, 1)


        def last_norm(dve, i):
            n = ND if i == NPT else P
            dve.wait_ge(rs_ready, 2 * NT + NPT + 1 + i + 1)
            if i >= 2:
                dve.wait_ge(yo_out[i % 2], 16 * (i // 2))
            dve.scalar_tensor_tensor(yo[i % 2][0:n, :], h[0:n, i, :], rs[0:n, 24 + i:25 + i], nlb[0:n, :],
                                     ALU.mult, ALU.mult).then_inc(yo_ready, 1)

        @block.vector
        def _(dve):
            c = Chain(dve, c_dve)
            tt, ts, stt = dve.tensor_tensor, dve.tensor_scalar, dve.scalar_tensor_tensor

            marks = iter(range(63))

            def signal(sem):
                col = next(marks)
                dve.memset(mark[:, col:col + 1], 0.0).then_inc(sem, 1)

            def low(par, half):
                dve.wait_ge(hi_ready, 2 * half + (par + 1))
                tt(wl[par][:, :], raw[par][:, :], wh[par][:, :].bitcast(F32), ALU.subtract).then_inc(lo_ready, 1)

            dve.memset(xin[ND:P, NPT, :], 0.0).then_inc(dve_const, 1)
            dve.wait_ge(nm_in, 16)

            def low_of_x(i):
                dve.wait_ge(xh_ready, i + 1)
                b = TB + 2 * (i % 2)
                tt(xl[:, :, i * P:(i + 1) * P], ps[:, b:b + 2, :].rearrange("p a (c t) -> p (a c) t", t=P),
                   xh[:, :, i * P:(i + 1) * P].bitcast(F32), ALU.subtract).then_inc(xt_free, 1)

            for i in range(NT):
                dve.wait_ge(rs_ready, i + 1)
                if i >= 2:
                    dve.wait_ge(xt_full, i - 1)
                stt(xn[i % 2][:, :], xin[:, i, :], rs[:, i:i + 1], nmb[:, :], ALU.mult, ALU.mult).then_inc(xn_ready, 1)
                if i == 1:
                    dve.wait_ge(ah_ready, 1)
                    tt(al[:, :, :], rawa[:, :, :], ah[:, :, :].bitcast(F32), ALU.subtract).then_inc(al_ready, 1)
                if i >= 1:
                    low_of_x(i - 1)
            low_of_x(NT - 1)
            low(0, 0)
            low(1, 0)
            dve.wait_ge(unit_full, 1)
            c(dve.memset(la[:, NPT, :, :], 0.0))
            c(dve.memset(m_tile[:, :, :], 1.0))
            c(dve.memset(m_ch[:, :, :], 1.0))
            c(dve.memset(m_seq[:, :, :], 1.0))
            c(dve.memset(sc[:, :, :], 0.0))
            c(dve.memset(qg[:, :, :], 0.0))
            c.sync()
            c(dve.memset(m_tile[:, :, 0:1], 0.0))
            c(dve.memset(m_ch[:, :, :].rearrange("p h (n t) -> p h n t", t=CH)[:, :, :, 0:1], 0.0))
            c(dve.memset(m_seq[:, :, :].rearrange("p h (n t) -> p h n t", t=DS)[:, :, :, 0:1], 0.0))
            dve.wait_ge(pool_const, 1)
            c(dve.tensor_copy(causal[:, :], causal_f[:, :]))
            c(dve.tensor_copy(causal8[:, :], causal8_f[:, :]))
            c.sync()
            signal(la_ready)
            for hd in range(H):
                n = N_AL + hd
                bank = 2 * (n % 2)
                dve.wait_ge(ls_act, hd + 1)
                c(ts(mnt[:, 0:SEQ], ps[:, bank, :], balpha[:, hd:hd + 1], 0.0, ALU.add, ALU.min))
                ts(mnt[:, SEQ:T], ps[:, bank + 1, 0:ND], balpha[:, hd:hd + 1], 0.0, ALU.add,
                   ALU.min).then_inc(unit_free[n % 2], 1)
                c.sync()
                dve.wait_ge(unit_free[n % 2], n // 2 + 1)
                c(tt(la[:, 0:NPT, hd, :], mnt[:, 0:SEQ].rearrange("p (j t) -> p j t", t=P),
                     abt[:, 0:SEQ].rearrange("p (j t) -> p j t", t=P), ALU.subtract))
                tt(la[:, NPT, hd, 0:ND], mnt[:, SEQ:T], abt[:, SEQ:T], ALU.subtract).then_inc(la_ready, 1)
            c.sync()
            dve.wait_ge(la_ready, H + 1)
            with dve.Fori(0, (G_G - G_QK) // 2) as i:
                for p in range(2):
                    low(p, i + 1)
            S_zero = dve.memset(S[:, :, :], 0.0)
            S_zero.then_inc(s_ready, 1)
            signal(sg_ready)
            per = 2 * (6 + 3 * (NCH - 1) + (H - 1))
            with dve.Fori(0, NPT // 2) as i:
                c.enter(i, per)
                for p in range(2):
                    j = i * 2 + p
                    if p == 0:
                        toks = bass.ds(i * (2 * P), P)
                    else:
                        toks = bass.ds(i * (2 * P) + P, P)
                    q_j, k_j = qk[:, 0:H, toks], qk[:, H:2 * H, toks]
                    ls_j = la[:, bass.ds(j, 1), :, :].rearrange("p a h t -> p (a h t)")
                    c(dve.tensor_tensor_scan(bt[:, :, :].rearrange("p h t -> p (h t)"),
                                             m_tile[:, :, :].rearrange("p h t -> p (h t)"), ls_j, 0.0,
                                             ALU.mult, ALU.add))
                    dve.tensor_tensor_scan(bc[:, :, :].rearrange("p h t -> p (h t)"),
                                           m_ch[:, :, :].rearrange("p h t -> p (h t)"), ls_j, 0.0,
                                           ALU.mult, ALU.add).then_inc(scans_done, 1)
                    c.sync()
                    c(tt(kst[:, :, :], bt[:, :, P - 1:P].to_broadcast((P, H, P)), bt[:, :, :], ALU.subtract))
                    off = 0
                    for n in range(NCH):
                        w = CH * (n + 1)
                        if n == 0:
                            ins = ts(dif[:, :, 0:w], bt[:, :, 0:w], -1.0, None, ALU.mult)
                        else:
                            ins = tt(dif[:, :, off:off + w], bt[:, :, CH * n - 1:CH * n].to_broadcast((P, H, w)),
                                     bt[:, :, 0:w], ALU.subtract)
                        if n == NCH - 1:
                            ins.then_inc(diffs_done, 1)
                        else:
                            c(ins)
                        off += w
                    dve.wait_ge(ebec_done, j + 1)
                    c(stt(qg[:, :, :], eb[:, :, :], QSCALE, q_j, ALU.mult, ALU.mult))
                    c(stt(ql[:, :, :], ec[:, :, :], QSCALE, q_j, ALU.mult, ALU.mult))
                    dve.wait_ge(exps_done, j + 1)
                    c(tt(kst[:, :, :], kst[:, :, :], k_j, ALU.mult))
                    off = 0
                    for n in range(NCH):
                        w = CH * (n + 1)
                        kk = qk[:, H:2 * H, bass.ds(i * (2 * P) + P * p, w)]
                        ins = tt(kiv[:, :, off:off + w], dif[:, :, off:off + w], kk, ALU.mult)
                        if n == NCH - 1:
                            ins.then_inc(gla_in, 1)
                        else:
                            c(ins)
                        off += w
                    for u in range(2):
                        dve.wait_ge(g_act, j * 2 + (u + 1))
                        dve.wait_ge(unit_free[u], j + (N_G // 2 + 1))
                        stt(sg[:, bass.ds(j * 2 + u, 1), :].rearrange("p a t -> p (a t)"), ta[:, :], 1.0, tb[:, :],
                            ALU.add, ALU.mult).then_inc(sg_ready, 1)
                        if u == 0:
                            dve.wait_ge(p1_full, j + 1)
                            c(dve.memset(mark[:, 63:64], 0.0))
                            for n in range(NCH):
                                w = CH * (n + 1)
                                q0 = CH * n
                                ins = dve.copy_predicated(
                                    sc[0:w, :, q0:q0 + CH],
                                    causal[0:w, q0:q0 + CH].rearrange("p (a t) -> p a t", a=1).to_broadcast((w, H, CH)),
                                    ps[0:w, TB, :].rearrange("p (h t) -> p h t", h=H)[:, :, q0:q0 + CH])
                                if n == NCH - 1:
                                    ins.then_inc(sc_ready, 1)
                                else:
                                    c(ins)
                    dve.wait_ge(kv_full, j + 1)
                    for hd in range(H):
                        ins = stt(S[:, hd, :], S[:, hd, :], eb[:, hd, P - 1:P],
                                  ps[:, TB + hd // 2, (hd % 2) * DV:(hd % 2 + 1) * DV], ALU.mult, ALU.add)
                        if hd == H - 1:
                            ins.then_inc(s_ready, 1)
                        else:
                            c(ins)
                    low(p, i + (G_G // 2 + 1))
                c.leave(NPT // 2)
            dve.wait_ge(sg_ready, 2 * NPT + 1)
            qd, kd = qk[:, 0:H, SEQ:T], qk[:, H:2 * H, SEQ:T]
            seqs = lambda ap: ap.rearrange("p h (s t) -> p h s t", t=DS)
            c(dve.tensor_tensor_scan(bt[:, :, :].rearrange("p h t -> p (h t)"),
                                     m_seq[:, :, :].rearrange("p h t -> p (h t)"),
                                     la[:, NPT, :, :].rearrange("p h t -> p (h t)"), 0.0, ALU.mult, ALU.add))
            c(dve.memset(qm[:, :, :, :], 0.0))
            c(dve.memset(sc[:, :, :], 0.0))
            c.sync()
            signal(scans_done)
            for hd in range(H):
                b_s = bt[:, hd, 0:ND].rearrange("p (s t) -> p s t", t=DS)
                ins = tt(kst[:, hd, 0:ND].rearrange("p (s t) -> p s t", t=DS),
                         b_s[:, :, DS - 1:DS].to_broadcast((P, DB, DS)), b_s, ALU.subtract)
                if hd == H - 1:
                    ins.then_inc(diffs_done, 1)
                else:
                    c(ins)
            dve.wait_ge(ebec_done, NPT + 1)
            c(stt(qg[:, :, 0:ND], eb[:, :, 0:ND], QSCALE, qd, ALU.mult, ALU.mult))
            c(tt(ql[:, :, 0:ND], ql[:, :, 0:ND], kd, ALU.mult))
            dve.wait_ge(exps_done, NPT + 1)
            c(tt(kst[:, :, 0:ND], kst[:, :, 0:ND], kd, ALU.mult))
            c.sync()
            for s in range(DB):
                t = slice(s * DS, (s + 1) * DS)
                ins = dve.tensor_copy(qm[:, s, :, t], qg[:, :, t])
                if s == DB - 1:
                    ins.then_inc(gla_in, 1)
                else:
                    c(ins)
            c.sync()
            signal(gla_in)
            dve.wait_ge(p1_full, NPT + 1)
            dve.copy_predicated(
                sc[0:ND, :, 0:ND], causal8[:, :].rearrange("p (a t) -> p a t", a=1).to_broadcast((ND, H, ND)),
                ps[0:ND, TB, :].rearrange("p (h t) -> p h t", h=H)[:, :, 0:ND]).then_inc(sc_ready, 1)
            for s in range(DB):
                dve.wait_ge(dkv_full, s + 1)
                dve.wait_ge(st_load[s % 3], 16 * (s // 3 + 1))
                for hd in range(H):
                    ins = stt(s0[s % 3][:, hd, :], s0[s % 3][:, hd, :], eb[:, hd, s * DS + DS - 1:s * DS + DS],
                              ps[:, TB + hd // 2, (hd % 2) * DV:(hd % 2 + 1) * DV], ALU.mult, ALU.add)
                    if hd == H - 1:
                        ins.then_inc(st_ready, 1)
                    else:
                        c(ins)
            dve.wait_ge(st_store, 16 * DB)
            dve.wait_ge(o_full, 1)
            c(dve.memset(up[:, :, 0:2], 0.0))
            c(dve.tensor_copy(ud[:, :, :, 0:2], hist[:, :, :].rearrange("p c (s w) -> p c s w", w=2)))
            for t in range(2):
                g0 = G_CONV + 3 * t
                uses = N_CONV // 2 + 3 * t
                for u in range(2):
                    ct = 2 * t + u
                    dve.wait_ge(unit_free[u], uses + 1)
                    wait_unit(dve, g0 + 1, 3 * t + 1, u, 2, 30)
                    c(tt(up[:, ct, 2:2 + HALF], pair[u][:, 0, 0:HALF], tmp[u][:, 0:HALF], ALU.mult))
                    c(tt(up[:, ct, 2 + HALF:2 + SEQ], pair[u][:, 1, 0:SEQ - HALF], tmp[u][:, HALF:SEQ], ALU.mult))
                    tt(ud[:, ct, :, 2:2 + DS], pair[u][:, 1, SEQ - HALF:HALF].rearrange("p (s t) -> p s t", t=DS),
                       tmp[u][:, SEQ:T].rearrange("p (s t) -> p s t", t=DS), ALU.mult).then_inc(unit_free[u], 1)
                    c.sync()
                    dve.wait_ge(unit_free[u], uses + 2)
                    for w in range(3):
                        zp, zd = tmp[u][:, 0:SEQ], tmp[u][:, SEQ:T].rearrange("p (s t) -> p s t", t=DS)
                        tap = wtap[:, w, ct:ct + 1]
                        if w == 0:
                            c(ts(zp, up[:, ct, 0:SEQ], tap, None, ALU.mult))
                            c(ts(zd, ud[:, ct, :, 0:DS], tap, None, ALU.mult))
                        else:
                            c(stt(zp, up[:, ct, w:w + SEQ], tap, zp, ALU.mult, ALU.add))
                            c(stt(zd, ud[:, ct, :, w:w + DS], tap, zd, ALU.mult, ALU.add))
                        c.sync()
                    if u == 0:
                        low(g0 % 2, g0 // 2 + 1)
                    else:
                        low((g0 + 1) % 2, (g0 + 1) // 2 + 1)
                for u in range(2):
                    ct = 2 * t + u
                    wait_unit(dve, g0 + 2, 3 * t + 2, u, 2, 30)
                    z2 = tmp[u][:, :].rearrange("p (a t) -> p a t", a=2)
                    tt(z2, pair[u][:, :, 0:HALF], z2, ALU.mult).then_inc(z_mul, 1)
                    dve.wait_ge(z_mul, ct + 1)
                    signal(unit_free[u])
                    dve.wait_ge(z_hi, ct + 1)
                    tt(zl[:, ct, :], tmp[u][:, :], zh[:, ct, :].bitcast(F32), ALU.subtract).then_inc(z_ready, 1)
                low((g0 + 2) % 2, (g0 + 2) // 2 + 1)
            c(dve.tensor_copy(cs[:, :, 0:2], up[:, :, SEQ:SEQ + 2]))
            dve.tensor_copy(cs[:, :, 2:].rearrange("p c (s w) -> p c s w", w=2), ud[:, :, :, DS:DS + 2]
                            ).then_inc(cs_ready, 1)
            c.sync()
            low(G_CO % 2, G_CO // 2 + 1)
            low((G_CO + 1) % 2, (G_CO + 1) // 2 + 1)
            dve.wait_ge(z_ready, H)
            for _ in range(2):
                signal(m1_ready)
            with dve.Fori(0, 2) as i:
                for p in range(2):
                    k = i * 2 + p
                    for u in range(2):
                        dve.wait_ge(unit_free[u], k + (N_GA // 2 + 1))
                        m = m1[:, bass.ds(k * 2 + u, 1), :].rearrange("p a t -> p (a t)")
                        tt(m, m, tmp[u][:, :], ALU.mult).then_inc(m1_ready, 1)
                    low(p, i + (G_GA // 2 + 1))
            with dve.Fori(0, 2) as i:
                for p in range(2):
                    low(p, i + (G_GB // 2 + 1))
            for j in range(NT):
                n = ND if j == NPT else P
                dve.wait_ge(og_full, j + 1)
                for b in range(2):
                    t3 = tmp[b][:, 0:4 * n].rearrange("p (c t) -> p c t", c=4)
                    if j:
                        dve.wait_ge(og_ready, 2 * j + b - 1)
                    tt(t3, ps[:, TB + 2 * (j % 2) + b, :].rearrange("p (c t) -> p c t", t=P)[:, :, 0:n],
                       sg[:, 4 * b:4 * b + 4, j * P:j * P + n], ALU.mult).then_inc(og_mul, 1)
                for b in range(2):
                    t3 = tmp[b][:, 0:4 * n].rearrange("p (c t) -> p c t", c=4)
                    dve.wait_ge(og_hi, 2 * j + b + 1)
                    tt(xl[:, 4 * b:4 * b + 4, j * P:j * P + n], t3,
                       xh[:, 4 * b:4 * b + 4, j * P:j * P + n].bitcast(F32), ALU.subtract).then_inc(og_ready, 1)
            dve.wait_ge(og_ready, 2 * NT)
            c(dve.memset(mh[:, :, T:TP].bitcast(F32), 0.0))
            c(dve.memset(ml[:, :, T:TP].bitcast(F32), 0.0))
            c.sync()
            with dve.Fori(0, 2) as i:
                for p in range(2):
                    k = i * 2 + p
                    for u in range(2):
                        wait_unit(dve, k + G_GO, k, u, 2, 50)
                        t2 = tmp[u][:, :].rearrange("p (a t) -> p a t", a=2)
                        one = bass.ds(k * 2 + u, 1)
                        tt(t2, pair[u][:, :, 0:HALF], sgb[:, one, :].rearrange("p b (a t) -> p (b a) t", a=2),
                           ALU.mult).then_inc(unit_free[u], 1)
                        dve.wait_ge(unit_free[u], k + (N_GO // 2 + 1))
                        tt(tmp[u][:, :], tmp[u][:, :], m1[:, one, :].rearrange("p a t -> p (a t)"),
                           ALU.add).then_inc(m_mul, 1)
                        dve.wait_ge(m_hi, k * 2 + (u + 1))
                        tt(ml[:, one, 0:T].rearrange("p a t -> p (a t)"), tmp[u][:, :],
                           mh[:, one, 0:T].rearrange("p a t -> p (a t)").bitcast(F32), ALU.subtract).then_inc(m_ready, 1)
                    low(p, i + (G_GO // 2 + 1))
            dve.wait_ge(m_ready, 2 * (G_WO - G_GO))
            dve.wait_ge(w_used, G_WO)
            dve.memset(h[ND:P, NPT, :], 0.0).then_inc(dve_const, 1)
            dve.wait_ge(dve_const, 2)
            dve.wait_ge(h_in, 32)
            for g in range(G_WO, G_END):
                k = g - G_WO
                for t in range(NT):
                    u = (NT * k + t) % 2
                    wait_unit(dve, g, k, t, NT, 54)
                    hv = h[:, t, k * 256:(k + 1) * 256]
                    tt(hv, hv, ps[:, 2 * u, 0:256], ALU.add).then_inc(h_ready, 1)
                    dve.wait_ge(h_ready, NT * k + t + 1)
                    signal(unit_free[u])
                if g < G_WO + 2:
                    low(g % 2, g // 2 + 1)
            dve.wait_ge(nf_in, 32)
            for i in range(NT + 1):
                if i < NT:
                    dve.wait_ge(rs_ready, NT + NPT + 1 + i + 1)
                    if i >= 2:
                        dve.wait_ge(x2t_full, i - 1)
                        dve.wait_ge(x2_out[i % 2], 16 * (i // 2))
                    stt(x2[i % 2][:, :], h[:, i, :], rs[:, 16 + i:17 + i], nfb[:, :], ALU.mult,
                        ALU.mult).then_inc(x2_ready, 1)
                if i >= 1:
                    dve.wait_ge(lg_full, i)
                    tt(lg[:, i - 1, :], ps[:, (i - 1) % 2, 0:NR], rb[:, :], ALU.add).then_inc(lg_ready, 1)
            dve.wait_ge(lg_ready, NT)

            def expert_low(m0, i=0):
                dve.wait_ge(hi_ready, 6 * i + (G_END + m0 + 1))
                tt(wl[m0 % 3][:, :], raw[(m0 + 2) % 6][:, :], wh[m0 % 3][:, :].bitcast(F32),
                   ALU.subtract).then_inc(lo_ready, 1)

            r = rt
            dve.wait_ge(moe_zero, 1)

            def wide(ap, w):
                return ap.rearrange("p (j a) -> p j a", a=1).to_broadcast((P, NT, w))

            def step_(ins):
                c(ins)
                c.sync()

            gl_, el = lg[:, :, 0:NG], lg[:, :, NG:NR]
            step_(dve.tensor_reduce(r["gmax"][:, :], gl_, AX.X, ALU.max))
            tt(r["gd"][:, :, :], gl_, wide(r["gmax"][:, :], NG), ALU.subtract).then_inc(r_dve, 1)
            step_(tt(r["go"][:, :, :], gl_, wide(r["gmax"][:, :], NG), ALU.is_ge))
            step_(stt(r["gc"][:, :, :], r["go"][:, :, :], -64.0, ig[:, :, :], ALU.mult, ALU.add))
            step_(dve.tensor_reduce(r["gi"][:, :], r["gc"][:, :, :], AX.X, ALU.min))
            step_(tt(r["go"][:, :, :], r["gc"][:, :, :], wide(r["gi"][:, :], NG), ALU.is_equal))
            step_(ts(r["go"][:, :, :], r["go"][:, :, :], 1e30, -1e30, ALU.mult, ALU.add))
            for g in range(NG):
                step_(tt(r["em"][:, :, g * NEG:(g + 1) * NEG], el[:, :, g * NEG:(g + 1) * NEG],
                         r["go"][:, :, g:g + 1].to_broadcast((P, NT, NEG)), ALU.add))
            for k, (mx, ix, eo) in enumerate((("m1v", "i1", "e1"), ("m2v", "i2", "e2"))):
                step_(dve.tensor_reduce(r[mx][:, :], r["em"][:, :, :], AX.X, ALU.max))
                step_(tt(r["c1"][:, :, :], r["em"][:, :, :], wide(r[mx][:, :], NE), ALU.is_ge))
                step_(stt(r["c1"][:, :, :], r["c1"][:, :, :], -64.0, r["io"][:, :, :], ALU.mult, ALU.add))
                step_(dve.tensor_reduce(r[ix][:, :], r["c1"][:, :, :], AX.X, ALU.min))
                step_(tt(r[eo][:, :, :], r["c1"][:, :, :], wide(r[ix][:, :], NE), ALU.is_equal))
                if k == 0:
                    step_(stt(r["em"][:, :, :], r["e1"][:, :, :], -3e30, r["em"][:, :, :], ALU.mult, ALU.add))
                step_(ts(r["ek"][:, k, :], r[ix][:, :], 64.0, None, ALU.add))
            tt(r["dd"][:, :], r["m2v"][:, :], r["m1v"][:, :], ALU.subtract).then_inc(r_dve, 1)
            step_(tt(r["mk"][:, :, :], r["e1"][:, :, :], r["e2"][:, :, :], ALU.add))
            tt(r["mk"][:, :, :], r["mk"][:, :, :], wide(valid[:, :], NE), ALU.mult).then_inc(r_dve, 1)
            dve.wait_ge(r_pos, 1)
            step_(dve.tensor_copy(r["cnt"][:, :], ps[:, UB + 1, 0:NE]))
            step_(ts(cnt_i[:, :], r["cnt"][:, :], float(B - 1), None, ALU.add))
            step_(ts(cnt_i[:, :], cnt_i[:, :], B.bit_length() - 1, None, ALU.arith_shift_right))
            step_(dve.tensor_copy(r["nb"][:, :], cnt_i[:, :]))
            step_(ts(r["xe"][:, :], r["nb"][:, :], -1.0, 0.0, ALU.add, ALU.max))
            step_(dve.tensor_tensor_scan(r["ci"][:, :], r["oneb"][:, :], r["xe"][:, :], 0.0, ALU.mult, ALU.add))
            step_(tt(r["base"][:, :], r["ci"][:, :], r["xe"][:, :], ALU.subtract))
            step_(ts(r["base"][:, :], r["base"][:, :], float(NE - 1), None, ALU.add))
            for k, eo in enumerate(("e1", "e2")):
                step_(tt(r["pr"][:, :, :], r[eo][:, :, :], ps[:, UB, 0:NT * NE].rearrange("p (j e) -> p j e", e=NE),
                         ALU.mult))
                step_(dve.tensor_reduce(r["pk"][:, k, :], r["pr"][:, :, :], AX.X, ALU.add))
                step_(tt(r["pr"][:, :, :], r[eo][:, :, :],
                         r["base"][:, :].rearrange("p (a e) -> p a e", a=1).to_broadcast((P, NT, NE)), ALU.mult))
                step_(dve.tensor_reduce(r["bk"][:, k, :], r["pr"][:, :, :], AX.X, ALU.add))
            step_(dve.tensor_copy(r["pi"][:, :, :], r["pk"][:, :, :]))
            step_(ts(r["qi"][:, :, :], r["pi"][:, :, :], B.bit_length() - 1, None, ALU.arith_shift_right))
            step_(dve.tensor_copy(r["q"][:, :, :], r["qi"][:, :, :]))
            step_(ts(r["is0"][:, :, :], r["q"][:, :, :], 0.0, None, ALU.is_equal))
            step_(tt(r["bk"][:, :, :], r["bk"][:, :, :], r["q"][:, :, :], ALU.add))
            step_(tt(r["t1"][:, :, :], r["ek"][:, :, :], r["bk"][:, :, :], ALU.subtract))
            step_(tt(r["t1"][:, :, :], r["t1"][:, :, :], r["is0"][:, :, :], ALU.mult))
            step_(tt(r["bk"][:, :, :], r["bk"][:, :, :], r["t1"][:, :, :], ALU.add))
            step_(stt(r["t2"][:, :, :], r["q"][:, :, :], -float(B), r["pk"][:, :, :], ALU.mult, ALU.add))
            step_(stt(r["t2"][:, :, :], r["t2"][:, :, :], float(NBLK), r["bk"][:, :, :], ALU.mult, ALU.add))
            dve.tensor_copy(r["sl"][:, :, :], r["t2"][:, :, :]).then_inc(slot_ready, 1)
            dve.wait_ge(r_act, 1)
            step_(dve.tensor_reduce(r["gsum"][:, :], r["gx"][:, :, :], AX.X, ALU.add))
            step_(dve.reciprocal(r["gtop"][:, :], r["gsum"][:, :]))
            dve.wait_ge(r_act, 2)
            step_(ts(r["gsum"][:, :], r["ex"][:, :], 1.0, None, ALU.add))
            step_(dve.reciprocal(r["gsum"][:, :], r["gsum"][:, :]))
            step_(tt(wts[:, 0, :], r["gtop"][:, :], r["gsum"][:, :], ALU.mult))
            step_(tt(wts[:, 1, :], wts[:, 0, :], r["ex"][:, :], ALU.mult))
            step_(tt(gex[:, :, :], r["ci"][0:1, :].rearrange("p (a e) -> p a e", a=1).to_broadcast((1, XB, NE)),
                     iox[:, :, :], ALU.is_le))
            step_(dve.tensor_reduce(xf[:, 0:XB], gex[:, :, :], AX.X, ALU.add))
            step_(ts(xf[:, 0:XB], xf[:, 0:XB], float(NE - 1), None, ALU.min))
            step_(dve.tensor_copy(xf[:, XB:XB + 1], r["ci"][0:1, NE - 1:NE]))
            dve.tensor_copy(xinfo[:, :], xf[:, :]).then_inc(xinfo_ready, 1)
            dve.wait_ge(tab_load, 16)
            ts(slots[:, :], slotd[:, :], 1, None, ALU.arith_shift_right).then_inc(idx_ready, 1)
            for m in range(3):
                expert_low(m)

            def block_low(e0, i=0):
                p = e0 % 2
                dve.wait_ge(bh_ready, 2 * i + (e0 + 1))
                tt(gl[p][:, :, 0:B], ps[:, TB + 2 * p, :].rearrange("p (k t) -> p k t", k=KD),
                   gh[p][:, :, 0:B].bitcast(F32), ALU.subtract).then_inc(bl_ready, 1)

            def hidden(e0, i=0):
                p = e0 % 2
                dve.wait_ge(si_ready, 2 * i + (e0 + 1))
                dve.wait_ge(w_used, 6 * i + (G_END + (3 * e0 + 1 if e0 else 2)))
                tt(hm[p][:, :], si[p][:, :], ps[0:B, 1, 0:DE], ALU.mult).then_inc(hm_ready, 1)

            def hidden_low(e0, i=0):
                p = e0 % 2
                dve.wait_ge(hh_ready, 2 * i + (e0 + 1))
                tt(hl[p][:, :, 0:B], ps[:, TB + 1 + 2 * p, 0:2 * B].rearrange("p (k t) -> p k t", k=2),
                   hh[p][:, :, 0:B].bitcast(F32), ALU.subtract).then_inc(hl_ready, 1)

            block_low(0)
            block_low(1)
            expert_low(3)
            hidden(0)
            hidden_low(0)
            expert_low(4)
            block_low(2)
            expert_low(5)
            hidden(1)
            expert_low(6)
            hidden_low(1)
            expert_low(7)

            def step(e0, i=0):
                block_low(e0 + 1, i)
                if e0 < NE - 1:
                    expert_low(3 * e0 + 2, i)
                hidden(e0, i)
                if e0 < NE - 1:
                    expert_low(3 * e0 + 3, i)
                hidden_low(e0, i)
                expert_low(3 * e0 + 4 if e0 < NE - 1 else 3 * NE - 1, i)

            with dve.Fori(0, (NE - 4) // 2) as i:
                step(2, i)
                step(3, i)
            step(NE - 2)
            step(NE - 1)
            nx = dve.value_load(xinfo[0:1, XB:XB + 1], min_val=0, max_val=XB)
            with dve.Fori(0, XB) as j:
                with dve.If(nx > j):
                    dve.wait_ge(e_bh, j + 1)
                    tt(gl[0][:, :, 0:B], ps[:, TB, :].rearrange("p (k t) -> p k t", k=KD),
                       gh[0][:, :, 0:B].bitcast(F32), ALU.subtract).then_inc(e_bl, 1)
                    dve.wait_ge(e_hi, j * 3 + 3)
                    for s in range(3):
                        tt(wl[s][:, :], raw[s][:, :], wh[s][:, :].bitcast(F32), ALU.subtract).then_inc(e_lo, 1)
                    dve.wait_ge(e_si, j + 1)
                    tt(hm[0][:, :], si[0][:, :], ps[0:B, 1, 0:DE], ALU.mult).then_inc(e_hm, 1)
                    dve.wait_ge(e_hh, j + 1)
                    tt(hl[0][:, :, 0:B], ps[:, TB + 1, 0:2 * B].rearrange("p (k t) -> p k t", k=2),
                       hh[0][:, :, 0:B].bitcast(F32), ALU.subtract).then_inc(e_hl, 1)
            for i in range(NT):
                n = ND if i == NPT else P
                dve.wait_ge(y2_in[i % 2], 16 * (i // 2 + 1))
                step_(stt(h[0:n, i, :], y2[i % 2][0:n, 0, :], wts[0:n, 0, i:i + 1], h[0:n, i, :], ALU.mult, ALU.add))
                stt(h[0:n, i, :], y2[i % 2][0:n, 1, :], wts[0:n, 1, i:i + 1], h[0:n, i, :], ALU.mult,
                    ALU.add).then_inc(hf_ready, 1)
                if i >= 1:
                    last_norm(dve, i - 1)
            last_norm(dve, NT - 1)

        @block.tensor
        def _(pe):
            mm = pe.matmul

            def tiles(ap, k):
                return ap[:, :].rearrange("p (k c) -> p k c", k=k)

            def carry(bank):
                mm(ps[:, bank, 0:2], ident[:, :], ident[:, 0:2], start=True, stop=True)

            def free(u, uses):
                if not isinstance(uses, int) or uses:
                    pe.wait_ge(unit_free[u], uses)

            def three(outs, k_tiles, left, right):
                last = []
                for k in range(k_tiles):
                    for n, (a, b) in enumerate(((0, 0), (0, 1), (1, 0))):
                        for o, out in enumerate(outs):
                            last.append(mm(out, left(a, k), right(b, k, o), start=k == 0 and n == 0,
                                           stop=k == k_tiles - 1 and n == 2))
                return last[-1]

            def feature_unit(p, u, c, x, kt=KD, width=256):
                w = (tiles(wh[p], kt), tiles(wl[p], kt))
                return three([pair[u][:, 0, 0:HALF], pair[u][:, 1, 0:HALF]], kt,
                             lambda a, k: w[a][:, k, c * P:(c + 1) * P],
                             lambda b, k, o: x[b][:, k, o * HALF:(o + 1) * HALF])

            def token_unit(p, u, t, x):
                w = (tiles(wh[p], KD), tiles(wl[p], KD))
                return three([ps[:, 2 * u, 0:256]], KD, lambda a, k: x[a][:, k, t * P:(t + 1) * P],
                             lambda b, k, o: w[b][:, k, :])

            X, Z, M = (xh, xl), (zh, zl), (mh, ml)

            pe.wait_ge(pool_const, 1)
            for i in range(NT):
                pe.wait_ge(xn_ready, i + 1)
                if i >= 2:
                    pe.wait_ge(xt_free, i - 1)
                for k in range(KD):
                    ins = pe.transpose(ps[:, TB + 2 * (i % 2) + k // 4, (k % 4) * P:(k % 4 + 1) * P],
                                       xn[i % 2][:, k * P:(k + 1) * P], ident[:, :])
                ins.then_inc(xt_full, 1)
            pe.wait_ge(al_ready, 1)
            pe.wait_ge(xt_free, NT)
            aw = (ah, al)
            for a0, a1, bank in ((0, SEQ, 0), (SEQ, T, 1)):
                ins = three([ps[:, bank, 0:a1 - a0]], KD, lambda a, k: aw[a][:, k, :],
                            lambda b, k, o: X[b][:, k, a0:a1])
            ins.then_inc(unit_full, 1)
            pe.wait_ge(unit_free[0], 1)
            pe.wait_ge(small_in, 16 * NSMALL)
            for hd in range(H):
                n = N_AL + hd
                free(n % 2, n // 2)
                for a0, a1, half in ((0, SEQ, 0), (SEQ, T, 1)):
                    ins = mm(ps[:, 2 * (n % 2) + half, 0:a1 - a0], wau[:, hd * P:(hd + 1) * P], aT[:, a0:a1],
                             start=True, stop=True)
                ins.then_inc(unit_full, 1)
            free(1, N_SC // 2)
            for ct in range(H):
                ins = pe.transpose(ps[:, 2, ct * 2 * DB:(ct + 1) * 2 * DB], sct[:, ct * P:(ct + 1) * P],
                                   ident[0:2 * DB, 0:2 * DB])
            ins.then_inc(unit_full, 1)
            with pe.Fori(0, 2) as i:
                for p in range(2):
                    pe.wait_ge(lo_ready, i * 2 + (p + 1))
                    for u in range(2):
                        free(u, i * 2 + (N_QK // 2 + p))
                        feature_unit(p, u, u, X).then_inc(w_used if u else unit_full, 1)
            with pe.Fori(0, 2) as i:
                for p in range(2):
                    pe.wait_ge(lo_ready, i * 2 + (G_V + p + 1))
                    for t in range(NT):
                        u = (NT * p + t) % 2
                        free(u, i * NT + (N_V // 2 + (NT * p + t) // 2))
                        token_unit(p, u, t, X).then_inc(w_used if t == NT - 1 else unit_full, 1)
            with pe.Fori(0, NPT // 2) as i:
                for p in range(2):
                    j = i * 2 + p
                    pe.wait_ge(lo_ready, i * 2 + (G_G + p + 1))
                    free(0, i * 2 + (N_G // 2 + p))
                    feature_unit(p, 0, 0, X).then_inc(unit_full, 1)
                    pe.wait_ge(gla_in, j + 1)
                    pe.wait_ge(s_ready, j + 1)
                    for hd in range(H):
                        pe.transpose(ps[:, TB + 1, hd * P:(hd + 1) * P], kst[:, hd, :], ident[:, :])
                    off = 0
                    for n in range(NCH):
                        w = CH * (n + 1)
                        for hd in range(H):
                            q0 = hd * P + CH * n
                            ins = mm(ps[0:w, TB, q0:q0 + CH], kiv[:, hd, off:off + w], ql[:, hd, CH * n:CH * (n + 1)],
                                     start=True, stop=True)
                        off += w
                    ins.then_inc(p1_full, 1)
                    free(1, i * 2 + (N_G // 2 + p))
                    feature_unit(p, 1, 1, X).then_inc(w_used, 1)
                    pe.wait_ge(kt_ready, j + 1)
                    pe.wait_ge(sc_ready, j + 1)
                    pe.wait_ge(on_ready, j + 1)
                    for hd in range(H):
                        out = ps[:, UB + hd // 2, (hd % 2) * DV:(hd % 2 + 1) * DV]
                        mm(out, sc[:, hd, :], v[:, bass.ds(j, 1), hd * DV:(hd + 1) * DV].rearrange("p a c -> p (a c)"),
                           start=True, stop=False)
                        mm(out, qg[:, hd, :], S[:, hd, :], start=False, stop=True)
                    for hd in range(H):
                        ins = mm(ps[:, TB + hd // 2, (hd % 2) * DV:(hd % 2 + 1) * DV], kt[:, hd, :],
                                 v[:, bass.ds(j, 1), hd * DV:(hd + 1) * DV].rearrange("p a c -> p (a c)"),
                                 start=True, stop=True)
                    ins.then_inc(kv_full, 1)
            pe.wait_ge(gla_in, NPT + 2)
            pe.wait_ge(s_ready, NPT + 1)
            for hd in range(H):
                pe.transpose(ps[0:ND, TB + 1, hd * P:(hd + 1) * P], kst[:, hd, 0:ND], ident[:, :])
            for hd in range(H):
                ins = mm(ps[0:ND, TB, hd * P:hd * P + ND], ql[:, hd, 0:ND], qg[:, hd, 0:ND], start=True, stop=True)
            ins.then_inc(p1_full, 1)
            pe.wait_ge(kt_ready, NPT + 1)
            pe.wait_ge(sc_ready, NPT + 1)
            pe.wait_ge(on_ready, NPT + 1)
            for hd in range(H):
                mm(ps[0:ND, UB + hd // 2, (hd % 2) * DV:(hd % 2 + 1) * DV], sc[0:ND, hd, 0:ND],
                   v[0:ND, NPT, hd * DV:(hd + 1) * DV], start=hd % 2 == 0, stop=False, skip_group_check=True)
            for s in range(DB):
                pe.wait_ge(st_load[s % 3], 16 * (s // 3 + 1))
                for hd in range(H):
                    ins = mm(ps[0:ND, UB + hd // 2, (hd % 2) * DV:(hd % 2 + 1) * DV], qm[:, s, hd, :],
                             s0[s % 3][:, hd, :], start=False, stop=s == DB - 1, skip_group_check=True)
                if s == DB - 1:
                    ins.then_inc(o_full, 1)
                pe.wait_ge(km_ready, s + 1)
                if s:
                    pe.wait_ge(st_ready, s)
                for hd in range(H):
                    ins = mm(ps[:, TB + hd // 2, (hd % 2) * DV:(hd % 2 + 1) * DV], ksm[s % 2][0:ND, hd, :],
                             v[0:ND, NPT, hd * DV:(hd + 1) * DV], start=True, stop=True)
                ins.then_inc(dkv_full, 1)
            for g in range(G_CONV, G_CO):
                pe.wait_ge(lo_ready, g + 1)
                for u in range(2):
                    free(u, N_CONV // 2 + g - G_CONV)
                    feature_unit(g % 2, u, u, X).then_inc(w_used if u else unit_full, 1)
            pe.wait_ge(z_ready, H)
            for g in range(G_CO, G_GA):
                pe.wait_ge(lo_ready, g + 1)
                for c in range(4):
                    free(c % 2, N_CO // 2 + 2 * (g - G_CO) + c // 2)
                    feature_unit(g % 2, c % 2, c, Z, kt=H).then_inc(w_used if c == 3 else unit_full, 1)
                if g == G_CO:
                    pe.wait_ge(cs_ready, 1)
                    pe.wait_ge(st_ready, DB)
                    for ct in range(H):
                        ins = pe.transpose(ps[0:2 + 2 * DB, TB, ct * P:(ct + 1) * P], cs[:, ct, :], ident[:, :])
                    ins.then_inc(cs_full, 1)
            for g0, n0 in ((G_GA, N_GA), (G_GB, N_GB)):
                with pe.Fori(0, 2) as i:
                    for p in range(2):
                        pe.wait_ge(lo_ready, i * 2 + (g0 + p + 1))
                        for u in range(2):
                            free(u, i * 2 + (n0 // 2 + p))
                            feature_unit(p, u, u, X).then_inc(w_used if u else unit_full, 1)
            pe.wait_ge(on_ready, NPT + 2)
            pe.wait_ge(cso_ready, 1)
            for j in range(NT):
                n = ND if j == NPT else P
                if j >= 2:
                    pe.wait_ge(og_mul, 2 * (j - 1))
                for k in range(KD):
                    c0 = (k % 4) * P
                    ins = pe.transpose(ps[:, TB + 2 * (j % 2) + k // 4, c0:c0 + n], v[0:n, j, k * P:(k + 1) * P],
                                       ident[0:n, 0:n])
                ins.then_inc(og_full, 1)
            pe.wait_ge(og_ready, 2 * NT)
            with pe.Fori(0, 2) as i:
                for p in range(2):
                    pe.wait_ge(lo_ready, i * 2 + (G_GO + p + 1))
                    for u in range(2):
                        free(u, i * 2 + (N_GO // 2 + p))
                        feature_unit(p, u, u, X).then_inc(w_used if u else unit_full, 1)
            pe.wait_ge(m_ready, 2 * (G_WO - G_GO))
            for g in range(G_WO, G_END):
                pe.wait_ge(lo_ready, g + 1)
                for t in range(NT):
                    n = N_WO + NT * (g - G_WO) + t
                    free(n % 2, n // 2)
                    token_unit(g % 2, n % 2, t, M).then_inc(w_used if t == NT - 1 else unit_full, 1)
            for u in range(2):
                free(u, N_END // 2)

            for i in range(NT + 1):
                if i < NT:
                    pe.wait_ge(x2_ready, i + 1)
                    if i >= 2:
                        pe.wait_ge(xr_ready, i - 1)
                    for k in range(KD):
                        ins = pe.transpose(ps[:, TB + 2 * (i % 2) + k // 4, (k % 4) * P:(k % 4 + 1) * P],
                                           x2[i % 2][:, k * P:(k + 1) * P], ident[:, :])
                    ins.then_inc(x2t_full, 1)
                if i >= 1:
                    pe.wait_ge(xr_ready, i)
                    if i >= 3:
                        pe.wait_ge(lg_ready, i - 2)
                    for k in range(KD):
                        ins = mm(ps[:, (i - 1) % 2, 0:NR], xr[(i - 1) % 2][:, k, :], wr[:, k, :], start=k == 0,
                                 stop=k == KD - 1)
                    ins.then_inc(lg_full, 1)
            pe.wait_ge(r_dve, 3)
            for t in range(NT):
                for t1 in range(t + 1):
                    mm(ps[:, UB, t * NE:(t + 1) * NE], (before if t1 == t else ones)[:, :], rt["mk"][:, t1, :],
                       start=t1 == 0, stop=t1 == t)
            for t in range(NT):
                ins = mm(ps[:, UB + 1, 0:NE], ones[:, :], rt["mk"][:, t, :], start=t == 0, stop=t == NT - 1)
            ins.then_inc(r_pos, 1)

            def block_t(e0, i=0):
                p = e0 % 2
                pe.wait_ge(xg_in[p], 16 * i + 16 * (e0 // 2 + 1))
                if e0 >= 2:
                    pe.wait_ge(bl_ready, 2 * i + (e0 - 1))
                carry(TB + 2 * p)
                for k in range(KD):
                    ins = pe.transpose(ps[:, TB + 2 * p, k * B:(k + 1) * B], xg[p][:, k * P:(k + 1) * P],
                                       ident[0:B, 0:B])
                ins.then_inc(bt_full, 1)

            def into_hidden(e0, which, i=0):
                p = e0 % 2
                m = 3 * e0 if which else max(3 * e0 - 1, 0)
                if e0 == 0:
                    m = which
                pe.wait_ge(lo_ready, 6 * i + (G_END + m + 1))
                pe.wait_ge(bl_ready, 2 * i + (e0 + 1))
                if e0:
                    pe.wait_ge(hm_ready if which else si_ready, 2 * i + e0)
                g, w = (gh[p], gl[p]), (tiles(wh[m % 3], KD), tiles(wl[m % 3], KD))
                three([ps[:, which, 0:DE]], KD, lambda a, k: g[a][:, k, :],
                      lambda b, k, o: w[b][:, k, :]).then_inc(w_used, 1)

            def hidden_t(e0, i=0):
                p = e0 % 2
                pe.wait_ge(hm_ready, 2 * i + (e0 + 1))
                if e0 >= 2:
                    pe.wait_ge(hl_ready, 2 * i + (e0 - 1))
                carry(TB + 1 + 2 * p)
                for c in range(DE // P):
                    ins = pe.transpose(ps[:, TB + 1 + 2 * p, c * B:(c + 1) * B], hm[p][:, c * P:(c + 1) * P],
                                       ident[0:B, 0:B])
                ins.then_inc(ht_full, 1)

            def down(e0, i=0):
                p = e0 % 2
                m = 3 * e0 + 4 if e0 < NE - 1 else 3 * NE - 1
                pe.wait_ge(lo_ready, 6 * i + (G_END + m + 1))
                pe.wait_ge(hl_ready, 2 * i + (e0 + 1))
                if e0:
                    pe.wait_ge(yb_ready, 2 * i + e0)
                g, w = (hh[p], hl[p]), (tiles(wh[m % 3], DE // P), tiles(wl[m % 3], DE // P))
                three([ps[:, 2, :], ps[:, 3, :]], DE // P, lambda a, k: g[a][:, k, :],
                      lambda b, k, o: w[b][:, k, o * 512:(o + 1) * 512]).then_inc(w_used, 1)

            pe.wait_ge(lg_ready, NT)
            block_t(0)
            into_hidden(0, 0)
            block_t(1)
            into_hidden(0, 1)
            hidden_t(0)
            into_hidden(1, 0)
            block_t(2)
            into_hidden(1, 1)
            down(0)
            hidden_t(1)

            def step(e0, i=0):
                into_hidden(e0, 0, i)
                block_t(e0 + 1, i)
                into_hidden(e0, 1, i)
                down(e0 - 1, i)
                hidden_t(e0, i)

            with pe.Fori(0, (NE - 4) // 2) as i:
                step(2, i)
                step(3, i)
            step(NE - 2)
            step(NE - 1)
            down(NE - 1)
            pe.wait_ge(xinfo_ready, 1)
            nx = pe.value_load(xinfo[0:1, XB:XB + 1], min_val=0, max_val=XB)
            pe.wait_ge(yb_ready, NE)
            with pe.Fori(0, XB) as j:
                with pe.If(nx > j):
                    pe.wait_ge(e_xg, j * 16 + 16)
                    carry(TB)
                    for k in range(KD):
                        ins = pe.transpose(ps[:, TB, k * B:(k + 1) * B], xg[0][:, k * P:(k + 1) * P], ident[0:B, 0:B])
                    ins.then_inc(e_xt, 1)
                    pe.wait_ge(e_bl, j + 1)
                    pe.wait_ge(e_lo, j * 3 + 3)
                    for s in range(2):
                        g, w = (gh[0], gl[0]), (tiles(wh[s], KD), tiles(wl[s], KD))
                        ins = three([ps[:, s, 0:DE]], KD, lambda a, k: g[a][:, k, :], lambda b, k, o: w[b][:, k, :])
                    ins.then_inc(e_gu, 1)
                    pe.wait_ge(e_hm, j + 1)
                    carry(TB + 1)
                    for c in range(DE // P):
                        ins = pe.transpose(ps[:, TB + 1, c * B:(c + 1) * B], hm[0][:, c * P:(c + 1) * P],
                                           ident[0:B, 0:B])
                    ins.then_inc(e_ht, 1)
                    pe.wait_ge(e_hl, j + 1)
                    g, w = (hh[0], hl[0]), (tiles(wh[2], DE // P), tiles(wl[2], DE // P))
                    three([ps[:, 2, :], ps[:, 3, :]], DE // P, lambda a, k: g[a][:, k, :],
                          lambda b, k, o: w[b][:, k, o * 512:(o + 1) * 512]).then_inc(e_y, 1)


_INS = ("x_prompt", "x_sample", "state_conv", "state_gla", "norm_mix", "w_in", "w_conv", "w_alpha_up", "b_alpha",
        "gla_norm", "w_conv_out", "w_gla_out", "w_o", "norm_ffn", "w_group_router", "b_group_router",
        "w_expert_router", "b_expert_router", "w_gate", "w_up", "w_down", "norm_final")
_OUTS = ((1, SEQ, D), (DB, DS, D), (1, 1, 2, DC), (1, 1, H, DK, DV), (1, DB, 2, DC), (1, DB, H, DK, DV))


def kernel(**inputs):
    import numpy as _np
    import concourse.bacc as _bacc
    from concourse.bass_utils import run_bass_kernel_spmd as _run

    nc = _bacc.Bacc("TRN2", target_bir_lowering=False, num_devices=1)
    arrays, args = {}, []
    for name in _INS:
        a = _np.ascontiguousarray(inputs[name])
        arrays[name] = a
        args.append(nc.dram_tensor(name, a.shape, F32, kind="ExternalInput").ap())
    outs = ("y_prompt", "y_sample", "conv_prompt_new", "gla_prompt_new", "conv_sample_new", "gla_sample_new")
    for name, shape in zip(outs, _OUTS):
        args.append(nc.dram_tensor(name, shape, F32, kind="ExternalOutput").ap())
    build(nc, *args)
    r = _run(nc, [arrays], core_ids=[0])
    return tuple(r.results[0][name] for name in outs)
```

```python
from contextlib import ExitStack

import concourse.bass as bass
from concourse import mybir

F32 = mybir.dt.float32
F32R = mybir.dt.float32r
I32 = mybir.dt.int32
U32 = mybir.dt.uint32
ALU = mybir.AluOpType
ACT = mybir.ActivationFunctionType
AX = mybir.AxisListType

P = 128
D = 1024
KD = D // P
SEQ = 512
DB, DS = 8, 8
ND = DB * DS
T = SEQ + ND
NT = (T + P - 1) // P
TP = NT * P
NPT = SEQ // P
HALF = T // 2
DC = D // 2
H = 4
DK = DC // H
DV = D // H
RANK = 16
CH = 32
NCH = P // CH
NG, NEG = 4, 8
NE = NG * NEG
NR = NG + NE
DE = 256
EPS = 1e-6
GATE_NORM = 16.0
QSCALE = DK ** -0.5
GW = 2048
C_CB, C_CC, C_CH, C_Q, C_K, C_V, C_G = 0, 512, 1024, 1536, 2048, 2560, 3584
C_A = 4608
C_GA = C_A + RANK
C_GB = C_GA + D
B = 64
XB = 2 * T // (B + 1)
NBLK = NE + XB
NSMALL = 11
FAR = 1 << 20
G_QK, G_V, G_G, G_CONV, G_GA, G_GB, G_CO, G_GO, G_WO, G_END = 0, 4, 8, 12, 18, 22, 26, 28, 32, 36
N_QK, N_V, N_G, N_CONV, N_GA, N_GB, N_CO, N_GO, N_WO, N_END = 2, 10, 30, 38, 50, 58, 66, 74, 82, 102
U_QK, U_V, U_G, U_CONV, U_GA, U_GB, U_CO, U_GO, U_WO = 0, 4, 20, 24, 30, 34, 38, 44, 48


class Chain:

    def __init__(self, eng, sem):
        self.eng, self.sem, self.n, self.off = eng, sem, 0, 0

    def __call__(self, ins):
        ins.then_inc(self.sem, 1)
        self.n += 1

    def sync(self):
        self.eng.wait_ge(self.sem, self.off + self.n)

    def enter(self, i, per):
        self.n0, self.per, self.off = self.n, per, i * per

    def leave(self, times):
        assert self.n - self.n0 == self.per, (self.n - self.n0, self.per)
        self.n, self.off = self.n0 + self.per * times, 0


def build(nc, x_prompt, x_sample, state_conv, state_gla, norm_mix, w_in, w_conv, w_alpha_up, b_alpha, gla_norm,
          w_conv_out, w_gla_out, w_o, norm_ffn, w_group_router, b_group_router, w_expert_router, b_expert_router,
          w_gate, w_up, w_down, norm_final,
          y_prompt, y_sample, conv_prompt_new, gla_prompt_new, conv_sample_new, gla_sample_new):
    rows_d = nc.dram_tensor("moe_rows", (T, D), F32).ap()
    table_d = nc.dram_tensor("slot_table", (B * NBLK, 1), I32).ap()
    res_d = nc.dram_tensor("moe_results", (2 * T, D), F32).ap()
    xp = x_prompt.rearrange("b (n p) d -> p (b n) d", p=P)
    xs = x_sample.rearrange("b t d -> (b t) d")
    win = w_in[0].rearrange("(k p) c -> p k c", p=P)
    wco = w_conv_out[0].rearrange("(k p) c -> p k c", p=P)
    wgo = w_gla_out[0].rearrange("(k p) c -> p k c", p=P)
    woo = w_o[0].rearrange("(k p) c -> p k c", p=P)
    st_in = state_gla[0].rearrange("s h d v -> s d h v")
    st_out = gla_sample_new[0].rearrange("s h d v -> s d h v")

    ctx = ExitStack()
    with ctx:
        place = [(nc.sbuf_base + 31) // 32 * 32]

        def sb(name, shape, dt=F32, at=None):
            n = 4
            for s in shape[1:]:
                n *= s
            if at is not None:
                place[0] = at
            t = nc.alloc_sbuf_tensor_at(name, shape, dt, offset=place[0])
            place[0] += (n + 31) // 32 * 32
            assert place[0] <= nc.sbuf_usable_end, (name, place[0] - nc.sbuf_usable_end)
            return t

        ident = sb("ident", [P, P])
        ones = sb("ones", [P, P])
        before = sb("before", [P, P])
        causal = sb("causal", [P, P], I32)
        causal8 = sb("causal8", [ND, ND], I32)
        inseq = sb("inseq", [ND, DB])
        ss = sb("ss", [P, 32])
        ms = sb("ms", [P, 32])
        rs = sb("rs", [P, 32])
        expo = sb("expo", [P, H])
        balpha = sb("balpha", [P, H])
        gn = sb("gn", [P, DV // P])
        gnh = sb("gnh", [P, DV // P + 1])
        wtap = sb("wtap", [P, 3, H])
        hist = sb("hist", [P, H, DB * 2])
        wr = sb("wr", [P, KD, NR])
        rb = sb("rb", [P, NR])
        xinfo = sb("xinfo", [1, XB + 1], I32)
        slotd = sb("slotd", [B, NBLK], I32)
        slots = sb("slots", [B, NBLK], I32)
        curs = [sb(f"curs{i}", [B, 1], I32) for i in range(2)]
        curd = [sb(f"curd{i}", [B, 1], I32) for i in range(2)]
        lg = sb("lg", [P, NT, NR])
        wts = sb("wts", [P, 2, NT])
        dlast = [sb(f"dlast{i}", [P, H]) for i in range(2)]
        mark = sb("mark", [P, 64])
        raw = [sb(f"raw{i}", [P, GW]) for i in range(2)]
        wh = [sb(f"wh{i}", [P, GW], F32R) for i in range(2)]
        wl = [sb(f"wl{i}", [P, GW], F32R) for i in range(2)]
        zone_a = place[0]
        raw += [sb(f"raw{i}", [P, GW]) for i in range(2, 6)]
        wh.append(sb("wh2", [P, GW], F32R))
        wl.append(sb("wl2", [P, GW], F32R))
        zone_b = place[0]
        xh = sb("xh", [P, KD, TP], F32R)
        xl = sb("xl", [P, KD, TP], F32R)
        zone_v = place[0]
        v = sb("v", [P, NT, D])
        zone_s = place[0]
        sg = sb("sg", [P, KD, T])
        zone_q = place[0]
        qk = sb("qk", [P, 2 * H, T])
        zone_z = place[0]
        xin = sb("xin", [P, NT, D], at=zone_v)
        la = sb("la", [P, NT, H, P], at=zone_a)
        s1 = place[0]
        nmb = sb("nmb", [P, D])
        xn = [sb(f"xn{i}", [P, D]) for i in range(2)]
        junk1 = sb("junk1", [P, D])
        rawa = sb("rawa", [P, KD, P])
        ah = sb("ah", [P, KD, P], F32R)
        al = sb("al", [P, KD, P], F32R)
        assert place[0] <= zone_b
        aT = sb("aT", [RANK, T], at=zone_z)
        wau = sb("wau", [RANK, H * DK])
        sct = sb("sct", [DB * 2, DC])
        causal_f = sb("causal_f", [P, P])
        causal8_f = sb("causal8_f", [ND, ND])
        far = sb("far", [B, NBLK], I32)
        abt = [sb(f"abt{i}", [P, T], at=None if i else zone_s) for i in range(2)]
        mnt = sb("mnt", [P, T])
        m_tile = sb("m_tile", [P, H, P], at=s1)
        m_ch = sb("m_ch", [P, H, P])
        m_seq = sb("m_seq", [P, H, P])
        bt = sb("bt", [P, H, P])
        bc = sb("bc", [P, H, P])
        eb = sb("eb", [P, H, P])
        ec = sb("ec", [P, H, P])
        qg0 = sb("qg0", [P, H, P])
        ql = sb("ql", [P, H, P])
        kst = sb("kst", [P, H, P])
        kt = sb("kt", [P, H, P])
        sc = sb("sc", [P, H, P])
        NKI = CH * NCH * (NCH + 1) // 2
        dif_at = place[0]
        dif = sb("dif", [P, H, NKI])
        S = sb("S", [P, H, DV], at=zone_z)
        ta = sb("ta", [P, T])
        tb = sb("tb", [P, T], at=dif_at + 4 * DB * H * ND)
        qg = [qg0, sb("qg1", [P, H, P])]
        kiv = sb("kiv", [P, H, NKI], at=dif_at)
        qm = sb("qm", [P, DB, H, ND], at=dif_at)
        assert place[0] <= zone_b - 4 * H * DV
        s0 = [sb("s0a", [P, H, DV], at=zone_b - 4 * H * DV), sb("s0b", [P, H, DV], at=zone_z + 4 * H * DV), S]
        ksm = [bc, ec]
        zh = sb("zh", [P, H, T], F32R, at=zone_q)
        zl = sb("zl", [P, H, T], F32R)
        m1 = sb("m1", [P, KD, T], at=zone_a)
        sgb = sb("sgb", [P, KD, T])
        up = sb("up", [P, H, SEQ + 2])
        assert place[0] <= zone_b
        ud = sb("ud", [P, H, DB, DS + 2])
        cs = sb("cs", [P, H, 2 + 2 * DB])
        assert place[0] <= zone_b
        h = sb("h", [P, NT, D], at=zone_v + 2 * 4 * KD * TP)
        tmp = [sb(f"tmp{i}", [P, T]) for i in range(2)]
        cso = sb("cso", [2 + 2 * DB, DC], at=zone_a + 2 * 4 * KD * T)
        mh = sb("mh", [P, KD, TP], F32R, at=zone_v)
        ml = sb("ml", [P, KD, TP], F32R)
        assert place[0] <= zone_v + 2 * 4 * KD * TP
        nfb = sb("nfb", [P, D], at=zone_b)
        nlb = sb("nlb", [P, D])
        x2 = [sb(f"x2{i}", [P, D]) for i in range(2)]
        junk = sb("junk", [P, D])
        xr = [sb(f"xr{i}", [P, KD, P]) for i in range(2)]
        io = sb("io", [P, NT, NE])
        ig = sb("ig", [P, NT, NG])
        valid = sb("valid", [P, NT])
        vals = sb("vals", [P, 2, NT], I32)
        oneb = sb("oneb", [P, NE])
        iox = sb("iox", [1, XB, NE])
        assert place[0] <= zone_v
        xg = [sb(f"xg{i}", [B, D]) for i in range(2)]
        gh = [sb(f"gh{i}", [P, KD, P], F32R) for i in range(2)]
        gl = [sb(f"gl{i}", [P, KD, P], F32R) for i in range(2)]
        yb = [sb(f"yb{i}", [B, D]) for i in range(2)]
        hh = [sb(f"hh{i}", [P, DE // P, P], F32R) for i in range(2)]
        hl = [sb(f"hl{i}", [P, DE // P, P], F32R) for i in range(2)]
        si = [sb(f"si{i}", [B, DE]) for i in range(2)]
        hm = [sb(f"hm{i}", [B, DE]) for i in range(2)]
        rt = {}
        for n, w in (("em", NE), ("c1", NE), ("e1", NE), ("e2", NE), ("mk", NE), ("pr", NE),
                     ("gd", NG), ("gx", NG), ("gc", NG), ("go", NG)):
            rt[n] = sb("r_" + n, [P, NT, w])
        for n in ("gmax", "gsum", "gtop", "gi", "m1v", "i1", "m2v", "i2", "dd", "ex"):
            rt[n] = sb("r_" + n, [P, NT])
        for n in ("pk", "bk", "ek", "q", "is0", "pf", "t1", "t2"):
            rt[n] = sb("r_" + n, [P, 2, NT])
        for n in ("pi", "qi", "sl"):
            rt[n] = sb("r_" + n, [P, 2, NT], I32)
        for n in ("cnt", "nb", "xe", "ci", "base"):
            rt[n] = sb("r_" + n, [P, NE])
        cnt_i = sb("cnt_i", [P, NE], I32)
        gex = sb("gex", [1, XB, NE])
        xf = sb("xf", [1, XB + 1])
        assert place[0] <= zone_v + 2 * 4 * KD * TP
        y2 = [sb(f"y2{i}", [P, 2, D], at=None if i else zone_a) for i in range(NT)]
        yo = [sb(f"yo{i}", [P, D]) for i in range(2)]
        assert place[0] <= zone_b

        ps = ctx.enter_context(nc.psum_tensor("ps", [P, 8, 512], F32))
        pair = [ps[:, 0:2, :], ps[:, 2:4, :]]
        TB, UB = 4, 6

        def sem(name):
            return ctx.enter_context(nc.semaphore(name))

        raw_in = [sem(f"raw_in{i}") for i in range(6)]
        x_in = [sem(f"x_in{i}") for i in range(NT)]
        nm_in, small_in, a_in, h_in, nf_in = (sem(n) for n in ("nm_in", "small_in", "a_in", "h_in", "nf_in"))
        pool_const, dve_const = sem("pool_const"), sem("dve_const")
        hi_ready, lo_ready, w_used = sem("hi_ready"), sem("lo_ready"), sem("w_used")
        unit_full = sem("unit_full")
        unit_free = [sem(f"unit_free{i}") for i in range(2)]
        sq_done, rs_ready = sem("sq_done"), sem("rs_ready")
        xn_ready, xt_full, xh_ready, xt_free = (sem(n) for n in ("xn_ready", "xt_full", "xh_ready", "xt_free"))
        ah_ready, al_ready, aT_ready = sem("ah_ready"), sem("al_ready"), sem("aT_ready")
        ls_act, la_ready = sem("ls_act"), sem("la_ready")
        r_const = sem("r_const")
        a_full, alpha_full, hist_full, hist_ready = (sem(n) for n in ("a_full", "alpha_full", "hist_full", "hist_ready"))
        scans_done, ebec_done, diffs_done, exps_done = (
            sem(n) for n in ("scans_done", "ebec_done", "diffs_done", "exps_done"))
        gla_in, p1_full, kt_ready, sc_ready, o_full, kv_full, on_ready, s_ready = (
            sem(n) for n in ("gla_in", "p1_full", "kt_ready", "sc_ready", "o_full", "kv_full", "on_ready", "s_ready"))
        g_act, sg_ready = sem("g_act"), sem("sg_ready")
        st_load = [sem(f"st_load{i}") for i in range(3)]
        st_store, km_ready, dkv_full, st_ready = (sem(n) for n in ("st_store", "km_ready", "dkv_full", "st_ready"))
        cc_ready, z_mul, z_hi, z_ready, cs_ready, cs_full, cso_ready = (
            sem(n) for n in ("cc_ready", "z_mul", "z_hi", "z_ready", "cs_ready", "cs_full", "cso_ready"))
        ya_ready, sig_ready, m1_ready, sgb_ready = (sem(n) for n in ("ya_ready", "sig_ready", "m1_ready", "sgb_ready"))
        og_full, og_mul, og_hi, og_ready = (sem(n) for n in ("og_full", "og_mul", "og_hi", "og_ready"))
        m_mul, m_hi, m_ready, h_ready = (sem(n) for n in ("m_mul", "m_hi", "m_ready", "h_ready"))
        x2_out = [sem(f"x2_out{i}") for i in range(2)]
        x2_ready, x2t_full, xr_ready, lg_full, lg_ready = (
            sem(n) for n in ("x2_ready", "x2t_full", "xr_ready", "lg_full", "lg_ready"))
        r_dve, r_act, r_pos, slot_ready, tab_init, tab_done, tab_load, idx_ready, moe_zero, xinfo_ready = (
            sem(n) for n in ("r_dve", "r_act", "r_pos", "slot_ready", "tab_init", "tab_done", "tab_load", "idx_ready",
                             "moe_zero", "xinfo_ready"))
        xg_in = [sem(f"xg_in{i}") for i in range(2)]
        y_out = [sem(f"y_out{i}") for i in range(2)]
        e_cur = sem("e_cur")
        bt_full, bh_ready, bl_ready, g_full, u_full, si_ready, hm_ready, ht_full, hh_ready, hl_ready, y_full, yb_ready = (
            sem(n) for n in ("bt_full", "bh_ready", "bl_ready", "g_full", "u_full", "si_ready", "hm_ready", "ht_full",
                             "hh_ready", "hl_ready", "y_full", "yb_ready"))
        e_raw, e_hi, e_lo, e_xg, e_xt, e_bh, e_bl, e_gu, e_si, e_hm, e_ht, e_hh, e_hl, e_y, e_yb, e_out = (
            sem("e_" + n) for n in ("raw", "hi", "lo", "xg", "xt", "bh", "bl", "gu", "si", "hm", "ht", "hh", "hl",
                                    "y", "yb", "out"))
        moe_done = sem("moe_done")
        y2_in = [sem(f"y2_in{i}") for i in range(NT)]
        hf_ready, yo_ready = sem("hf_ready"), sem("yo_ready")
        yo_out = [sem(f"yo_out{i}") for i in range(2)]
        out_done = sem("out_done")
        c_act, c_dve, c_pool = sem("c_act"), sem("c_dve"), sem("c_pool")

        def raw_count(m):
            return m // 6 + 1 + (G_END // 2 if (m + 2) % 6 < 2 else 0)

        block = ctx.enter_context(nc.Block())

        def unit_free_count(n_even, step, c):
            return n_even // 2 + step + c // 2

        def wait_unit(eng, g, k, c, ncol, base):
            if c == ncol - 1:
                eng.wait_ge(w_used, g + 1)
            else:
                eng.wait_ge(unit_full, base + k * (ncol - 1) + c + 1)

        def store(sp, i):
            sp.wait_ge(yo_ready, i + 1)
            dst = y_sample.rearrange("b t d -> (b t) d") if i == NPT else y_prompt[0, i * P:(i + 1) * P, :]
            sp.dma_start(dst, yo[i % 2][0:ND if i == NPT else P, :]).then_inc(yo_out[i % 2], 16)

        @block.sync
        def _(sp):
            for i in range(NPT):
                sp.dma_start(xin[:, i, :], xp[:, i, :]).then_inc(x_in[i], 16)
                if i == 0:
                    sp.dma_start(nmb[:, :], norm_mix.to_broadcast((P, D))).then_inc(nm_in, 16)
            sp.wait_ge(dve_const, 1)
            sp.dma_start(xin[0:ND, NPT, :], xs).then_inc(x_in[NPT], 16)
            sp.dma_start(rawa[:, :, :], win[:, :, C_A:C_A + P]).then_inc(a_in, 16)
            sp.dma_start(wau[:, :], w_alpha_up[0]).then_inc(small_in, 16)
            sp.dma_start(balpha[:, :], b_alpha[0].rearrange("(h p) -> p h", p=P),
                         allow_slow_non_contiguous=True).then_inc(small_in, 16)
            sp.dma_start(sct[:, :], state_conv[0].rearrange("s w c -> (s w) c")).then_inc(small_in, 16)
            sp.dma_start(gn[:, :], gla_norm[0].rearrange("(c p) -> p c", p=P),
                         allow_slow_non_contiguous=True).then_inc(small_in, 16)
            for w in range(3):
                sp.dma_start(wtap[:, w, :], w_conv[0, w].rearrange("(c p) -> p c", p=P),
                         allow_slow_non_contiguous=True).then_inc(small_in, 16)
            sp.dma_start(wr[:, :, 0:NG], w_group_router[0].rearrange("(k p) e -> p k e", p=P)).then_inc(small_in, 16)
            sp.dma_start(wr[:, :, NG:NR], w_expert_router[0].rearrange("(k p) e -> p k e", p=P)).then_inc(small_in, 16)
            sp.dma_start(rb[:, 0:NG], b_group_router.to_broadcast((P, NG))).then_inc(small_in, 16)
            sp.dma_start(rb[:, NG:NR], b_expert_router.to_broadcast((P, NE))).then_inc(small_in, 16)

            def load(par, src, kt=KD):
                sp.dma_start(raw[par][:, :].rearrange("p (k c) -> p k c", k=kt), src).then_inc(raw_in[par], 16)

            for g in range(2):
                load(g, win[:, :, C_Q + g * 256:C_Q + (g + 1) * 256])
            with sp.Fori(0, (G_CONV - 2) // 2) as i:
                for p in range(2):
                    sp.wait_ge(lo_ready, 2 * i + p + 1)
                    load(p, win[:, :, bass.ds(i * 512 + (C_Q + 512 + p * 256), 256)])
            conv = [c + t * 256 for t in range(2) for c in (C_CC, C_CH, C_CB)]
            for g in range(G_CONV, G_CONV + 2):
                sp.wait_ge(lo_ready, g - 1)
                load(g % 2, win[:, :, conv[g - G_CONV]:conv[g - G_CONV] + 256])
            sp.wait_ge(s_ready, NPT + 1)
            sp.dma_start(gla_prompt_new[0, 0].rearrange("h d v -> d h v"), S[:, :, :]).then_inc(out_done, 16)
            for s in range(2):
                if s == 0:
                    sp.wait_ge(tab_init, 16)
                    sp.wait_ge(sg_ready, 2 * NPT + 1)
                sp.dma_start(s0[s][:, :, :], st_in[s]).then_inc(st_load[s], 16)
            sp.wait_ge(out_done, 16)
            sp.dma_start(s0[2][:, :, :], st_in[2]).then_inc(st_load[2], 16)
            for s in range(DB):
                sp.wait_ge(st_ready, s + 1)
                sp.dma_start(st_out[s], s0[s % 3][:, :, :]).then_inc(st_store, 16)
                if s + 3 < DB:
                    sp.wait_ge(st_store, 16 * (s + 1))
                    sp.dma_start(s0[s % 3][:, :, :], st_in[s + 3]).then_inc(st_load[s % 3], 16)
            for g in range(G_CONV + 2, G_GA):
                sp.wait_ge(lo_ready, g - 1)
                load(g % 2, win[:, :, conv[g - G_CONV]:conv[g - G_CONV] + 256])
            with sp.Fori(0, (G_CO - G_GA) // 2) as i:
                for p in range(2):
                    sp.wait_ge(lo_ready, 2 * i + (G_GA + p - 1))
                    load(p, win[:, :, bass.ds(i * 512 + (C_GA + p * 256), 256)])
            sp.wait_ge(cso_ready, 1)
            sp.dma_start(conv_prompt_new[0, 0], cso[0:2, :]).then_inc(out_done, 16)
            sp.dma_start(conv_sample_new[0].rearrange("s w c -> (s w) c"), cso[2:2 + 2 * DB, :]).then_inc(out_done, 16)
            for g in range(G_CO, G_GO):
                sp.wait_ge(lo_ready, g - 1)
                load(g % 2, wco[:, :, (g - G_CO) * 512:(g - G_CO + 1) * 512], kt=H)
            with sp.Fori(0, 2) as i:
                for p in range(2):
                    sp.wait_ge(lo_ready, 2 * i + (G_GO + p - 1))
                    load(p, wgo[:, :, bass.ds(i * 512 + p * 256, 256)])
            sp.wait_ge(dve_const, 2)
            sp.dma_start(h[:, 0:NPT, :], xp).then_inc(h_in, 16)
            sp.dma_start(h[0:ND, NPT, :], xs).then_inc(h_in, 16)
            for g in range(G_WO, G_WO + 2):
                sp.wait_ge(lo_ready, g - 1)
                load(g % 2, woo[:, :, (g - G_WO) * 256:(g - G_WO + 1) * 256])
            sp.wait_ge(w_used, G_WO)
            sp.dma_start(nfb[:, :], norm_ffn.to_broadcast((P, D))).then_inc(nf_in, 16)
            sp.dma_start(nlb[:, :], norm_final.rearrange("(a d) -> a d", a=1).to_broadcast((P, D))).then_inc(nf_in, 16)
            for g in range(G_WO + 2, G_END):
                sp.wait_ge(lo_ready, g - 1)
                load(g % 2, woo[:, :, (g - G_WO) * 256:(g - G_WO + 1) * 256])

            def expert(m_slot, which, e):
                dst = raw[(m_slot + 2) % 6]
                if which == "down":
                    src = w_down[0, e].rearrange("(k p) d -> p k d", p=P)
                else:
                    src = (w_gate if which == "gate" else w_up)[0, e].rearrange("(k p) c -> p k c", p=P)
                return dst[:, :].rearrange("p (k c) -> p k c", k=DE // P if which == "down" else KD), src

            sp.wait_ge(m_ready, 2 * (G_WO - G_GO))
            for m, (which, e) in enumerate((("gate", 0), ("up", 0), ("gate", 1), ("up", 1), ("down", 0))):
                if m >= 4:
                    sp.wait_ge(lo_ready, G_END + m - 5)
                dst, src = expert(m, which, e)
                sp.dma_start(dst, src).then_inc(raw_in[(m + 2) % 6], 16)
            with sp.Fori(0, (NE - 2) // 2) as i:
                for r in range(6):
                    q = r // 3
                    which = ("gate", "up", "down")[r % 3]
                    e = i * 2 + (2 + q - (which == "down"))
                    sp.wait_ge(lo_ready, 6 * i + (G_END + 5 + r - 5))
                    dst = raw[(5 + r + 2) % 6]
                    if which == "down":
                        src = w_down[0, bass.ds(e, 1)].rearrange("e (k p) d -> p (e k) d", p=P)
                    else:
                        src = (w_gate if which == "gate" else w_up)[0, bass.ds(e, 1)].rearrange(
                            "e (k p) c -> p (e k) c", p=P)
                    sp.dma_start(dst[:, :].rearrange("p (k c) -> p k c", k=DE // P if which == "down" else KD),
                                 src).then_inc(raw_in[(5 + r + 2) % 6], 16)
            m = 3 * NE - 1
            sp.wait_ge(lo_ready, G_END + m - 5)
            dst, src = expert(m, "down", NE - 1)
            sp.dma_start(dst, src).then_inc(raw_in[(m + 2) % 6], 16)
            sp.wait_ge(xinfo_ready, 1)
            nx = sp.value_load(xinfo[0:1, XB:XB + 1], min_val=0, max_val=XB)
            sp.wait_ge(lo_ready, G_END + 3 * NE)
            with sp.Fori(0, XB) as j:
                with sp.If(nx > j):
                    sp.wait_ge(e_yb, j + 1)
                    e = sp.value_load(xinfo[0:1, bass.ds(j, 1)], min_val=0, max_val=NE - 1)
                    for s, w in enumerate((w_gate, w_up, w_down)):
                        kt = DE // P if s == 2 else KD
                        sp.dma_start(raw[s][:, :].rearrange("p (k c) -> p k c", k=kt),
                                     w[0, bass.ds(e, 1)].rearrange("e (k p) c -> p (e k) c", p=P)).then_inc(e_raw, 16)
            sp.wait_ge(moe_done, 1)
            for i in range(NT):
                n = ND if i == NPT else P
                sp.dma_start(y2[i][0:n, :, :], res_d[2 * i * P:2 * (i * P + n), :].rearrange(
                    "(p k) d -> p k d", k=2)).then_inc(y2_in[i], 16)
            for i in range(NT):
                store(sp, i)
            sp.wait_ge(yo_out[0], 16 * ((NT + 1) // 2))
            sp.wait_ge(yo_out[1], 16 * (NT // 2))
            sp.wait_ge(out_done, 16 * 3)
            sp.wait_ge(st_store, 16 * DB)

        @block.gpsimd
        def _(pool):
            c = Chain(pool, c_pool)
            c(pool.memset(ident[:, :], 0.0))
            c(pool.memset(ones[:, :], 1.0))
            c(pool.memset(expo[:, :], -0.5))
            c.sync()
            c(pool.affine_select(out=ident[:, :], in_=ident[:, :], compare_op=ALU.not_equal, fill=1.0, base=0,
                                 pattern=[[-1, P]], channel_multiplier=1))
            c(pool.affine_select(out=before[:, :], in_=ones[:, :], compare_op=ALU.is_gt, fill=0.0, base=0,
                                 pattern=[[1, P]], channel_multiplier=-1))
            c(pool.affine_select(out=causal_f[:, :], in_=ones[:, :], compare_op=ALU.is_ge, fill=0.0, base=0,
                                 pattern=[[1, P]], channel_multiplier=-1))
            c(pool.affine_select(out=inseq[:, :], in_=ones[0:ND, 0:DB], compare_op=ALU.is_ge, fill=0.0, base=0,
                                 pattern=[[-DS, DB]], channel_multiplier=1))
            c.sync()
            c(pool.affine_select(out=inseq[:, :], in_=inseq[:, :], compare_op=ALU.is_ge, fill=0.0, base=DS - 1,
                                 pattern=[[DS, DB]], channel_multiplier=-1))
            c(pool.affine_select(out=causal8_f[:, :], in_=causal_f[0:ND, 0:ND], compare_op=ALU.is_ge, fill=0.0,
                                 base=0, pattern=[[-DS, DB], [0, DS]], channel_multiplier=1))
            c.sync()
            pool.memset(far[:, :], FAR).then_inc(pool_const, 1)
            pool.wait_ge(pool_const, 1)
            pool.dma_start(table_d.rearrange("(p b) a -> p (b a)", b=NBLK), far[:, :]).then_inc(tab_init, 16)

            def carry():
                return pool.tensor_tensor(ms[:, 29:30], expo[:, 0:1], expo[:, 0:1], ALU.add)

            def rms(n, lo, hi, size, rows=P):
                pool.wait_ge(sq_done, n + 1)
                c(pool.tensor_scalar(ms[0:rows, lo:hi], ss[0:rows, lo:hi], 1.0 / size, EPS, ALU.mult, ALU.add))
                c.sync()
                pool.tensor_tensor(rs[0:rows, lo:hi], ms[0:rows, lo:hi], expo[0:rows, 0:hi - lo], ALU.pow).then_inc(rs_ready, 1)

            for i in range(NT):
                rms(i, i, i + 1, D)
            for j in range(NPT):
                rms(NT + j, 8 + 4 * (j % 2), 12 + 4 * (j % 2), DV)
            pool.wait_ge(kt_ready, NPT + 1)
            for s in range(DB):
                if s >= 2:
                    pool.wait_ge(dkv_full, s - 1)
                pool.tensor_scalar(ksm[s % 2][0:ND, :, :], kt[0:ND, :, :], inseq[:, s:s + 1], None,
                                   ALU.mult).then_inc(km_ready, 1)
            pool.wait_ge(sq_done, NT + NPT + 1)
            c(pool.tensor_scalar(ms[0:ND, 8:12], ss[0:ND, 8:12], 1.0 / DV, EPS, ALU.mult, ALU.add))
            c.sync()
            pool.tensor_tensor(rs[0:ND, 8:12], ms[0:ND, 8:12], expo[0:ND, 0:H], ALU.pow).then_inc(rs_ready, 1)
            pool.wait_ge(w_used, G_WO)
            c(pool.iota(io[:, :, :], pattern=[[0, NT], [1, NE]], base=0, channel_multiplier=0,
                        allow_small_or_imprecise_dtypes=True))
            c(pool.iota(ig[:, :, :], pattern=[[0, NT], [1, NG]], base=0, channel_multiplier=0,
                        allow_small_or_imprecise_dtypes=True))
            for k in range(2):
                c(pool.iota(vals[:, k, :], pattern=[[2 * P, NT]], base=k, channel_multiplier=2))
            c(pool.iota(iox[:, :, :], pattern=[[1, XB], [0, NE]], base=0, channel_multiplier=0,
                        allow_small_or_imprecise_dtypes=True))
            c(pool.memset(valid[:, :], 1.0))
            c(pool.memset(oneb[:, :], 1.0))
            c.sync()
            pool.memset(valid[ND:P, NPT:NT], 0.0).then_inc(r_const, 1)
            pool.wait_ge(r_const, 1)
            for i in range(NT + 2):
                if i < NT:
                    rms(NT + NPT + 1 + i, 16 + i, 17 + i, D)
                if i >= 2:
                    n = ND if i - 2 == NPT else P
                    pool.wait_ge(x2_ready, i - 1)
                    pool.dma_start(rows_d[(i - 2) * P:(i - 2) * P + n, :], x2[i % 2][0:n, :]).then_inc(x2_out[i % 2], 16)
            pool.wait_ge(w_used, G_END)
            for m in range(3):
                pool.wait_ge(hi_ready, G_END + m + 1)
                pool.tensor_tensor(wl[m][:, :], raw[m + 2][:, :], wh[m][:, :].bitcast(F32),
                                   ALU.subtract).then_inc(lo_ready, 1)
            for i in range(2):
                c(pool.memset(xg[i][:, :], 0.0))
                c.sync()
                c(pool.memset(gh[i][:, :, :].bitcast(F32), 0.0))
                c(pool.memset(gl[i][:, :, :].bitcast(F32), 0.0))
                c(pool.memset(hh[i][:, :, :].bitcast(F32), 0.0))
                c(pool.memset(hl[i][:, :, :].bitcast(F32), 0.0))
            c.sync()
            pool.memset(ms[:, 30:31], 0.0).then_inc(moe_zero, 1)
            pool.wait_ge(tab_init, 16)
            pool.wait_ge(slot_ready, 1)
            for i in range(NT):
                n = ND if i == NPT else P
                for k in range(2):
                    pool.indirect_dma_start(
                        out=table_d, out_offset=bass.IndirectOffsetOnAxis(ap=rt["sl"][0:n, k, i:i + 1].bitcast(U32), axis=0),
                        in_=vals[0:n, k, i:i + 1], in_offset=None).then_inc(tab_done, 16)
            pool.wait_ge(tab_done, 16 * 2 * NT)
            pool.dma_start(slotd[:, :], table_d.rearrange("(p b) a -> p (b a)", b=NBLK)).then_inc(tab_load, 16)
            pool.wait_ge(idx_ready, 1)
            pool.wait_ge(x2_out[0], 16 * ((NT + 1) // 2))
            pool.wait_ge(x2_out[1], 16 * (NT // 2))

            def gather(p, e):
                if not isinstance(e, int) or e >= 2:
                    pool.wait_ge(bt_full, e - 1)
                c(pool.tensor_copy(curs[p][:, :], slots[:, bass.ds(e, 1)]))
                c.sync()
                c(carry())
                pool.indirect_dma_start(
                    out=xg[p][:, :], out_offset=None, in_=rows_d,
                    in_offset=bass.IndirectOffsetOnAxis(ap=curs[p][:, 0:1].bitcast(U32), axis=0),
                    bounds_check=T - 1, oob_is_err=False).then_inc(xg_in[p], 16)

            def scatter(p, e, before_it):
                pool.wait_ge(yb_ready, e + 1)
                if not isinstance(before_it, int) or before_it:
                    pool.wait_ge(y_out[p], 16 * before_it)
                c(pool.tensor_copy(curd[p][:, :], slotd[:, bass.ds(e, 1)]))
                c.sync()
                c(carry())
                pool.indirect_dma_start(
                    out=res_d, out_offset=bass.IndirectOffsetOnAxis(ap=curd[p][:, 0:1].bitcast(U32), axis=0),
                    in_=yb[p][:, :], in_offset=None, bounds_check=2 * T - 1, oob_is_err=False).then_inc(y_out[p], 16)

            for e in range(4):
                gather(e % 2, e)
                if e >= 3:
                    scatter(0, 0, 0)
            for e in range(1, 3):
                gather(1 - e % 2, e + 3)
                scatter(e % 2, e, e // 2)
            loops = (NE - 4) // 2
            with pool.Fori(0, loops) as i:
                c.enter(i, 8)
                for p in range(2):
                    gather(p, i * 2 + (6 + p))
                    scatter(1 - p, i * 2 + (3 + p), i + (1 + p))
                c.leave(loops)
            scatter(1, NE - 1, NE // 2 - 1)
            pool.wait_ge(xinfo_ready, 1)
            nx = pool.value_load(xinfo[0:1, XB:XB + 1], min_val=0, max_val=XB)
            for p in range(2):
                pool.wait_ge(y_out[p], 16 * NE // 2)
                pool.wait_ge(xg_in[p], 16 * (NE + 2) // 2)
            with pool.Fori(0, XB) as j:
                with pool.If(nx > j):
                    pool.tensor_copy(curs[0][:, :], slots[:, bass.ds(j + NE, 1)]).then_inc(e_cur, 1)
                    pool.tensor_copy(curd[0][:, :], slotd[:, bass.ds(j + NE, 1)]).then_inc(e_cur, 1)
                    pool.wait_ge(e_cur, j * 5 + 2)
                    carry().then_inc(e_cur, 1)
                    pool.indirect_dma_start(
                        out=xg[0][:, :], out_offset=None, in_=rows_d,
                        in_offset=bass.IndirectOffsetOnAxis(ap=curs[0][:, 0:1].bitcast(U32), axis=0),
                        bounds_check=T - 1, oob_is_err=False).then_inc(e_xg, 16)
                    pool.wait_ge(e_cur, j * 5 + 3)
                    pool.wait_ge(e_yb, j + 2)
                    carry().then_inc(e_cur, 1)
                    pool.indirect_dma_start(
                        out=res_d, out_offset=bass.IndirectOffsetOnAxis(ap=curd[0][:, 0:1].bitcast(U32), axis=0),
                        in_=yb[0][:, :], in_offset=None, bounds_check=2 * T - 1,
                        oob_is_err=False).then_inc(e_out, 16)
                    pool.wait_ge(e_cur, j * 5 + 4)
                    pool.wait_ge(e_out, j * 16 + 16)
                    carry().then_inc(e_cur, 1)
            pool.memset(ms[:, 31:32], 0.0).then_inc(moe_done, 1)
            for i in range(NT):
                rms(2 * NT + NPT + 1 + i, 24 + i, 25 + i, D, ND if i == NPT else P)

        @block.scalar
        def _(act):
            c = Chain(act, c_act)
            copy = act.copy

            def carry():
                c.sync()
                c(act.mul(gnh[:, 2:3], gnh[:, 0:1], 1.0))

            def high(par, half):
                act.wait_ge(raw_in[par], 16 * half + 16)
                if not isinstance(half, int) or half:
                    act.wait_ge(w_used, 2 * half + (par - 1))
                copy(wh[par][:, :], raw[par][:, :]).then_inc(hi_ready, 1)

            def squares(i):
                act.wait_ge(x_in[i], 16)
                if i:
                    act.wait_ge(sq_done, i)
                act.activation(junk1[:, :], xin[:, i, :], ACT.Square, accum_out=ss[:, i:i + 1]).then_inc(sq_done, 1)

            def high_of_x(i):
                act.wait_ge(xt_full, i + 1)
                b = TB + 2 * (i % 2)
                copy(xh[:, :, i * P:(i + 1) * P], ps[:, b:b + 2, :].rearrange("p a (c t) -> p (a c) t", t=P)
                     ).then_inc(xh_ready, 1)

            for i in range(NT):
                squares(i)
            for i in range(NT):
                high_of_x(i)
                if i == 1:
                    act.wait_ge(a_in, 16)
                    copy(ah[:, :, :], rawa[:, :, :]).then_inc(ah_ready, 1)
            high(0, 0)
            act.wait_ge(a_full, 1)
            c(copy(aT[:, 0:HALF], ps[0:RANK, UB, 0:HALF]))
            copy(aT[:, HALF:T], ps[0:RANK, UB + 1, 0:HALF]).then_inc(aT_ready, 1)
            act.wait_ge(small_in, 16 * NSMALL)
            c(act.mul(gnh[:, 0:DV // P], gn[:, :], 0.5))
            high(1, 0)

            def log_terms(heads):
                for hd in heads:
                    bank, t = TB + 2 * (hd % 2), abt[hd % 2]
                    act.wait_ge(alpha_full, hd + 1)
                    if hd >= 2:
                        act.wait_ge(la_ready, hd)
                    c(act.activation(t[:, 0:SEQ], ps[:, bank, :], ACT.Abs, bias=balpha[:, hd:hd + 1]))
                    c(act.activation(t[:, SEQ:T], ps[:, bank + 1, 0:ND], ACT.Abs, bias=balpha[:, hd:hd + 1]))
                c.sync()
                for hd in heads:
                    c(act.activation(abt[hd % 2][:, :], abt[hd % 2][:, :], ACT.Exp, scale=-1.0))
                c.sync()
                for hd in heads:
                    act.activation(abt[hd % 2][:, :], abt[hd % 2][:, :], ACT.Ln, bias=1.0).then_inc(ls_act, 1)

            log_terms((0, 1))

            def pair_view(par):
                return pair[par][:, :, 0:HALF]

            def halves(ap):
                return ap.rearrange("p (a t) -> p a t", a=2)

            with act.Fori(0, 2) as i:
                for p in range(2):
                    g = i * 2 + p
                    for u in range(2):
                        wait_unit(act, g, g, u, 2, U_QK)
                        copy(qk[:, bass.ds(i * 4 + (2 * p + u), 1), :].rearrange("p b (a t) -> p (b a) t", a=2),
                             pair_view(u)).then_inc(unit_free[u], 1)
                    high(p, i + 1)
            log_terms((2, 3))
            def decays(j):
                act.wait_ge(scans_done, j + 1)
                c(act.activation(eb[:, :, :], bt[:, :, :], ACT.Exp, scale=1 / GATE_NORM))
                if j < NPT:
                    act.activation(ec[:, :, :], bc[:, :, :], ACT.Exp, scale=1 / GATE_NORM).then_inc(ebec_done, 1)
                else:
                    act.activation(ql[:, :, :], bt[:, :, :], ACT.Exp, scale=-1 / GATE_NORM).then_inc(ebec_done, 1)
                act.wait_ge(diffs_done, j + 1)
                if j < NPT:
                    c(act.activation(kst[:, :, :], kst[:, :, :], ACT.Exp, scale=1 / GATE_NORM))
                    act.activation(dif[:, :, :], dif[:, :, :], ACT.Exp, scale=1 / GATE_NORM).then_inc(exps_done, 1)
                else:
                    act.activation(kst[:, :, 0:ND], kst[:, :, 0:ND], ACT.Exp,
                                   scale=1 / GATE_NORM).then_inc(exps_done, 1)

            for k in range(G_G - G_V):
                for t in range(NT):
                    u = (NT * k + t) % 2
                    wait_unit(act, k + G_V, k, t, NT, U_V)
                    copy(v[:, t, k * 256:(k + 1) * 256], ps[:, 2 * u, 0:256]).then_inc(unit_free[u], 1)
                high(k % 2, (G_V + k) // 2 + 1)
                if k == 1:
                    decays(0)
            act.wait_ge(hist_full, 1)
            copy(hist[:, :, :], ps[:, TB, 0:H * DB * 2].rearrange("p (c s) -> p c s", c=H)).then_inc(hist_ready, 1)

            def normed_output(j):
                n, s0_ = (ND, 8) if j == NPT else (P, 8 + 4 * (j % 2))
                for step, func in enumerate((ACT.Square, ACT.Copy)):
                    if step:
                        act.wait_ge(rs_ready, NT + j + 1)
                    for hd in range(H):
                        src = ps[0:n, UB + hd // 2, (hd % 2) * DV:(hd % 2 + 1) * DV]
                        dst = v[0:n, j, hd * DV:(hd + 1) * DV]
                        col = slice(s0_ + hd, s0_ + hd + 1)
                        if step:
                            ins = act.activation(dst, src, func, scale=rs[0:n, col])
                        else:
                            ins = act.activation(dst, src, func, accum_out=ss[0:n, col])
                        if hd == H - 1:
                            ins.then_inc(on_ready if step else sq_done, 1)
                        else:
                            c(ins)

            act.mul(gnh[:, 2:3], gnh[:, 0:1], 1.0).then_inc(on_ready, 1)
            for j in range(NPT):
                for u in range(2):
                    wait_unit(act, j + G_G, j, u, 2, U_G)
                    act.wait_ge(sg_ready, j * 2 + (u + 1))
                    act.activation(halves(ta[:, :]), pair_view(u), ACT.Tanh, scale=0.5).then_inc(g_act, 1)
                    act.activation(halves(tb[:, :]), pair_view(u), ACT.Copy,
                                   scale=gnh[:, u:u + 1]).then_inc(unit_free[u], 1)
                    if u == 0:
                        act.wait_ge(p1_full, j + 1)
                        copy(kt[:, :, :], ps[:, TB + 1, :].rearrange("p (h d) -> p h d", h=H)
                             ).then_inc(kt_ready, 1)
                        decays(j + 1)
                act.wait_ge(kv_full, j + 1)
                if j < NPT - 1:
                    normed_output(j)
                    high(j % 2, j // 2 + (G_G // 2 + 1))
            normed_output(NPT - 1)
            act.wait_ge(p1_full, NPT + 1)
            copy(kt[0:ND, :, :], ps[0:ND, TB + 1, :].rearrange("p (h d) -> p h d", h=H)).then_inc(kt_ready, 1)
            high((NPT - 1) % 2, (NPT - 1) // 2 + (G_G // 2 + 1))
            act.wait_ge(o_full, 1)
            act.wait_ge(dkv_full, DB)
            normed_output(NPT)
            act.wait_ge(st_store, 16 * DB)
            for t in range(2):
                g0 = G_CONV + 3 * t
                for u in range(2):
                    wait_unit(act, g0, 3 * t, u, 2, U_CONV)
                    if t:
                        act.wait_ge(z_ready, 2 * t)
                    copy(halves(tmp[u][:, :]), pair_view(u)).then_inc(unit_free[u], 1)
                high(g0 % 2, g0 // 2 + 1)
                high((g0 + 1) % 2, (g0 + 1) // 2 + 1)
                for u in range(2):
                    act.wait_ge(z_mul, 2 * t + u + 1)
                    copy(zh[:, 2 * t + u, :], tmp[u][:, :]).then_inc(z_hi, 1)
                high((g0 + 2) % 2, (g0 + 2) // 2 + 1)
            for g0, base, dst in ((G_GA, U_GA, m1), (G_GB, U_GB, sgb)):
                with act.Fori(0, 2) as i:
                    c.enter(i, 4)
                    for p in range(2):
                        k = i * 2 + p
                        for u in range(2):
                            wait_unit(act, k + g0, k, u, 2, base)
                            carry()
                            act.activation(dst[:, bass.ds(k * 2 + u, 1), :].rearrange("p b (a t) -> p (b a) t", a=2),
                                           pair_view(u), ACT.Sigmoid).then_inc(unit_free[u], 1)
                        high(p, i + (g0 // 2 + 1))
                    c.leave(2)
                if g0 == G_GA:
                    act.wait_ge(cs_full, 1)
                    copy(cso[:, :], ps[0:2 + 2 * DB, TB, :]).then_inc(cso_ready, 1)
            for j in range(NT):
                n = ND if j == NPT else P
                for b in range(2):
                    act.wait_ge(og_mul, 2 * j + b + 1)
                    copy(xh[:, 4 * b:4 * b + 4, j * P:j * P + n],
                         tmp[b][:, 0:4 * n].rearrange("p (c t) -> p c t", c=4)).then_inc(og_hi, 1)
                if j == 2:
                    high(G_CO % 2, G_CO // 2 + 1)
            high((G_CO + 1) % 2, (G_CO + 1) // 2 + 1)
            with act.Fori(0, 2) as i:
                for p in range(2):
                    k = i * 2 + p
                    for u in range(2):
                        act.wait_ge(m_mul, k * 2 + (u + 1))
                        copy(mh[:, bass.ds(k * 2 + u, 1), 0:T].rearrange("p a t -> p (a t)"),
                             tmp[u][:, :]).then_inc(m_hi, 1)
                    high(p, i + (G_GO // 2 + 1))
            for g in range(G_WO, G_WO + 2):
                high(g % 2, g // 2 + 1)
            for i in range(NT + 3):
                if i < NT:
                    act.wait_ge(h_ready, 4 * NT - (NT - 1 - i))
                    act.wait_ge(sq_done, NT + NPT + 1 + i)
                    act.activation(junk[:, :], h[:, i, :], ACT.Square,
                                   accum_out=ss[:, 16 + i:17 + i]).then_inc(sq_done, 1)
                if i >= 3:
                    act.wait_ge(x2t_full, i - 2)
                    if i >= 5:
                        act.wait_ge(lg_full, i - 4)
                    b = TB + 2 * ((i - 3) % 2)
                    copy(xr[(i - 3) % 2][:, :, :], ps[:, b:b + 2, :].rearrange("p a (c t) -> p (a c) t", t=P)
                         ).then_inc(xr_ready, 1)

            def expert_high(m0, i=0):
                s = (m0 + 2) % 6
                act.wait_ge(raw_in[s], 16 * i + 16 * raw_count(m0))
                act.wait_ge(w_used, 6 * i + (G_END + max(m0 - 2, 0)))
                copy(wh[m0 % 3][:, :], raw[s][:, :]).then_inc(hi_ready, 1)

            for m in range(3):
                expert_high(m)
            for n, (dst, src) in enumerate(((rt["gx"], rt["gd"]), (rt["ex"], rt["dd"]))):
                act.wait_ge(r_dve, n + 1)
                act.activation(dst[:], src[:], ACT.Exp).then_inc(r_act, 1)

            def block_high(e0, i=0):
                act.wait_ge(bt_full, 2 * i + (e0 + 1))
                if e0 >= 2:
                    act.wait_ge(w_used, 6 * i + (G_END + 3 * e0 - 5))
                copy(gh[e0 % 2][:, :, 0:B], ps[:, TB + 2 * (e0 % 2), :].rearrange("p (k t) -> p k t", k=KD)
                     ).then_inc(bh_ready, 1)

            def silu(e0, i=0):
                act.wait_ge(w_used, 6 * i + (G_END + max(3 * e0 - 1, 0) + 1))
                act.activation(si[e0 % 2][:, :], ps[0:B, 0, 0:DE], ACT.Silu).then_inc(si_ready, 1)

            def hidden_high(e0, i=0):
                act.wait_ge(ht_full, 2 * i + (e0 + 1))
                copy(hh[e0 % 2][:, :, 0:B], ps[:, TB + 1 + 2 * (e0 % 2), 0:2 * B].rearrange("p (k t) -> p k t", k=2)
                     ).then_inc(hh_ready, 1)

            def result(e0, i=0):
                act.wait_ge(w_used, 6 * i + (G_END + (3 * e0 + 5 if e0 < NE - 1 else 3 * NE)))
                if e0 >= 2:
                    act.wait_ge(y_out[e0 % 2], 16 * i + 16 * (e0 // 2))
                copy(yb[e0 % 2][:, :].rearrange("p (a c) -> p a c", a=2), ps[0:B, 2:4, :]).then_inc(yb_ready, 1)

            act.wait_ge(moe_zero, 1)
            block_high(0)
            silu(0)
            block_high(1)
            expert_high(3)
            hidden_high(0)
            expert_high(4)
            silu(1)
            block_high(2)
            expert_high(5)
            expert_high(6)
            hidden_high(1)
            result(0)
            expert_high(7)

            def step(e0, i=0):
                silu(e0, i)
                block_high(e0 + 1, i)
                if e0 < NE - 1:
                    expert_high(3 * e0 + 2, i)
                    expert_high(3 * e0 + 3, i)
                else:
                    expert_high(3 * NE - 1)
                hidden_high(e0, i)
                result(e0 - 1, i)
                if e0 < NE - 1:
                    expert_high(3 * e0 + 4, i)

            with act.Fori(0, (NE - 4) // 2) as i:
                step(2, i)
                step(3, i)
            step(NE - 2)
            step(NE - 1)
            result(NE - 1)
            act.wait_ge(xinfo_ready, 1)
            nx = act.value_load(xinfo[0:1, XB:XB + 1], min_val=0, max_val=XB)
            c.sync()
            act.mul(gnh[:, 2:3], gnh[:, 0:1], 1.0).then_inc(e_yb, 1)
            with act.Fori(0, XB) as j:
                with act.If(nx > j):
                    act.wait_ge(e_xt, j + 1)
                    copy(gh[0][:, :, 0:B], ps[:, TB, :].rearrange("p (k t) -> p k t", k=KD)).then_inc(e_bh, 1)
                    act.wait_ge(e_raw, j * 48 + 48)
                    for s in range(3):
                        copy(wh[s][:, :], raw[s][:, :]).then_inc(e_hi, 1)
                    act.wait_ge(e_gu, j + 1)
                    act.activation(si[0][:, :], ps[0:B, 0, 0:DE], ACT.Silu).then_inc(e_si, 1)
                    act.wait_ge(e_ht, j + 1)
                    copy(hh[0][:, :, 0:B], ps[:, TB + 1, 0:2 * B].rearrange("p (k t) -> p k t", k=2)).then_inc(e_hh, 1)
                    act.wait_ge(e_y, j + 1)
                    copy(yb[0][:, :].rearrange("p (a c) -> p a c", a=2), ps[0:B, 2:4, :]).then_inc(e_yb, 1)
            for i in range(NT):
                n = ND if i == NPT else P
                act.wait_ge(hf_ready, i + 1)
                act.wait_ge(sq_done, 2 * NT + NPT + 1 + i)
                act.activation(junk[0:n, :], h[0:n, i, :], ACT.Square,
                               accum_out=ss[0:n, 24 + i:25 + i]).then_inc(sq_done, 1)


        def last_norm(dve, i):
            n = ND if i == NPT else P
            dve.wait_ge(rs_ready, 2 * NT + NPT + 1 + i + 1)
            if i >= 2:
                dve.wait_ge(yo_out[i % 2], 16 * (i // 2))
            dve.scalar_tensor_tensor(yo[i % 2][0:n, :], h[0:n, i, :], rs[0:n, 24 + i:25 + i], nlb[0:n, :],
                                     ALU.mult, ALU.mult).then_inc(yo_ready, 1)

        @block.vector
        def _(dve):
            c = Chain(dve, c_dve)
            tt, ts, stt = dve.tensor_tensor, dve.tensor_scalar, dve.scalar_tensor_tensor

            marks = iter(range(63))

            def signal(sem):
                col = next(marks)
                dve.memset(mark[:, col:col + 1], 0.0).then_inc(sem, 1)

            def low(par, half):
                dve.wait_ge(hi_ready, 2 * half + (par + 1))
                tt(wl[par][:, :], raw[par][:, :], wh[par][:, :].bitcast(F32), ALU.subtract).then_inc(lo_ready, 1)

            dve.memset(xin[ND:P, NPT, :], 0.0).then_inc(dve_const, 1)
            dve.wait_ge(nm_in, 16)

            def low_of_x(i):
                dve.wait_ge(xh_ready, i + 1)
                b = TB + 2 * (i % 2)
                tt(xl[:, :, i * P:(i + 1) * P], ps[:, b:b + 2, :].rearrange("p a (c t) -> p (a c) t", t=P),
                   xh[:, :, i * P:(i + 1) * P].bitcast(F32), ALU.subtract).then_inc(xt_free, 1)

            for i in range(NT):
                dve.wait_ge(rs_ready, i + 1)
                if i >= 2:
                    dve.wait_ge(xt_full, i - 1)
                stt(xn[i % 2][:, :], xin[:, i, :], rs[:, i:i + 1], nmb[:, :], ALU.mult, ALU.mult).then_inc(xn_ready, 1)
                if i >= 2:
                    low_of_x(i - 2)
            low_of_x(NT - 2)
            dve.wait_ge(ah_ready, 1)
            tt(al[:, :, :], rawa[:, :, :], ah[:, :, :].bitcast(F32), ALU.subtract).then_inc(al_ready, 1)
            low_of_x(NT - 1)
            for u in range(2):
                signal(unit_free[u])
            low(0, 0)
            low(1, 0)
            dve.wait_ge(a_full, 1)
            signal(la_ready)
            c(dve.memset(la[:, NPT, :, ND:P], 0.0))
            def log_sigmoid(hd):
                bank = TB + 2 * (hd % 2)
                dve.wait_ge(ls_act, hd + 1)
                dve.wait_ge(la_ready, hd + 1)
                c(ts(mnt[:, 0:SEQ], ps[:, bank, :], balpha[:, hd:hd + 1], 0.0, ALU.add, ALU.min))
                c(ts(mnt[:, SEQ:T], ps[:, bank + 1, 0:ND], balpha[:, hd:hd + 1], 0.0, ALU.add, ALU.min))
                c.sync()
                c(tt(la[:, 0:NPT, hd, :], mnt[:, 0:SEQ].rearrange("p (j t) -> p j t", t=P),
                     abt[hd % 2][:, 0:SEQ].rearrange("p (j t) -> p j t", t=P), ALU.subtract))
                tt(la[:, NPT, hd, 0:ND], mnt[:, SEQ:T], abt[hd % 2][:, SEQ:T], ALU.subtract).then_inc(la_ready, 1)

            for hd in range(2):
                log_sigmoid(hd)
            c(dve.memset(m_tile[:, :, :], 1.0))
            c(dve.memset(m_ch[:, :, :], 1.0))
            c(dve.memset(m_seq[:, :, :], 1.0))
            c(dve.memset(sc[:, :, :], 0.0))
            c(dve.memset(qg[0][:, :, :], 0.0))
            c.sync()
            c(dve.memset(m_tile[:, :, 0:1], 0.0))
            c(dve.memset(m_ch[:, :, :].rearrange("p h (n t) -> p h n t", t=CH)[:, :, :, 0:1], 0.0))
            c(dve.memset(m_seq[:, :, :].rearrange("p h (n t) -> p h n t", t=DS)[:, :, :, 0:1], 0.0))
            dve.wait_ge(pool_const, 1)
            c(dve.tensor_copy(causal[:, :], causal_f[:, :]))
            c(dve.tensor_copy(causal8[:, :], causal8_f[:, :]))
            c.sync()
            with dve.Fori(0, (G_V - G_QK) // 2) as i:
                for p in range(2):
                    low(p, i + 1)
            for hd in range(2, H):
                log_sigmoid(hd)
            c.sync()
            dve.wait_ge(la_ready, H + 1)
            def prepare(j):
                toks = slice(j * P, (j + 1) * P)
                q_j, k_j = qk[:, 0:H, toks], qk[:, H:2 * H, toks]
                ls_j = la[:, j, :, :].rearrange("p h t -> p (h t)")
                c(dve.tensor_tensor_scan(bt[:, :, :].rearrange("p h t -> p (h t)"),
                                         m_tile[:, :, :].rearrange("p h t -> p (h t)"), ls_j, 0.0,
                                         ALU.mult, ALU.add))
                dve.tensor_tensor_scan(bc[:, :, :].rearrange("p h t -> p (h t)"),
                                       m_ch[:, :, :].rearrange("p h t -> p (h t)"), ls_j, 0.0,
                                       ALU.mult, ALU.add).then_inc(scans_done, 1)
                c.sync()
                c(tt(kst[:, :, :], bt[:, :, P - 1:P].to_broadcast((P, H, P)), bt[:, :, :], ALU.subtract))
                off = 0
                for n in range(NCH):
                    w = CH * (n + 1)
                    if n == 0:
                        ins = ts(dif[:, :, 0:w], bt[:, :, 0:w], -1.0, None, ALU.mult)
                    else:
                        ins = tt(dif[:, :, off:off + w], bt[:, :, CH * n - 1:CH * n].to_broadcast((P, H, w)),
                                 bt[:, :, 0:w], ALU.subtract)
                    if n == NCH - 1:
                        ins.then_inc(diffs_done, 1)
                    else:
                        c(ins)
                    off += w
                dve.wait_ge(ebec_done, j + 1)
                c(dve.tensor_copy(dlast[j % 2][:, :], eb[:, :, P - 1:P].rearrange("p h a -> p (h a)")))
                c(stt(qg[j % 2][:, :, :], eb[:, :, :], QSCALE, q_j, ALU.mult, ALU.mult))
                c(stt(ql[:, :, :], ec[:, :, :], QSCALE, q_j, ALU.mult, ALU.mult))
                dve.wait_ge(exps_done, j + 1)
                c(tt(kst[:, :, :], kst[:, :, :], k_j, ALU.mult))
                off = 0
                for n in range(NCH):
                    w = CH * (n + 1)
                    ins = tt(kiv[:, :, off:off + w], dif[:, :, off:off + w], qk[:, H:2 * H, j * P:j * P + w], ALU.mult)
                    if n == NCH - 1:
                        ins.then_inc(gla_in, 1)
                    else:
                        c(ins)
                    off += w

            for g in range(G_V, G_G):
                low(g % 2, g // 2 + 1)
                if g == G_V + 1:
                    prepare(0)
            dve.wait_ge(hist_ready, 1)
            S_zero = dve.memset(S[:, :, :], 0.0)
            S_zero.then_inc(s_ready, 1)
            signal(sg_ready)

            def prepare_decode():
                qd, kd = qk[:, 0:H, SEQ:T], qk[:, H:2 * H, SEQ:T]
                dve.tensor_tensor_scan(bt[:, :, :].rearrange("p h t -> p (h t)"),
                                       m_seq[:, :, :].rearrange("p h t -> p (h t)"),
                                       la[:, NPT, :, :].rearrange("p h t -> p (h t)"), 0.0, ALU.mult,
                                       ALU.add).then_inc(scans_done, 1)
                dve.wait_ge(scans_done, NPT + 1)
                for hd in range(H):
                    b_s = bt[:, hd, 0:ND].rearrange("p (s t) -> p s t", t=DS)
                    ins = tt(kst[:, hd, 0:ND].rearrange("p (s t) -> p s t", t=DS),
                             b_s[:, :, DS - 1:DS].to_broadcast((P, DB, DS)), b_s, ALU.subtract)
                    if hd == H - 1:
                        ins.then_inc(diffs_done, 1)
                    else:
                        c(ins)
                c(dve.memset(qm[:, :, :, :], 0.0))
                dve.wait_ge(ebec_done, NPT + 1)
                c(stt(qg[0][:, :, 0:ND], eb[:, :, 0:ND], QSCALE, qd, ALU.mult, ALU.mult))
                c(tt(ql[:, :, 0:ND], ql[:, :, 0:ND], kd, ALU.mult))
                dve.wait_ge(exps_done, NPT + 1)
                tt(kst[:, :, 0:ND], kst[:, :, 0:ND], kd, ALU.mult).then_inc(gla_in, 1)
                c.sync()
                for s in range(DB):
                    t = slice(s * DS, (s + 1) * DS)
                    ins = dve.tensor_copy(qm[:, s, :, t], qg[0][:, :, t])
                    if s == DB - 1:
                        ins.then_inc(gla_in, 1)
                    else:
                        c(ins)

            for j in range(NPT):
                for u in range(2):
                    dve.wait_ge(g_act, j * 2 + (u + 1))
                    dve.wait_ge(unit_free[u], j + (N_G // 2 + 1))
                    stt(sg[:, 2 * j + u, :], ta[:, :], 1.0, tb[:, :], ALU.add, ALU.mult).then_inc(sg_ready, 1)
                    if u == 0:
                        dve.wait_ge(p1_full, j + 1)
                        for n in range(NCH):
                            w = CH * (n + 1)
                            q0 = CH * n
                            ins = dve.copy_predicated(
                                sc[0:w, :, q0:q0 + CH],
                                causal[0:w, q0:q0 + CH].rearrange("p (a t) -> p a t", a=1).to_broadcast((w, H, CH)),
                                ps[0:w, TB, :].rearrange("p (h t) -> p h t", h=H)[:, :, q0:q0 + CH])
                            if n == NCH - 1:
                                ins.then_inc(sc_ready, 1)
                            else:
                                c(ins)
                        if j < NPT - 1:
                            prepare(j + 1)
                        else:
                            prepare_decode()
                dve.wait_ge(kv_full, j + 1)
                for hd in range(H):
                    ins = stt(S[:, hd, :], S[:, hd, :], dlast[j % 2][:, hd:hd + 1],
                              ps[:, TB + hd // 2, (hd % 2) * DV:(hd % 2 + 1) * DV], ALU.mult, ALU.add)
                    if hd == H - 1:
                        ins.then_inc(s_ready, 1)
                    else:
                        c(ins)
                if j < NPT - 1:
                    low(j % 2, j // 2 + (G_G // 2 + 1))
            c(dve.memset(sc[0:ND, :, 0:ND], 0.0))
            c.sync()
            dve.wait_ge(p1_full, NPT + 1)
            dve.copy_predicated(
                sc[0:ND, :, 0:ND], causal8[:, :].rearrange("p (a t) -> p a t", a=1).to_broadcast((ND, H, ND)),
                ps[0:ND, TB, :].rearrange("p (h t) -> p h t", h=H)[:, :, 0:ND]).then_inc(sc_ready, 1)
            low((NPT - 1) % 2, (NPT - 1) // 2 + (G_G // 2 + 1))
            for s in range(DB):
                dve.wait_ge(dkv_full, s + 1)
                dve.wait_ge(st_load[s % 3], 16 * (s // 3 + 1))
                for hd in range(H):
                    ins = stt(s0[s % 3][:, hd, :], s0[s % 3][:, hd, :], eb[:, hd, s * DS + DS - 1:s * DS + DS],
                              ps[:, TB + hd // 2, (hd % 2) * DV:(hd % 2 + 1) * DV], ALU.mult, ALU.add)
                    if hd == H - 1:
                        ins.then_inc(st_ready, 1)
                    else:
                        c(ins)
            dve.wait_ge(st_store, 16 * DB)
            dve.wait_ge(o_full, 1)
            c(dve.memset(up[:, :, 0:2], 0.0))
            c(dve.tensor_copy(ud[:, :, :, 0:2], hist[:, :, :].rearrange("p c (s w) -> p c s w", w=2)))
            for t in range(2):
                g0 = G_CONV + 3 * t
                uses = N_CONV // 2 + 3 * t
                for u in range(2):
                    ct = 2 * t + u
                    dve.wait_ge(unit_free[u], uses + 1)
                    wait_unit(dve, g0 + 1, 3 * t + 1, u, 2, U_CONV)
                    c(tt(up[:, ct, 2:2 + HALF], pair[u][:, 0, 0:HALF], tmp[u][:, 0:HALF], ALU.mult))
                    c(tt(up[:, ct, 2 + HALF:2 + SEQ], pair[u][:, 1, 0:SEQ - HALF], tmp[u][:, HALF:SEQ], ALU.mult))
                    tt(ud[:, ct, :, 2:2 + DS], pair[u][:, 1, SEQ - HALF:HALF].rearrange("p (s t) -> p s t", t=DS),
                       tmp[u][:, SEQ:T].rearrange("p (s t) -> p s t", t=DS), ALU.mult).then_inc(unit_free[u], 1)
                    c.sync()
                    dve.wait_ge(unit_free[u], uses + 2)
                    for w in range(3):
                        zp, zd = tmp[u][:, 0:SEQ], tmp[u][:, SEQ:T].rearrange("p (s t) -> p s t", t=DS)
                        tap = wtap[:, w, ct:ct + 1]
                        if w == 0:
                            c(ts(zp, up[:, ct, 0:SEQ], tap, None, ALU.mult))
                            c(ts(zd, ud[:, ct, :, 0:DS], tap, None, ALU.mult))
                        else:
                            c(stt(zp, up[:, ct, w:w + SEQ], tap, zp, ALU.mult, ALU.add))
                            c(stt(zd, ud[:, ct, :, w:w + DS], tap, zd, ALU.mult, ALU.add))
                        c.sync()
                    if u == 0:
                        low(g0 % 2, g0 // 2 + 1)
                    else:
                        low((g0 + 1) % 2, (g0 + 1) // 2 + 1)
                for u in range(2):
                    ct = 2 * t + u
                    wait_unit(dve, g0 + 2, 3 * t + 2, u, 2, U_CONV)
                    z2 = tmp[u][:, :].rearrange("p (a t) -> p a t", a=2)
                    tt(z2, pair[u][:, :, 0:HALF], z2, ALU.mult).then_inc(z_mul, 1)
                    dve.wait_ge(z_mul, ct + 1)
                    signal(unit_free[u])
                    dve.wait_ge(z_hi, ct + 1)
                    tt(zl[:, ct, :], tmp[u][:, :], zh[:, ct, :].bitcast(F32), ALU.subtract).then_inc(z_ready, 1)
                low((g0 + 2) % 2, (g0 + 2) // 2 + 1)
            c(dve.tensor_copy(cs[:, :, 0:2], up[:, :, SEQ:SEQ + 2]))
            dve.tensor_copy(cs[:, :, 2:].rearrange("p c (s w) -> p c s w", w=2), ud[:, :, :, DS:DS + 2]
                            ).then_inc(cs_ready, 1)
            c.sync()
            dve.wait_ge(z_ready, H)
            with dve.Fori(0, (G_CO - G_GA) // 2) as i:
                for p in range(2):
                    low(p, i + (G_GA // 2 + 1))
            dve.wait_ge(unit_free[0], N_GB // 2)
            dve.wait_ge(unit_free[1], N_GB // 2)
            unit = 0
            for j in range(NT):
                n = ND if j == NPT else P
                dve.wait_ge(og_full, j + 1)
                for b in range(2):
                    t3 = tmp[b][:, 0:4 * n].rearrange("p (c t) -> p c t", c=4)
                    if j:
                        dve.wait_ge(og_ready, 2 * j + b - 1)
                    tt(t3, ps[:, TB + 2 * (j % 2) + b, :].rearrange("p (c t) -> p c t", t=P)[:, :, 0:n],
                       sg[:, 4 * b:4 * b + 4, j * P:j * P + n], ALU.mult).then_inc(og_mul, 1)
                for _ in range(1 if j in (0, NT - 1) else 2):
                    g, u = G_CO + unit // 4, unit % 4
                    wait_unit(dve, g, unit // 4, u, 4, U_CO)
                    m = m1[:, unit, :].rearrange("p (a t) -> p a t", a=2)
                    tt(m, pair[u % 2][:, :, 0:HALF], m, ALU.mult).then_inc(unit_free[u % 2], 1)
                    unit += 1
                if j == 2:
                    low(G_CO % 2, G_CO // 2 + 1)
                for b in range(2):
                    t3 = tmp[b][:, 0:4 * n].rearrange("p (c t) -> p c t", c=4)
                    dve.wait_ge(og_hi, 2 * j + b + 1)
                    tt(xl[:, 4 * b:4 * b + 4, j * P:j * P + n], t3,
                       xh[:, 4 * b:4 * b + 4, j * P:j * P + n].bitcast(F32), ALU.subtract).then_inc(og_ready, 1)
            assert unit == 4 * (G_GO - G_CO)
            low((G_CO + 1) % 2, (G_CO + 1) // 2 + 1)
            dve.wait_ge(og_ready, 2 * NT)
            dve.wait_ge(w_used, G_GO)
            dve.memset(h[ND:P, NPT, :], 0.0).then_inc(dve_const, 1)
            c(dve.memset(mh[:, :, T:TP].bitcast(F32), 0.0))
            c(dve.memset(ml[:, :, T:TP].bitcast(F32), 0.0))
            c.sync()
            with dve.Fori(0, 2) as i:
                for p in range(2):
                    k = i * 2 + p
                    for u in range(2):
                        wait_unit(dve, k + G_GO, k, u, 2, U_GO)
                        t2 = tmp[u][:, :].rearrange("p (a t) -> p a t", a=2)
                        one = bass.ds(k * 2 + u, 1)
                        tt(t2, pair[u][:, :, 0:HALF], sgb[:, one, :].rearrange("p b (a t) -> p (b a) t", a=2),
                           ALU.mult).then_inc(unit_free[u], 1)
                        dve.wait_ge(unit_free[u], k + (N_GO // 2 + 1))
                        tt(tmp[u][:, :], tmp[u][:, :], m1[:, one, :].rearrange("p a t -> p (a t)"),
                           ALU.add).then_inc(m_mul, 1)
                        dve.wait_ge(m_hi, k * 2 + (u + 1))
                        tt(ml[:, one, 0:T].rearrange("p a t -> p (a t)"), tmp[u][:, :],
                           mh[:, one, 0:T].rearrange("p a t -> p (a t)").bitcast(F32), ALU.subtract).then_inc(m_ready, 1)
                    low(p, i + (G_GO // 2 + 1))
            dve.wait_ge(dve_const, 2)
            dve.wait_ge(h_in, 32)

            def normed(i):
                dve.wait_ge(rs_ready, NT + NPT + 1 + i + 1)
                if i >= 2:
                    dve.wait_ge(x2t_full, i - 1)
                    dve.wait_ge(x2_out[i % 2], 16 * (i // 2))
                stt(x2[i % 2][:, :], h[:, i, :], rs[:, 16 + i:17 + i], nfb[:, :], ALU.mult,
                    ALU.mult).then_inc(x2_ready, 1)

            for g in range(G_WO, G_END):
                k = g - G_WO
                for t in range(NT):
                    u = (NT * k + t) % 2
                    wait_unit(dve, g, k, t, NT, U_WO)
                    hv = h[:, t, k * 256:(k + 1) * 256]
                    tt(hv, hv, ps[:, 2 * u, 0:256], ALU.add).then_inc(h_ready, 1)
                    dve.wait_ge(h_ready, NT * k + t + 1)
                    signal(unit_free[u])
                    if g == G_END - 1 and t >= 2:
                        dve.wait_ge(nf_in, 32)
                        normed(t - 2)
                if g < G_WO + 2:
                    low(g % 2, g // 2 + 1)
            for i in range(NT):
                if i + 3 < NT:
                    normed(i + 3)
                dve.wait_ge(lg_full, i + 1)
                tt(lg[:, i, :], ps[:, 1 + 2 * (i % 2), 0:NR], rb[:, :], ALU.add).then_inc(lg_ready, 1)
            dve.wait_ge(lg_ready, NT)

            def expert_low(m0, i=0):
                dve.wait_ge(hi_ready, 6 * i + (G_END + m0 + 1))
                tt(wl[m0 % 3][:, :], raw[(m0 + 2) % 6][:, :], wh[m0 % 3][:, :].bitcast(F32),
                   ALU.subtract).then_inc(lo_ready, 1)

            r = rt
            dve.wait_ge(r_const, 1)

            def wide(ap, w):
                return ap.rearrange("p (j a) -> p j a", a=1).to_broadcast((P, NT, w))

            def step_(ins):
                c(ins)
                c.sync()

            gl_, el = lg[:, :, 0:NG], lg[:, :, NG:NR]
            step_(dve.tensor_reduce(r["gmax"][:, :], gl_, AX.X, ALU.max))
            tt(r["gd"][:, :, :], gl_, wide(r["gmax"][:, :], NG), ALU.subtract).then_inc(r_dve, 1)
            step_(tt(r["go"][:, :, :], gl_, wide(r["gmax"][:, :], NG), ALU.is_ge))
            step_(stt(r["gc"][:, :, :], r["go"][:, :, :], -64.0, ig[:, :, :], ALU.mult, ALU.add))
            step_(dve.tensor_reduce(r["gi"][:, :], r["gc"][:, :, :], AX.X, ALU.min))
            step_(tt(r["go"][:, :, :], r["gc"][:, :, :], wide(r["gi"][:, :], NG), ALU.is_equal))
            step_(ts(r["go"][:, :, :], r["go"][:, :, :], 1e30, -1e30, ALU.mult, ALU.add))
            for g in range(NG):
                step_(tt(r["em"][:, :, g * NEG:(g + 1) * NEG], el[:, :, g * NEG:(g + 1) * NEG],
                         r["go"][:, :, g:g + 1].to_broadcast((P, NT, NEG)), ALU.add))
            for k, (mx, ix, eo) in enumerate((("m1v", "i1", "e1"), ("m2v", "i2", "e2"))):
                step_(dve.tensor_reduce(r[mx][:, :], r["em"][:, :, :], AX.X, ALU.max))
                step_(tt(r["c1"][:, :, :], r["em"][:, :, :], wide(r[mx][:, :], NE), ALU.is_ge))
                step_(stt(r["c1"][:, :, :], r["c1"][:, :, :], -64.0, io[:, :, :], ALU.mult, ALU.add))
                step_(dve.tensor_reduce(r[ix][:, :], r["c1"][:, :, :], AX.X, ALU.min))
                step_(tt(r[eo][:, :, :], r["c1"][:, :, :], wide(r[ix][:, :], NE), ALU.is_equal))
                if k == 0:
                    step_(stt(r["em"][:, :, :], r["e1"][:, :, :], -3e30, r["em"][:, :, :], ALU.mult, ALU.add))
                step_(ts(r["ek"][:, k, :], r[ix][:, :], 64.0, None, ALU.add))
            tt(r["dd"][:, :], r["m2v"][:, :], r["m1v"][:, :], ALU.subtract).then_inc(r_dve, 1)
            step_(tt(r["mk"][:, :, :], r["e1"][:, :, :], r["e2"][:, :, :], ALU.add))
            tt(r["mk"][:, :, :], r["mk"][:, :, :], wide(valid[:, :], NE), ALU.mult).then_inc(r_dve, 1)
            dve.wait_ge(r_pos, 1)
            step_(dve.tensor_copy(r["cnt"][:, :], ps[:, UB, NT * NE:(NT + 1) * NE]))
            step_(ts(cnt_i[:, :], r["cnt"][:, :], float(B - 1), None, ALU.add))
            step_(ts(cnt_i[:, :], cnt_i[:, :], B.bit_length() - 1, None, ALU.arith_shift_right))
            step_(dve.tensor_copy(r["nb"][:, :], cnt_i[:, :]))
            step_(ts(r["xe"][:, :], r["nb"][:, :], -1.0, 0.0, ALU.add, ALU.max))
            step_(dve.tensor_tensor_scan(r["ci"][:, :], oneb[:, :], r["xe"][:, :], 0.0, ALU.mult, ALU.add))
            step_(tt(r["base"][:, :], r["ci"][:, :], r["xe"][:, :], ALU.subtract))
            step_(ts(r["base"][:, :], r["base"][:, :], float(NE - 1), None, ALU.add))
            for k, eo in enumerate(("e1", "e2")):
                step_(tt(r["pr"][:, :, :], r[eo][:, :, :], ps[:, UB, 0:NT * NE].rearrange("p (j e) -> p j e", e=NE),
                         ALU.mult))
                step_(dve.tensor_reduce(r["pk"][:, k, :], r["pr"][:, :, :], AX.X, ALU.add))
                step_(tt(r["pr"][:, :, :], r[eo][:, :, :],
                         r["base"][:, :].rearrange("p (a e) -> p a e", a=1).to_broadcast((P, NT, NE)), ALU.mult))
                step_(dve.tensor_reduce(r["bk"][:, k, :], r["pr"][:, :, :], AX.X, ALU.add))
            step_(dve.tensor_copy(r["pi"][:, :, :], r["pk"][:, :, :]))
            step_(ts(r["qi"][:, :, :], r["pi"][:, :, :], B.bit_length() - 1, None, ALU.arith_shift_right))
            step_(dve.tensor_copy(r["q"][:, :, :], r["qi"][:, :, :]))
            step_(ts(r["is0"][:, :, :], r["q"][:, :, :], 0.0, None, ALU.is_equal))
            step_(tt(r["bk"][:, :, :], r["bk"][:, :, :], r["q"][:, :, :], ALU.add))
            step_(tt(r["t1"][:, :, :], r["ek"][:, :, :], r["bk"][:, :, :], ALU.subtract))
            step_(tt(r["t1"][:, :, :], r["t1"][:, :, :], r["is0"][:, :, :], ALU.mult))
            step_(tt(r["bk"][:, :, :], r["bk"][:, :, :], r["t1"][:, :, :], ALU.add))
            step_(stt(r["t2"][:, :, :], r["q"][:, :, :], -float(B), r["pk"][:, :, :], ALU.mult, ALU.add))
            step_(stt(r["t2"][:, :, :], r["t2"][:, :, :], float(NBLK), r["bk"][:, :, :], ALU.mult, ALU.add))
            dve.tensor_copy(r["sl"][:, :, :], r["t2"][:, :, :]).then_inc(slot_ready, 1)
            dve.wait_ge(r_act, 1)
            step_(dve.tensor_reduce(r["gsum"][:, :], r["gx"][:, :, :], AX.X, ALU.add))
            step_(dve.reciprocal(r["gtop"][:, :], r["gsum"][:, :]))
            dve.wait_ge(r_act, 2)
            step_(ts(r["gsum"][:, :], r["ex"][:, :], 1.0, None, ALU.add))
            step_(dve.reciprocal(r["gsum"][:, :], r["gsum"][:, :]))
            step_(tt(wts[:, 0, :], r["gtop"][:, :], r["gsum"][:, :], ALU.mult))
            step_(tt(wts[:, 1, :], wts[:, 0, :], r["ex"][:, :], ALU.mult))
            step_(tt(gex[:, :, :], r["ci"][0:1, :].rearrange("p (a e) -> p a e", a=1).to_broadcast((1, XB, NE)),
                     iox[:, :, :], ALU.is_le))
            step_(dve.tensor_reduce(xf[:, 0:XB], gex[:, :, :], AX.X, ALU.add))
            step_(ts(xf[:, 0:XB], xf[:, 0:XB], float(NE - 1), None, ALU.min))
            step_(dve.tensor_copy(xf[:, XB:XB + 1], r["ci"][0:1, NE - 1:NE]))
            dve.tensor_copy(xinfo[:, :], xf[:, :]).then_inc(xinfo_ready, 1)
            dve.wait_ge(tab_load, 16)
            ts(slots[:, :], slotd[:, :], 1, None, ALU.arith_shift_right).then_inc(idx_ready, 1)

            def block_low(e0, i=0):
                p = e0 % 2
                dve.wait_ge(bh_ready, 2 * i + (e0 + 1))
                tt(gl[p][:, :, 0:B], ps[:, TB + 2 * p, :].rearrange("p (k t) -> p k t", k=KD),
                   gh[p][:, :, 0:B].bitcast(F32), ALU.subtract).then_inc(bl_ready, 1)

            def hidden(e0, i=0):
                p = e0 % 2
                dve.wait_ge(si_ready, 2 * i + (e0 + 1))
                dve.wait_ge(w_used, 6 * i + (G_END + (3 * e0 + 1 if e0 else 2)))
                tt(hm[p][:, :], si[p][:, :], ps[0:B, 1, 0:DE], ALU.mult).then_inc(hm_ready, 1)

            def hidden_low(e0, i=0):
                p = e0 % 2
                dve.wait_ge(hh_ready, 2 * i + (e0 + 1))
                tt(hl[p][:, :, 0:B], ps[:, TB + 1 + 2 * p, 0:2 * B].rearrange("p (k t) -> p k t", k=2),
                   hh[p][:, :, 0:B].bitcast(F32), ALU.subtract).then_inc(hl_ready, 1)

            block_low(0)
            block_low(1)
            expert_low(3)
            hidden(0)
            hidden_low(0)
            expert_low(4)
            block_low(2)
            expert_low(5)
            hidden(1)
            expert_low(6)
            hidden_low(1)
            expert_low(7)

            def step(e0, i=0):
                block_low(e0 + 1, i)
                if e0 < NE - 1:
                    expert_low(3 * e0 + 2, i)
                else:
                    expert_low(3 * NE - 1)
                hidden(e0, i)
                if e0 < NE - 1:
                    expert_low(3 * e0 + 3, i)
                hidden_low(e0, i)
                if e0 < NE - 1:
                    expert_low(3 * e0 + 4, i)

            with dve.Fori(0, (NE - 4) // 2) as i:
                step(2, i)
                step(3, i)
            step(NE - 2)
            step(NE - 1)
            nx = dve.value_load(xinfo[0:1, XB:XB + 1], min_val=0, max_val=XB)
            with dve.Fori(0, XB) as j:
                with dve.If(nx > j):
                    dve.wait_ge(e_bh, j + 1)
                    tt(gl[0][:, :, 0:B], ps[:, TB, :].rearrange("p (k t) -> p k t", k=KD),
                       gh[0][:, :, 0:B].bitcast(F32), ALU.subtract).then_inc(e_bl, 1)
                    dve.wait_ge(e_hi, j * 3 + 3)
                    for s in range(3):
                        tt(wl[s][:, :], raw[s][:, :], wh[s][:, :].bitcast(F32), ALU.subtract).then_inc(e_lo, 1)
                    dve.wait_ge(e_si, j + 1)
                    tt(hm[0][:, :], si[0][:, :], ps[0:B, 1, 0:DE], ALU.mult).then_inc(e_hm, 1)
                    dve.wait_ge(e_hh, j + 1)
                    tt(hl[0][:, :, 0:B], ps[:, TB + 1, 0:2 * B].rearrange("p (k t) -> p k t", k=2),
                       hh[0][:, :, 0:B].bitcast(F32), ALU.subtract).then_inc(e_hl, 1)
            for i in range(NT):
                n = ND if i == NPT else P
                dve.wait_ge(y2_in[i], 16)
                step_(stt(h[0:n, i, :], y2[i][0:n, 0, :], wts[0:n, 0, i:i + 1], h[0:n, i, :], ALU.mult, ALU.add))
                stt(h[0:n, i, :], y2[i][0:n, 1, :], wts[0:n, 1, i:i + 1], h[0:n, i, :], ALU.mult,
                    ALU.add).then_inc(hf_ready, 1)
                if i >= 1:
                    last_norm(dve, i - 1)
            last_norm(dve, NT - 1)

        @block.tensor
        def _(pe):
            mm = pe.matmul

            def tiles(ap, k):
                return ap[:, :].rearrange("p (k c) -> p k c", k=k)

            def carry(bank):
                mm(ps[:, bank, 0:2], ident[:, :], ident[:, 0:2], start=True, stop=True)

            def free(u, uses):
                if not isinstance(uses, int) or uses:
                    pe.wait_ge(unit_free[u], uses)

            def three(outs, k_tiles, left, right):
                last = []
                for k in range(k_tiles):
                    for n, (a, b) in enumerate(((0, 0), (0, 1), (1, 0))):
                        for o, out in enumerate(outs):
                            last.append(mm(out, left(a, k), right(b, k, o), start=k == 0 and n == 0,
                                           stop=k == k_tiles - 1 and n == 2))
                return last[-1]

            def feature_unit(p, u, c, x, kt=KD, width=256):
                w = (tiles(wh[p], kt), tiles(wl[p], kt))
                return three([pair[u][:, 0, 0:HALF], pair[u][:, 1, 0:HALF]], kt,
                             lambda a, k: w[a][:, k, c * P:(c + 1) * P],
                             lambda b, k, o: x[b][:, k, o * HALF:(o + 1) * HALF])

            def token_unit(p, u, t, x):
                w = (tiles(wh[p], KD), tiles(wl[p], KD))
                return three([ps[:, 2 * u, 0:256]], KD, lambda a, k: x[a][:, k, t * P:(t + 1) * P],
                             lambda b, k, o: w[b][:, k, :])

            X, Z, M = (xh, xl), (zh, zl), (mh, ml)

            pe.wait_ge(pool_const, 1)
            for i in range(NT):
                pe.wait_ge(xn_ready, i + 1)
                if i >= 2:
                    pe.wait_ge(xt_free, i - 1)
                for k in range(KD):
                    ins = pe.transpose(ps[:, TB + 2 * (i % 2) + k // 4, (k % 4) * P:(k % 4 + 1) * P],
                                       xn[i % 2][:, k * P:(k + 1) * P], ident[:, :])
                ins.then_inc(xt_full, 1)
            pe.wait_ge(al_ready, 1)
            pe.wait_ge(xt_free, NT)
            aw = (ah, al)
            for a0, a1, bank in ((0, HALF, UB), (HALF, T, UB + 1)):
                ins = three([ps[:, bank, 0:a1 - a0]], KD, lambda a, k: aw[a][:, k, :],
                            lambda b, k, o: X[b][:, k, a0:a1])
            ins.then_inc(a_full, 1)

            def alpha(hd):
                if hd >= 2:
                    pe.wait_ge(la_ready, hd)
                for a0, a1, half in ((0, SEQ, 0), (SEQ, T, 1)):
                    ins = mm(ps[:, TB + 2 * (hd % 2) + half, 0:a1 - a0], wau[:, hd * P:(hd + 1) * P], aT[:, a0:a1],
                             start=True, stop=True)
                ins.then_inc(alpha_full, 1)

            pe.wait_ge(aT_ready, 1)
            pe.wait_ge(small_in, 16 * NSMALL)
            for hd in range(2):
                alpha(hd)
            with pe.Fori(0, 2) as i:
                for p in range(2):
                    pe.wait_ge(lo_ready, i * 2 + (p + 1))
                    for u in range(2):
                        free(u, i * 2 + (N_QK // 2 + p))
                        feature_unit(p, u, u, X).then_inc(w_used if u else unit_full, 1)
            for hd in range(2, H):
                alpha(hd)
            with pe.Fori(0, 2) as i:
                for p in range(2):
                    pe.wait_ge(lo_ready, i * 2 + (G_V + p + 1))
                    for t in range(NT):
                        u = (NT * p + t) % 2
                        free(u, i * NT + (N_V // 2 + (NT * p + t) // 2))
                        token_unit(p, u, t, X).then_inc(w_used if t == NT - 1 else unit_full, 1)
            pe.wait_ge(la_ready, H)
            for ct in range(H):
                ins = pe.transpose(ps[:, TB, ct * 2 * DB:(ct + 1) * 2 * DB], sct[:, ct * P:(ct + 1) * P],
                                   ident[0:2 * DB, 0:2 * DB])
            ins.then_inc(hist_full, 1)
            pe.wait_ge(hist_ready, 1)
            pe.wait_ge(la_ready, H + 1)
            for j in range(NPT):
                p = j % 2
                pe.wait_ge(lo_ready, G_G + j + 1)
                free(0, N_G // 2 + j)
                feature_unit(p, 0, 0, X).then_inc(unit_full, 1)
                pe.wait_ge(gla_in, j + 1)
                pe.wait_ge(s_ready, j + 1)
                for hd in range(H):
                    pe.transpose(ps[:, TB + 1, hd * P:(hd + 1) * P], kst[:, hd, :], ident[:, :])
                off = 0
                for n in range(NCH):
                    w = CH * (n + 1)
                    for hd in range(H):
                        q0 = hd * P + CH * n
                        ins = mm(ps[0:w, TB, q0:q0 + CH], kiv[:, hd, off:off + w], ql[:, hd, CH * n:CH * (n + 1)],
                                 start=True, stop=True)
                    off += w
                ins.then_inc(p1_full, 1)
                free(1, N_G // 2 + j)
                feature_unit(p, 1, 1, X).then_inc(w_used, 1)
                pe.wait_ge(kt_ready, j + 1)
                pe.wait_ge(sc_ready, j + 1)
                pe.wait_ge(on_ready, j + 1)
                for hd in range(H):
                    out = ps[:, UB + hd // 2, (hd % 2) * DV:(hd % 2 + 1) * DV]
                    mm(out, sc[:, hd, :], v[:, j, hd * DV:(hd + 1) * DV], start=True, stop=False)
                    mm(out, qg[j % 2][:, hd, :], S[:, hd, :], start=False, stop=True)
                for hd in range(H):
                    ins = mm(ps[:, TB + hd // 2, (hd % 2) * DV:(hd % 2 + 1) * DV], kt[:, hd, :],
                             v[:, j, hd * DV:(hd + 1) * DV], start=True, stop=True)
                ins.then_inc(kv_full, 1)
            pe.wait_ge(gla_in, NPT + 1)
            pe.wait_ge(s_ready, NPT + 1)
            for hd in range(H):
                pe.transpose(ps[0:ND, TB + 1, hd * P:(hd + 1) * P], kst[:, hd, 0:ND], ident[:, :])
            for hd in range(H):
                ins = mm(ps[0:ND, TB, hd * P:hd * P + ND], ql[:, hd, 0:ND], qg[0][:, hd, 0:ND], start=True, stop=True)
            ins.then_inc(p1_full, 1)
            pe.wait_ge(kt_ready, NPT + 1)
            pe.wait_ge(sc_ready, NPT + 1)
            pe.wait_ge(on_ready, NPT + 1)
            for hd in range(H):
                mm(ps[0:ND, UB + hd // 2, (hd % 2) * DV:(hd % 2 + 1) * DV], sc[0:ND, hd, 0:ND],
                   v[0:ND, NPT, hd * DV:(hd + 1) * DV], start=hd % 2 == 0, stop=False, skip_group_check=True)
            pe.wait_ge(gla_in, NPT + 2)
            for s in range(DB):
                pe.wait_ge(st_load[s % 3], 16 * (s // 3 + 1))
                for hd in range(H):
                    ins = mm(ps[0:ND, UB + hd // 2, (hd % 2) * DV:(hd % 2 + 1) * DV], qm[:, s, hd, :],
                             s0[s % 3][:, hd, :], start=False, stop=s == DB - 1, skip_group_check=True)
                if s == DB - 1:
                    ins.then_inc(o_full, 1)
                pe.wait_ge(km_ready, s + 1)
                if s:
                    pe.wait_ge(st_ready, s)
                for hd in range(H):
                    ins = mm(ps[:, TB + hd // 2, (hd % 2) * DV:(hd % 2 + 1) * DV], ksm[s % 2][0:ND, hd, :],
                             v[0:ND, NPT, hd * DV:(hd + 1) * DV], start=True, stop=True)
                ins.then_inc(dkv_full, 1)
            for g in range(G_CONV, G_GA):
                pe.wait_ge(lo_ready, g + 1)
                for u in range(2):
                    free(u, N_CONV // 2 + g - G_CONV)
                    feature_unit(g % 2, u, u, X).then_inc(w_used if u else unit_full, 1)
            for g0, n0 in ((G_GA, N_GA), (G_GB, N_GB)):
                with pe.Fori(0, 2) as i:
                    for p in range(2):
                        pe.wait_ge(lo_ready, i * 2 + (g0 + p + 1))
                        for u in range(2):
                            free(u, i * 2 + (n0 // 2 + p))
                            feature_unit(p, u, u, X).then_inc(w_used if u else unit_full, 1)
                if g0 == G_GA:
                    pe.wait_ge(cs_ready, 1)
                    pe.wait_ge(st_ready, DB)
                    for ct in range(H):
                        ins = pe.transpose(ps[0:2 + 2 * DB, TB, ct * P:(ct + 1) * P], cs[:, ct, :], ident[:, :])
                    ins.then_inc(cs_full, 1)

            def output_t(j):
                n = ND if j == NPT else P
                if j >= 2:
                    pe.wait_ge(og_mul, 2 * (j - 1))
                for k in range(KD):
                    c0 = (k % 4) * P
                    ins = pe.transpose(ps[:, TB + 2 * (j % 2) + k // 4, c0:c0 + n], v[0:n, j, k * P:(k + 1) * P],
                                       ident[0:n, 0:n])
                ins.then_inc(og_full, 1)

            pe.wait_ge(on_ready, NPT + 2)
            pe.wait_ge(cso_ready, 1)
            pe.wait_ge(z_ready, H)
            output_t(0)
            output_t(1)
            for g in range(G_CO, G_GO):
                pe.wait_ge(lo_ready, g + 1)
                for c in range(4):
                    unit = 4 * (g - G_CO) + c
                    free(c % 2, N_CO // 2 + unit // 2)
                    feature_unit(g % 2, c % 2, c, Z, kt=H).then_inc(w_used if c == 3 else unit_full, 1)
                    if unit in (0, 2, 4):
                        output_t(2 + unit // 2)
            pe.wait_ge(og_ready, 2 * NT)
            with pe.Fori(0, 2) as i:
                for p in range(2):
                    pe.wait_ge(lo_ready, i * 2 + (G_GO + p + 1))
                    for u in range(2):
                        free(u, i * 2 + (N_GO // 2 + p))
                        feature_unit(p, u, u, X).then_inc(w_used if u else unit_full, 1)
            def normed_t(i):
                pe.wait_ge(x2_ready, i + 1)
                if i >= 2:
                    pe.wait_ge(xr_ready, i - 1)
                for k in range(KD):
                    ins = pe.transpose(ps[:, TB + 2 * (i % 2) + k // 4, (k % 4) * P:(k % 4 + 1) * P],
                                       x2[i % 2][:, k * P:(k + 1) * P], ident[:, :])
                ins.then_inc(x2t_full, 1)

            def logits(i):
                pe.wait_ge(xr_ready, i + 1)
                if i >= 2:
                    pe.wait_ge(lg_ready, i - 1)
                for k in range(KD):
                    ins = mm(ps[:, 1 + 2 * (i % 2), 0:NR], xr[i % 2][:, k, :], wr[:, k, :], start=k == 0,
                             stop=k == KD - 1)
                ins.then_inc(lg_full, 1)

            pe.wait_ge(m_ready, 2 * (G_WO - G_GO))
            for g in range(G_WO, G_END):
                pe.wait_ge(lo_ready, g + 1)
                for t in range(NT):
                    n = N_WO + NT * (g - G_WO) + t
                    free(n % 2, n // 2)
                    token_unit(g % 2, n % 2, t, M).then_inc(w_used if t == NT - 1 else unit_full, 1)
                    if g == G_END - 1 and t >= NT - 2:
                        normed_t(t - (NT - 2))
            for i in range(NT):
                logits(i)
                if i + 2 < NT:
                    normed_t(i + 2)
            pe.wait_ge(r_dve, 3)
            mk = rt["mk"]
            mm(ps[:, UB, 0:NT * NE].rearrange("p (j e) -> p j e", e=NE), before[:, :], mk[:, :, :], start=True,
               stop=False, skip_group_check=True)
            for t in range(NT):
                ins = mm(ps[:, UB, (t + 1) * NE:(NT + 1) * NE].rearrange("p (j e) -> p j e", e=NE), ones[:, :],
                         mk[:, t:t + 1, :].to_broadcast((P, NT - t, NE)), start=False, stop=t == NT - 1,
                         skip_group_check=True)
            ins.then_inc(r_pos, 1)

            def block_t(e0, i=0):
                p = e0 % 2
                pe.wait_ge(xg_in[p], 16 * i + 16 * (e0 // 2 + 1))
                if e0 >= 2:
                    pe.wait_ge(bl_ready, 2 * i + (e0 - 1))
                carry(TB + 2 * p)
                for k in range(KD):
                    ins = pe.transpose(ps[:, TB + 2 * p, k * B:(k + 1) * B], xg[p][:, k * P:(k + 1) * P],
                                       ident[0:B, 0:B])
                ins.then_inc(bt_full, 1)

            def into_hidden(e0, which, i=0):
                p = e0 % 2
                m = 3 * e0 if which else max(3 * e0 - 1, 0)
                if e0 == 0:
                    m = which
                pe.wait_ge(lo_ready, 6 * i + (G_END + m + 1))
                pe.wait_ge(bl_ready, 2 * i + (e0 + 1))
                if e0:
                    pe.wait_ge(hm_ready if which else si_ready, 2 * i + e0)
                g, w = (gh[p], gl[p]), (tiles(wh[m % 3], KD), tiles(wl[m % 3], KD))
                three([ps[:, which, 0:DE]], KD, lambda a, k: g[a][:, k, :],
                      lambda b, k, o: w[b][:, k, :]).then_inc(w_used, 1)

            def hidden_t(e0, i=0):
                p = e0 % 2
                pe.wait_ge(hm_ready, 2 * i + (e0 + 1))
                if e0 >= 2:
                    pe.wait_ge(hl_ready, 2 * i + (e0 - 1))
                carry(TB + 1 + 2 * p)
                for c in range(DE // P):
                    ins = pe.transpose(ps[:, TB + 1 + 2 * p, c * B:(c + 1) * B], hm[p][:, c * P:(c + 1) * P],
                                       ident[0:B, 0:B])
                ins.then_inc(ht_full, 1)

            def down(e0, i=0):
                p = e0 % 2
                m = 3 * e0 + 4 if e0 < NE - 1 else 3 * NE - 1
                pe.wait_ge(lo_ready, 6 * i + (G_END + m + 1))
                pe.wait_ge(hl_ready, 2 * i + (e0 + 1))
                if e0:
                    pe.wait_ge(yb_ready, 2 * i + e0)
                g, w = (hh[p], hl[p]), (tiles(wh[m % 3], DE // P), tiles(wl[m % 3], DE // P))
                three([ps[:, 2, :], ps[:, 3, :]], DE // P, lambda a, k: g[a][:, k, :],
                      lambda b, k, o: w[b][:, k, o * 512:(o + 1) * 512]).then_inc(w_used, 1)

            pe.wait_ge(lg_ready, NT)
            for u in range(2):
                free(u, N_END // 2)
            block_t(0)
            into_hidden(0, 0)
            block_t(1)
            into_hidden(0, 1)
            hidden_t(0)
            into_hidden(1, 0)
            block_t(2)
            into_hidden(1, 1)
            down(0)
            hidden_t(1)

            def step(e0, i=0):
                into_hidden(e0, 0, i)
                block_t(e0 + 1, i)
                into_hidden(e0, 1, i)
                down(e0 - 1, i)
                hidden_t(e0, i)

            with pe.Fori(0, (NE - 4) // 2) as i:
                step(2, i)
                step(3, i)
            step(NE - 2)
            step(NE - 1)
            down(NE - 1)
            pe.wait_ge(xinfo_ready, 1)
            nx = pe.value_load(xinfo[0:1, XB:XB + 1], min_val=0, max_val=XB)
            pe.wait_ge(yb_ready, NE)
            with pe.Fori(0, XB) as j:
                with pe.If(nx > j):
                    pe.wait_ge(e_xg, j * 16 + 16)
                    carry(TB)
                    for k in range(KD):
                        ins = pe.transpose(ps[:, TB, k * B:(k + 1) * B], xg[0][:, k * P:(k + 1) * P], ident[0:B, 0:B])
                    ins.then_inc(e_xt, 1)
                    pe.wait_ge(e_bl, j + 1)
                    pe.wait_ge(e_lo, j * 3 + 3)
                    for s in range(2):
                        g, w = (gh[0], gl[0]), (tiles(wh[s], KD), tiles(wl[s], KD))
                        ins = three([ps[:, s, 0:DE]], KD, lambda a, k: g[a][:, k, :], lambda b, k, o: w[b][:, k, :])
                    ins.then_inc(e_gu, 1)
                    pe.wait_ge(e_hm, j + 1)
                    carry(TB + 1)
                    for c in range(DE // P):
                        ins = pe.transpose(ps[:, TB + 1, c * B:(c + 1) * B], hm[0][:, c * P:(c + 1) * P],
                                           ident[0:B, 0:B])
                    ins.then_inc(e_ht, 1)
                    pe.wait_ge(e_hl, j + 1)
                    g, w = (hh[0], hl[0]), (tiles(wh[2], DE // P), tiles(wl[2], DE // P))
                    three([ps[:, 2, :], ps[:, 3, :]], DE // P, lambda a, k: g[a][:, k, :],
                          lambda b, k, o: w[b][:, k, o * 512:(o + 1) * 512]).then_inc(e_y, 1)


_INS = ("x_prompt", "x_sample", "state_conv", "state_gla", "norm_mix", "w_in", "w_conv", "w_alpha_up", "b_alpha",
        "gla_norm", "w_conv_out", "w_gla_out", "w_o", "norm_ffn", "w_group_router", "b_group_router",
        "w_expert_router", "b_expert_router", "w_gate", "w_up", "w_down", "norm_final")
_OUTS = ((1, SEQ, D), (DB, DS, D), (1, 1, 2, DC), (1, 1, H, DK, DV), (1, DB, 2, DC), (1, DB, H, DK, DV))


def kernel(**inputs):
    import numpy as _np
    import concourse.bacc as _bacc
    from concourse.bass_utils import run_bass_kernel_spmd as _run

    nc = _bacc.Bacc("TRN2", target_bir_lowering=False, num_devices=1)
    arrays, args = {}, []
    for name in _INS:
        a = _np.ascontiguousarray(inputs[name])
        arrays[name] = a
        args.append(nc.dram_tensor(name, a.shape, F32, kind="ExternalInput").ap())
    outs = ("y_prompt", "y_sample", "conv_prompt_new", "gla_prompt_new", "conv_sample_new", "gla_sample_new")
    for name, shape in zip(outs, _OUTS):
        args.append(nc.dram_tensor(name, shape, F32, kind="ExternalOutput").ap())
    build(nc, *args)
    r = _run(nc, [arrays], core_ids=[0])
    return tuple(r.results[0][name] for name in outs)
```
